# Optimizing a Trainium2 kernel written in Bass

```python
import jax, jax.numpy as jnp
from jax import lax
import numpy as np

D_MODEL = 1024
BATCH = 1
SEQ = 512
DEPTH = 2
DEC_BATCH = 8
DEC_SEQ = 16
PAST_LEN = 256

CHUNK = 64
N_HEADS = 8
HEAD_DIM = 64
ATT_W = N_HEADS * HEAD_DIM
IDX_HEADS = 4
IDX_DIM = 64
TOPK_MAX = 256
CONV_W = 512
CONV_K = 3
D_FF = 2816
Q_BLOCK = 64
ROPE_THETA = 10000.0
EPS = 1e-6
NEG = -1e30
IDX_SCALE = (IDX_DIM ** -0.5) * (IDX_HEADS ** -0.5)
IN_SIZES = (ATT_W, ATT_W, ATT_W, IDX_HEADS * IDX_DIM, IDX_DIM, IDX_HEADS, CONV_W, CONV_W, CONV_W, 2 * D_MODEL)
W_IN_COLS = sum(IN_SIZES)

kernel_name = 'dsa_shortconv_macaron_stream_step'

def rms_norm(x, g):
    xf = x.astype(jnp.float32)
    y = xf * lax.rsqrt(jnp.mean(xf * xf, axis=-1, keepdims=True) + EPS)
    return (y * g.astype(jnp.float32)).astype(x.dtype)

def half_swiglu(x, g, w_up, w_down):
    h = rms_norm(x, g)
    a, b = jnp.split(h @ w_up, 2, axis=-1)
    return x + 0.5 * ((jax.nn.silu(a) * b) @ w_down)

def rope(x, pos):
    half = x.shape[-1] // 2
    freqs = ROPE_THETA ** (-jnp.arange(half, dtype=jnp.float32) / half)
    ang = pos.astype(jnp.float32)[:, None] * freqs[None, :]
    cos = jnp.cos(ang)[:, None, :]
    sin = jnp.sin(ang)[:, None, :]
    xf = x.astype(jnp.float32)
    x1, x2 = xf[..., :half], xf[..., half:]
    return jnp.concatenate([x1 * cos - x2 * sin, x1 * sin + x2 * cos], axis=-1).astype(x.dtype)

def dsa_attend(q, qi, wi, k_all, v_all, ki_all, q_pos, k_pos, top_k):
    B = q.shape[0]
    s_idx = jnp.einsum('bthd,bsd->bths', qi, ki_all).astype(jnp.float32)
    score = jnp.einsum('bths,bth->bts', jax.nn.relu(s_idx), wi.astype(jnp.float32)) * IDX_SCALE
    q_chunk = q_pos // CHUNK
    k_chunk = k_pos // CHUNK
    adm = k_chunk[None, :] <= q_chunk[:, None]
    score = jnp.where(adm[None], score, NEG)
    _, idx = lax.top_k(score, top_k)
    valid = k_chunk[idx] <= q_chunk[None, :, None]
    bidx = jnp.arange(B)[:, None, None]
    k_sel = k_all[bidx, idx]
    v_sel = v_all[bidx, idx]
    logits = jnp.einsum('bthd,btkhd->bhtk', q, k_sel).astype(jnp.float32) * (HEAD_DIM ** -0.5)
    logits = jnp.where(valid[:, None], logits, NEG)
    p = jax.nn.softmax(logits, axis=-1).astype(v_sel.dtype)
    return jnp.einsum('bhtk,btkhd->bthd', p, v_sel)

def sparse_attention(q, qi, wi, k_all, v_all, ki_all, q_pos, k_pos, top_k):
    B, T = q.shape[0], q.shape[1]
    if T <= Q_BLOCK:
        return dsa_attend(q, qi, wi, k_all, v_all, ki_all, q_pos, k_pos, top_k)
    nb = T // Q_BLOCK

    def blk(a):
        return jnp.moveaxis(a.reshape((B, nb, Q_BLOCK) + a.shape[2:]), 1, 0)

    xs = (blk(q), blk(qi), blk(wi), q_pos.reshape(nb, Q_BLOCK))
    out = lax.map(lambda s: dsa_attend(s[0], s[1], s[2], k_all, v_all, ki_all, s[3], k_pos, top_k), xs)
    return jnp.moveaxis(out, 0, 1).reshape(B, T, N_HEADS, HEAD_DIM)

def split_cols(p):
    offs = []
    acc = 0
    for s in IN_SIZES[:-1]:
        acc += s
        offs.append(acc)
    return jnp.split(p, offs, axis=-1)

def layer(x, pos, k_past, v_past, ki_past, conv_past,
          ffn1_norm, ffn1_up, ffn1_down, mix_norm, w_in, conv_w, w_branch, w_out,
          ffn2_norm, ffn2_up, ffn2_down):
    B, T, _ = x.shape
    x = half_swiglu(x, ffn1_norm, ffn1_up, ffn1_down)
    h = rms_norm(x, mix_norm)
    q, k, v, qi, ki, wi, cb, cc, cx, gates = split_cols(h @ w_in)
    q = rope(q.reshape(B, T, N_HEADS, HEAD_DIM), pos)
    k = rope(k.reshape(B, T, N_HEADS, HEAD_DIM), pos)
    v = v.reshape(B, T, N_HEADS, HEAD_DIM)
    qi = rope(qi.reshape(B, T, IDX_HEADS, IDX_DIM), pos)
    ki = rope(ki[:, :, None, :], pos)[:, :, 0, :]
    u = cc * cx
    if k_past is None:
        k_all, v_all, ki_all = k, v, ki
        k_pos = pos
        conv_prev = jnp.zeros((B, CONV_K - 1, CONV_W), u.dtype)
    else:
        k_all = jnp.concatenate([k_past, k], axis=1)
        v_all = jnp.concatenate([v_past, v], axis=1)
        ki_all = jnp.concatenate([ki_past, ki], axis=1)
        k_pos = jnp.arange(k_all.shape[1])
        conv_prev = conv_past
    top_k = min(TOPK_MAX, k_all.shape[1] // 4)
    o_att = sparse_attention(q, qi, wi, k_all, v_all, ki_all, pos, k_pos, top_k).reshape(B, T, ATT_W)
    u_pad = jnp.concatenate([conv_prev, u], axis=1)
    y_conv = conv_w[0] * u_pad[:, 0:T]
    for j in range(1, CONV_K):
        y_conv = y_conv + conv_w[j] * u_pad[:, j:j + T]
    o_conv = cb * y_conv
    y_a = o_att @ w_branch[:ATT_W]
    y_b = o_conv @ w_branch[ATT_W:]
    g_a, g_b = jnp.split(jax.nn.sigmoid(gates), 2, axis=-1)
    x = x + (g_a * y_a + g_b * y_b) @ w_out
    x = half_swiglu(x, ffn2_norm, ffn2_up, ffn2_down)
    return x, k, v, ki, u_pad[:, -(CONV_K - 1):]

def setup_inputs(seed: int = 0) -> dict:
    key = jax.random.key(seed)
    ks = jax.random.split(key, 20)
    f = jnp.float32

    def w(k, shape, fan_in):
        return jax.random.normal(k, shape, f) * (fan_in ** -0.5)

    def gain(k, shape):
        return 1.0 + 0.01 * jax.random.normal(k, shape, f)

    return {
        'x_prompt': jax.random.normal(ks[0], (BATCH, SEQ, D_MODEL), f),
        'x_sample': jax.random.normal(ks[1], (DEC_BATCH, DEC_SEQ, D_MODEL), f),
        'cache_k': jax.random.normal(ks[2], (DEPTH, DEC_BATCH, PAST_LEN, N_HEADS, HEAD_DIM), f),
        'cache_v': jax.random.normal(ks[3], (DEPTH, DEC_BATCH, PAST_LEN, N_HEADS, HEAD_DIM), f),
        'cache_kidx': jax.random.normal(ks[4], (DEPTH, DEC_BATCH, PAST_LEN, IDX_DIM), f),
        'state_conv': jax.random.normal(ks[5], (DEPTH, DEC_BATCH, CONV_K - 1, CONV_W), f),
        'ffn1_norm': gain(ks[6], (DEPTH, D_MODEL)),
        'ffn1_up': w(ks[7], (DEPTH, D_MODEL, 2 * D_FF), D_MODEL),
        'ffn1_down': w(ks[8], (DEPTH, D_FF, D_MODEL), D_FF),
        'mix_norm': gain(ks[9], (DEPTH, D_MODEL)),
        'w_in': w(ks[10], (DEPTH, D_MODEL, W_IN_COLS), D_MODEL),
        'conv_w': w(ks[11], (DEPTH, CONV_K, CONV_W), CONV_K),
        'w_branch': w(ks[12], (DEPTH, ATT_W + CONV_W, D_MODEL), ATT_W),
        'w_out': w(ks[13], (DEPTH, D_MODEL, D_MODEL), D_MODEL),
        'ffn2_norm': gain(ks[14], (DEPTH, D_MODEL)),
        'ffn2_up': w(ks[15], (DEPTH, D_MODEL, 2 * D_FF), D_MODEL),
        'ffn2_down': w(ks[16], (DEPTH, D_FF, D_MODEL), D_FF),
        'final_norm': gain(ks[17], (D_MODEL,)),
    }

def reference(x_prompt, x_sample, cache_k, cache_v, cache_kidx, state_conv,
              ffn1_norm, ffn1_up, ffn1_down, mix_norm, w_in, conv_w, w_branch, w_out,
              ffn2_norm, ffn2_up, ffn2_down, final_norm):
    pos_p = jnp.arange(x_prompt.shape[1])
    pos_s = cache_k.shape[2] + jnp.arange(x_sample.shape[1])
    xp, xs = x_prompt, x_sample
    kp, vp, kip, cp = [], [], [], []
    kss, vss, kis, cs = [], [], [], []
    for i in range(DEPTH):
        wts = (ffn1_norm[i], ffn1_up[i], ffn1_down[i], mix_norm[i], w_in[i], conv_w[i],
               w_branch[i], w_out[i], ffn2_norm[i], ffn2_up[i], ffn2_down[i])
        xp, k1, v1, ki1, c1 = layer(xp, pos_p, None, None, None, None, *wts)
        xs, k2, v2, ki2, c2 = layer(xs, pos_s, cache_k[i], cache_v[i], cache_kidx[i], state_conv[i], *wts)
        kp.append(k1); vp.append(v1); kip.append(ki1); cp.append(c1)
        kss.append(k2); vss.append(v2); kis.append(ki2); cs.append(c2)
    y_prompt = rms_norm(xp, final_norm)
    y_sample = rms_norm(xs, final_norm)
    return (y_prompt, y_sample,
            jnp.stack(kp), jnp.stack(vp), jnp.stack(kip), jnp.stack(cp),
            jnp.stack(kss), jnp.stack(vss), jnp.stack(kis), jnp.stack(cs))


_drawn_inputs = setup_inputs


def setup_inputs(seed=0):
    import zlib

    import numpy as np

    out = dict(_drawn_inputs(seed))
    spreads = {}
    factors = {'ffn1_norm': 4.025,
     'ffn2_norm': 51.784,
     'final_norm': 188.797,
     'mix_norm': 3.648,
     'cache_k': 3.185,
     'cache_v': 4.357}
    for name, (base, spread) in spreads.items():
        noise = np.random.default_rng([zlib.crc32(name.encode()), seed]).standard_normal(out[name].shape)
        drawn = base * np.exp(spread * noise) if base else spread * noise
        out[name] = __import__('jax').numpy.asarray(drawn.astype(out[name].dtype))
    for name, factor in factors.items():
        out[name] = (out[name] * factor).astype(out[name].dtype)
    return out
```

```python
from contextlib import ExitStack

import numpy as np

import concourse.bass as bass
from concourse import mybir

D_MODEL, SEQ, DEPTH, STREAMS, NEW, PAST = 1024, 512, 2, 8, 16, 256
HEADS, HD, ATT_W = 8, 64, 512
IDX_HEADS, CONV_W, D_FF = 4, 512, 2816
EPS = 1e-6
TOP_PROMPT = min(256, SEQ // 4)
TOP_STREAM = min(256, (PAST + NEW) // 4)

P = 128
T = SEQ + STREAMS * NEW
HALF = T // 2
KB = D_MODEL // P
TT = T // P
FB = D_FF // P
GROUPS = [8, 7, 7]
AB = ATT_W // P
CB = CONV_W // P

FFN_TILES = 2 * FB + KB * len(GROUPS)
PROJ = 2 + 1 + 1 + AB + AB + AB + 3 * CB
MIX_TILES = PROJ + 3 * KB + KB
FFN1_AT, MIX_AT, FFN2_AT = 0, FFN_TILES, FFN_TILES + MIX_TILES
GATE_AT = MIX_AT + PROJ
OUT_AT = GATE_AT + 3 * KB
TILES = 2 * FFN_TILES + MIX_TILES
MIX_RES, GATE_RES = FFN_TILES, FFN_TILES + PROJ
OUT_RES, FFN2_RES = GATE_RES + 2 * KB, GATE_RES + 3 * KB
RESULTS = FFN2_RES + FFN_TILES
ALL_TILES = DEPTH * TILES

NEG = -1e30
TAKEN = -3.0e38
MASK = -float(2 ** 100)

IDX_UNITS = [(t, h) for t in (3, 2, 1) for h in range(IDX_HEADS)] + [(4, h) for h in range(IDX_HEADS)]
IDX_COLS = {1: 2 * P, 2: 3 * P, 3: 4 * P, 4: PAST + P}
SLOTS = IDX_COLS[4] + (-TOP_STREAM) % 8
ROUNDS = {1: TOP_PROMPT // 8, 2: TOP_PROMPT // 8, 3: TOP_PROMPT // 8, 4: (TOP_STREAM + 7) // 8}
NROUNDS = max(ROUNDS.values())

ATT_UNITS = []
for _b in range(STREAMS):
    ATT_UNITS.append(("stream", _b, 0))
    ATT_UNITS += [("prompt", (4 * _b + i) // HEADS, (4 * _b + i) % HEADS) for i in range(4)]
NU = len(ATT_UNITS)
GROUP_OF, _g = [], -1
for _kind, _, _h in ATT_UNITS:
    _g += 1 if _kind == "stream" or _h % 2 == 0 else 0
    GROUP_OF.append(_g)
LAST_OF = [u for u in range(NU) if u == NU - 1 or GROUP_OF[u + 1] != GROUP_OF[u]]
NG = len(LAST_OF)

F = mybir.dt.float32
R = mybir.dt.float32r
B16 = mybir.dt.bfloat16
ALU = mybir.AluOpType
ACT = mybir.ActivationFunctionType
AX = mybir.AxisListType.X


def build(nc, wts, x_in, gains_in, cos_in, sin_in, ident_in, bmask_in, convw_in, state_in,
          kcache_in, vcache_in, kidx_in, y_out, k_out, v_out, ki_out, conv_out):
    ctx = ExitStack()
    with ctx:
        spot = [(nc.sbuf_base + 31) // 32 * 32]

        def at(name, shape, dt, offset):
            return nc.alloc_sbuf_tensor_at(name, shape, dt, offset=offset)

        def new(name, shape, dt=F):
            offset = spot[0]
            spot[0] += (int(np.prod(shape[1:])) * (2 if dt == B16 else 4) + 31) // 32 * 32
            assert spot[0] <= nc.sbuf_usable_end, (name, spot[0] - nc.sbuf_usable_end)
            return at(name, shape, dt, offset), offset

        x, _ = new("x", [P, KB, T])
        h_hi, _ = new("h_hi", [P, KB, T], R)
        h_lo, _ = new("h_lo", [P, KB, T], R)
        g_hi, _ = new("g_hi", [P, KB, T], R)
        g_lo, _ = new("g_lo", [P, KB, T], R)
        w_raw, _ = new("w_raw", [P, 2, KB * P])
        w_hi, _ = new("w_hi", [P, 2, KB * P], R)
        w_lo, _ = new("w_lo", [P, 2, KB * P], R)
        m_hi, mix_at = new("m_hi", [P, KB, T], R)
        m_lo, _ = new("m_lo", [P, KB, T], R)
        part = 4 * T
        qT = at("qT", [P, AB, T], F, mix_at)
        kT = at("kT", [P, AB, T], F, mix_at + 4 * part)
        qiT = at("qiT", [P, 2, T], F, mix_at + 8 * part)
        kiT = at("kiT", [P, T], F, mix_at + 10 * part)
        v_sb = at("v_sb", [P, TT, ATT_W], F, mix_at + 11 * part)
        masks = at("masks", [P, 10 * P], B16, mix_at + 15 * part)
        cos_t, _ = new("cos_t", [P, T])
        sin_t, _ = new("sin_t", [P, T])
        r, _ = new("r", [P, T])
        sq, sq_at = new("sq", [P, T])
        acc, _ = new("acc", [P, T])
        q_diag = at("q_diag", [P, 2, AB, P], F, sq_at)
        caches, cache_at = new("caches", [P, 2, 2, KB * P])
        scores = at("scores", [P, 9 * P], F, cache_at)
        s_scores = at("s_scores", [P, SLOTS], F, cache_at + 4 * 9 * P)
        ki_cache = at("ki_cache", [P, 4, PAST], F, cache_at + 8 * KB * P)
        qi_diag = at("qi_diag", [P, 2, 4, P], F, cache_at + 12 * KB * P)
        assert 4 * 9 * P + 4 * SLOTS <= 8 * KB * P
        tmp, tmp_at = new("tmp", [P, 3, T])
        pT = at("pT", [P, 2, 4 * P], F, tmp_at)
        prob, prob_at = new("prob", [P, 2, 4 * P])
        prob3 = at("prob3", [P, 4 * P], F, tmp_at + 4 * 8 * P)
        probs = [prob[:, 0, :], prob[:, 1, :], prob3[:, :]]
        s_mask, _ = new("s_mask", [P, IDX_COLS[4]], B16)
        bmask, _ = new("bmask", [P, P], B16)
        ident, _ = new("ident", [P, P])
        ident_b, _ = new("ident_b", [P, P], B16)
        spread, _ = new("spread", [P, 2, HEADS, NEW], B16)
        ones, _ = new("ones", [P, 1])
        gains, _ = new("gains", [P, (3 * DEPTH + 1) * KB])
        gain, _ = new("gain", [P, KB])
        convw, _ = new("convw", [P, CB, 3])
        state, _ = new("state", [P, CB, STREAMS, 2])
        tails, _ = new("tails", [P, CB, 2 + 2 * STREAMS])
        top8, _ = new("top8", [P, 4, 8])
        wi, _ = new("wi", [P, TT, IDX_HEADS])
        r_tok, _ = new("r_tok", [P, TT])
        neg_max, _ = new("neg_max", [P, 4])
        total, _ = new("total", [P, 4])
        inv, _ = new("inv", [P, 4])
        waited, _ = new("waited", [P, 1])

        lin = [ctx.enter_context(nc.psum_tensor(f"lin{i}", [P, 2, 512], F)) for i in range(2)]
        bank = ctx.enter_context(nc.psum_tensor("bank", [P, 4, 512], F))
        logit_banks = [bank[:, 0, :], bank[:, 1, :], lin[0][:, 0, :]]
        turn_banks = [bank[:, 2, :], lin[1][:, 1, :]]
        out_banks = [bank[:, 3, :], lin[1][:, 0, :]]

        def halves(ap):
            return ap.rearrange("p (a n) -> p a n", a=2)

        def res(slot):
            return lin[slot][:, :, 0:HALF]

        def flat(slot):
            return lin[slot][:, :, :].rearrange("p a n -> p (a n)")

        class Signal:
            def __init__(self, name, per_layer, ahead=0):
                self.sem = ctx.enter_context(nc.semaphore(name))
                self.per_layer, self.ahead = per_layer, ahead

            def count(self, L, k):
                return L * self.per_layer + (k + self.ahead)

        raw_in = [ctx.enter_context(nc.semaphore(f"raw_in{i}")) for i in range(2)]
        consts_in = ctx.enter_context(nc.semaphore("consts_in"))
        x_landed = ctx.enter_context(nc.semaphore("x_landed"))
        hi_ready = Signal("hi_ready", TILES)
        lo_ready = Signal("lo_ready", TILES)
        tile_done = Signal("tile_done", TILES)
        evacuated = Signal("evacuated", RESULTS, 2)
        silu_done = Signal("silu_done", 2 * FB)
        silu_scaled = Signal("silu_scaled", 2 * FB)
        g_hi_done = Signal("g_hi_done", 2 * FB)
        g_ready = Signal("g_ready", 2 * FB)
        armed = Signal("armed", 3, 1)
        sq_done = Signal("sq_done", 3 * KB, KB)
        acc_done = Signal("acc_done", 3 * KB, KB)
        h_hi_done = Signal("h_hi_done", 3 * KB, KB)
        h_ready = Signal("h_ready", 3 * KB, KB)
        sum_done = Signal("sum_done", 3, 1)
        mean_done = Signal("mean_done", 3, 1)
        root_done = Signal("root_done", 3, 1)
        newton = Signal("newton", 15, 5)
        turned_r = Signal("turned_r", 1)
        r_tok_done = Signal("r_tok_done", 1)
        swapped = Signal("swapped", 11)
        sin_done = Signal("sin_done", 11)
        roped = Signal("roped", 11)
        wi_done = Signal("wi_done", 1)
        layer_in = Signal("layer_in", 48)
        diag_cleared = Signal("diag_cleared", 1)
        qi_placed = Signal("qi_placed", IDX_HEADS)
        idx_products = Signal("idx_products", 16)
        relu_done = Signal("relu_done", 16)
        idx_added = Signal("idx_added", 16)
        scores_ready = Signal("scores_ready", 1)
        top_found = Signal("top_found", NROUNDS)
        top_taken = Signal("top_taken", NROUNDS)
        masks_ready = Signal("masks_ready", 1)
        cx_scaled = Signal("cx_scaled", CB)
        conv_step = Signal("conv_step", 8 * CB)
        tails_kept = Signal("tails_kept", CB)
        o_conv_hi = Signal("o_conv_hi", CB)
        o_conv_lo = Signal("o_conv_lo", CB)
        q_diag_cleared = Signal("q_diag_cleared", 1)
        q_placed = Signal("q_placed", STREAMS)
        cache_in = [Signal(f"cache_in{i}", 16 * STREAMS) for i in range(2)]
        logits_done = Signal("logits_done", NU)
        max_done = Signal("max_done", NU)
        exp_done = Signal("exp_done", NU)
        inv_done = Signal("inv_done", NU)
        prob_done = Signal("prob_done", NU)
        turned = Signal("turned", NU)
        pT_done = Signal("pT_done", NU)
        pv_done = Signal("pv_done", NU)
        o_kept = Signal("o_kept", NG)
        o_att_hi = Signal("o_att_hi", AB)
        o_att_lo = Signal("o_att_lo", AB)
        gate_done = Signal("gate_done", 2 * KB)
        mixed = Signal("mixed", 3 * KB, 1)
        m_hi_done = Signal("m_hi_done", KB)
        m_ready = Signal("m_ready", KB)
        stored = Signal("stored", 16 * 4)
        y_scaled = ctx.enter_context(nc.semaphore("y_scaled"))
        y_stored = ctx.enter_context(nc.semaphore("y_stored"))
        ones_set = ctx.enter_context(nc.semaphore("ones_set"))

        block = ctx.enter_context(nc.Block())
        NCONST = 5

        @block.sync
        def _(sp):
            for s in range(2):
                sp.dma_start(w_raw[:, s, :], wts[s]).then_inc(raw_in[s], 16)
            with sp.Fori(0, ALL_TILES // 2) as i:
                for s in range(2):
                    sp.wait_ge(lo_ready.sem, 2 * i + (s + 1))
                    sp.dma_start(w_raw[:, s, :], wts[2 * i + (s + 2)]).then_inc(raw_in[s], 16)

        @block.gpsimd
        def _(pool):
            with pool.Fori(0, ALL_TILES // 2 + 1) as i:
                for s in range(2):
                    pool.wait_ge(hi_ready.sem, 2 * i + (s + 1))
                    nc.gpsimd.tensor_tensor(w_lo[:, s, :], w_raw[:, s, :], w_hi[:, s, :].bitcast(F),
                                            ALU.subtract).then_inc(lo_ready.sem, 1)

        @block.tensor
        def _(pe):
            def passes(out, s, c, rhs_hi, rhs_lo, first, last):
                whi, wlo = w_hi[:, s, c * P:(c + 1) * P], w_lo[:, s, c * P:(c + 1) * P]
                for n, (w, a) in enumerate(((whi, rhs_hi), (whi, rhs_lo), (wlo, rhs_hi))):
                    for half in range(2):
                        ins = nc.tensor.matmul(out[:, half, :], w, a[:, half * HALF:(half + 1) * HALF],
                                               start=first and n == 0, stop=last and n == 2)
                return ins

            def linear(L, n, m, s, hi, lo, blocks=KB, credit=True):
                pe.wait_ge(evacuated.sem, evacuated.count(L, m - 1))
                pe.wait_ge(lo_ready.sem, lo_ready.count(L, n + 1))
                for c in range(blocks):
                    ins = passes(res(s), s, c, hi[:, c, :], lo[:, c, :], c == 0, c == blocks - 1)
                ins.then_inc(tile_done.sem, 1)

            def token_major(L, n, s, slot, width, out):
                for t in range(TT):
                    for c in range(KB):
                        w = [z[:, s, c * width:(c + 1) * width] for z in (w_hi, w_lo)]
                        tok = [z[:, c, t * P:(t + 1) * P] for z in (h_hi, h_lo)]
                        for i, (a, b) in enumerate(((0, 0), (0, 1), (1, 0))):
                            ins = nc.tensor.matmul(out(t), tok[a], w[b], start=c == 0 and i == 0,
                                                   stop=c == KB - 1 and i == 2)
                ins.then_inc(tile_done.sem, 1)

            def sum_squares(L, p):
                pe.wait_ge(acc_done.sem, acc_done.count(L, p * KB))
                for half in range(2):
                    ins = nc.tensor.matmul(bank[:, 2 + half, 0:HALF], ones[:, 0:1].to_broadcast([P, P]),
                                           acc[:, half * HALF:(half + 1) * HALF], start=True, stop=True)
                ins.then_inc(sum_done.sem, 1)

            def ffn(L, f, n0, m0):
                done = 0
                for nb in GROUPS:
                    with pe.Fori(0, nb) as i:
                        if done == 0:
                            pe.wait_ge(h_ready.sem, h_ready.count(L, (0, 2)[f] * KB))
                        for s in range(2):
                            linear(L, n0 + s + 2 * i, m0 + s + 2 * i, s, h_hi, h_lo)
                    n0, m0, done = n0 + 2 * nb, m0 + 2 * nb, done + nb
                    with pe.Fori(0, KB // 2) as i:
                        pe.wait_ge(g_ready.sem, g_ready.count(L, f * FB + done))
                        for s in range(2):
                            linear(L, n0 + s + 2 * i, m0 + s + 2 * i, s, g_hi, g_lo, nb)
                    n0, m0 = n0 + KB, m0 + KB
                sum_squares(L, (1, 3)[f])

            def idx_unit(L, u):
                t, h = IDX_UNITS[u]
                out = bank[:, u % 4, :]
                lane = slice(64 * (h % 2), 64 * (h % 2) + 64)
                if u >= 4:
                    pe.wait_ge(relu_done.sem, relu_done.count(L, u - 3))
                if t < 4:
                    ins = nc.tensor.matmul(out[:, 0:IDX_COLS[t]], qiT[lane, h // 2, t * P:(t + 1) * P],
                                           kiT[lane, 0:IDX_COLS[t]], start=True, stop=True)
                else:
                    pe.wait_ge(qi_placed.sem, qi_placed.count(L, h + 1))
                    for pair in range(4):
                        nc.tensor.matmul(out[:, 0:PAST], qi_diag[:, h % 2, pair, :], ki_cache[:, pair, :],
                                         start=pair == 0, stop=pair == 3)
                    ins = nc.tensor.matmul(out[:, PAST:PAST + P], qiT[lane, h // 2, SEQ:T], kiT[lane, SEQ:T],
                                           start=True, stop=True)
                ins.then_inc(idx_products.sem, 1)

            def logits(L, u):
                kind, a, h = ATT_UNITS[u]
                out = logit_banks[u % 3]
                if u >= 3:
                    pe.wait_ge(exp_done.sem, exp_done.count(L, u - 2))
                if kind == "stream":
                    pe.wait_ge(q_placed.sem, q_placed.count(L, a + 1))
                    pe.wait_ge(cache_in[a % 2].sem, cache_in[a % 2].count(L, 32 * (a // 2 + 1)))
                    nc.tensor.matmul(out[:, 0:PAST + P], spread[:, a % 2, :, :].rearrange("p h t -> p (h t)"),
                                     s_mask[:, :], start=True, stop=False)
                    for c in range(AB):
                        w = q_diag[:, a % 2, c, :]
                        nc.tensor.matmul(out[:, 0:PAST], w, caches[:, a % 2, 0, c * PAST:(c + 1) * PAST],
                                         start=False, stop=False)
                        ins = nc.tensor.matmul(out[:, PAST:PAST + P], w, kT[:, c, SEQ:T],
                                               start=False, stop=c == AB - 1)
                else:
                    n = (a + 1) * P
                    lane = slice(64 * (h % 2), 64 * (h % 2) + 64)
                    nc.tensor.matmul(out[:, 0:n], ident_b[:, :], masks[:, a * n // 2:a * n // 2 + n],
                                     start=True, stop=False)
                    ins = nc.tensor.matmul(out[:, 0:n], qT[lane, h // 2, a * P:(a + 1) * P],
                                           kT[lane, h // 2, 0:n], start=False, stop=True)
                ins.then_inc(logits_done.sem, 1)

            def blocks_of(u):
                kind, a, _ = ATT_UNITS[u]
                return 3 if kind == "stream" else a + 1

            def turn(L, u):
                if u >= 2:
                    pe.wait_ge(pT_done.sem, pT_done.count(L, u - 1))
                pe.wait_ge(prob_done.sem, prob_done.count(L, u + 1))
                for c in range(blocks_of(u)):
                    ins = nc.tensor.transpose(turn_banks[u % 2][:, c * P:(c + 1) * P],
                                              probs[u % 3][:, c * P:(c + 1) * P], ident[:, :])
                ins.then_inc(turned.sem, 1)

            def weigh(L, u):
                kind, a, h = ATT_UNITS[u]
                g, nb = GROUP_OF[u], blocks_of(u)
                out = out_banks[g % 2]
                if g >= 2:
                    pe.wait_ge(o_kept.sem, o_kept.count(L, g - 1))
                pe.wait_ge(pT_done.sem, pT_done.count(L, u + 1))
                if kind == "stream":
                    for c in range(AB):
                        for b in range(nb):
                            v = (caches[:, a % 2, 1, b * ATT_W + c * P:b * ATT_W + (c + 1) * P] if b < 2
                                 else v_sb[:, TT - 1, c * P:(c + 1) * P])
                            ins = nc.tensor.matmul(out[:, c * 32:(c + 1) * 32], v,
                                                   pT[:, u % 2, b * P + c * 32:b * P + (c + 1) * 32],
                                                   start=b == 0, stop=b == nb - 1)
                else:
                    lane = slice(64 * (h % 2), 64 * (h % 2) + 64)
                    for b in range(nb):
                        ins = nc.tensor.matmul(out[lane, 0:P], v_sb[:, b, h * HD:(h + 1) * HD],
                                               pT[:, u % 2, b * P:(b + 1) * P], start=b == 0, stop=b == nb - 1)
                ins.then_inc(pv_done.sem, 1)

            pe.wait_ge(consts_in, 16 * NCONST)
            pe.wait_ge(ones_set, 1)
            sum_squares(0, 0)
            with pe.Fori(0, DEPTH) as L:
                ffn(L, 0, FFN1_AT, 0)
                pe.wait_ge(h_ready.sem, h_ready.count(L, KB))
                n = MIX_AT
                m = MIX_RES

                def proj():
                    nonlocal n, m
                    linear(L, n, m, n % 2, h_hi, h_lo)
                    n, m = n + 1, m + 1
                proj()
                proj()
                proj()
                pe.wait_ge(newton.sem, newton.count(L, 5))
                for t in range(TT):
                    ins = nc.tensor.matmul(bank[:, 1, t:t + 1], r[0:1, t * P:(t + 1) * P], ones[0:1, 0:1],
                                           start=True, stop=True)
                ins.then_inc(turned_r.sem, 1)
                pe.wait_ge(evacuated.sem, evacuated.count(L, m - 1))
                pe.wait_ge(lo_ready.sem, lo_ready.count(L, n + 1))
                token_major(L, n, n % 2, n % 2, IDX_HEADS,
                            lambda t: flat(1)[:, t * IDX_HEADS:(t + 1) * IDX_HEADS])
                n, m = n + 1, m + 1
                proj()
                pe.wait_ge(roped.sem, roped.count(L, 3))
                pe.wait_ge(r_tok_done.sem, r_tok_done.count(L, 1))
                for u in range(8):
                    idx_unit(L, u)
                proj()
                pe.wait_ge(layer_in.sem, layer_in.count(L, 48))
                for u in range(8, 16):
                    idx_unit(L, u)
                for _ in range(2 + AB):
                    proj()
                for j in range(AB):
                    pe.wait_ge(evacuated.sem, evacuated.count(L, m - 1))
                    pe.wait_ge(lo_ready.sem, lo_ready.count(L, n + 1))
                    token_major(L, n, n % 2, n % 2, P, lambda t: flat(n % 2)[:, t * P:(t + 1) * P])
                    n, m = n + 1, m + 1
                for _ in range(3 * CB):
                    proj()
                pe.wait_ge(masks_ready.sem, masks_ready.count(L, 1))
                pe.wait_ge(evacuated.sem, evacuated.count(L, m))
                for step in range(NU + 3):
                    if step < NU:
                        logits(L, step)
                    if 0 <= step - 2 < NU:
                        turn(L, step - 2)
                    if 0 <= step - 3 < NU:
                        weigh(L, step - 3)
                with pe.Fori(0, KB // 2) as jj:
                    pe.wait_ge(o_kept.sem, o_kept.count(L, NG))
                    for j2 in range(2):
                        for s in range(2):
                            pe.wait_ge(evacuated.sem, evacuated.count(L, GATE_RES - 1 + 2 * j2 + s + 4 * jj))
                            ring = (3 * j2 + s) % 2
                            pe.wait_ge(lo_ready.sem, lo_ready.count(L, GATE_AT + 1 + 3 * j2 + s + 6 * jj))
                            for c in range(KB):
                                ins = passes(res(s), ring, c, h_hi[:, c, :], h_lo[:, c, :], c == 0, c == KB - 1)
                            ins.then_inc(tile_done.sem, 1)
                        ring = (3 * j2 + 2) % 2
                        pe.wait_ge(o_att_lo.sem, o_att_lo.count(L, AB))
                        pe.wait_ge(lo_ready.sem, lo_ready.count(L, GATE_AT + 3 + 3 * j2 + 6 * jj))
                        pe.wait_ge(mixed.sem, mixed.count(L, 3 * j2 + 6 * jj))
                        for part_ in range(2):
                            for c in range(AB):
                                b = part_ * AB + c
                                ins = passes(bank[:, 2 * part_:2 * part_ + 2, 0:HALF], ring, b,
                                             g_hi[:, b, :], g_lo[:, b, :], c == 0, c == AB - 1)
                        ins.then_inc(tile_done.sem, 1)
                with pe.Fori(0, KB // 2) as i:
                    pe.wait_ge(m_ready.sem, m_ready.count(L, KB))
                    for s in range(2):
                        linear(L, OUT_AT + s + 2 * i, OUT_RES + s + 2 * i, s, m_hi, m_lo)
                sum_squares(L, 2)
                ffn(L, 1, FFN2_AT, FFN2_RES)

        @block.scalar
        def _(act):
            def split(L, k, i=0, step=2):
                s = k % 2
                act.wait_ge(tile_done.sem, L * TILES + (k - 1) + (step * i))
                act.wait_ge(raw_in[s], L * (8 * TILES) + 16 * (k // 2 + 1) + (8 * step) * i)
                nc.scalar.activation(w_hi[:, s, :], w_raw[:, s, :], ACT.Copy).then_inc(hi_ready.sem, 1)

            def norm_block(j, arrived):
                arrived()
                nc.scalar.activation(sq[:, :], x[:, j, :], ACT.Square).then_inc(sq_done.sem, 1)
                nc.scalar.activation(h_hi[:, j, :], x[:, j, :], ACT.Copy,
                                     scale=gain[:, j:j + 1]).then_inc(h_hi_done.sem, 1)

            def root(L, p):
                act.wait_ge(mean_done.sem, mean_done.count(L, p))
                nc.scalar.activation(tmp[:, 1, :], tmp[:, 0, :], ACT.Sqrt).then_inc(root_done.sem, 1)

            def closing(L, n0, m0, p):
                for j in range(KB):
                    split(L, n0 + j + 2)

                    def arrived():
                        if j:
                            act.wait_ge(acc_done.sem, acc_done.count(L, (p - 1) * KB + j))
                        act.wait_ge(evacuated.sem, evacuated.count(L, m0 + j + 1))
                    norm_block(j, arrived)
                root(L, p)

            def ffn(L, f, n0, m0):
                done = 0
                for g, nb in enumerate(GROUPS):
                    with act.Fori(0, nb) as i:
                        split(L, n0 + 2, i)
                        act.wait_ge(evacuated.sem, evacuated.count(L, m0 + 1 + 2 * i))
                        nc.scalar.activation(tmp[:, 1, :], tmp[:, 0, :], ACT.Silu).then_inc(silu_done.sem, 1)
                        split(L, n0 + 3, i)
                        act.wait_ge(evacuated.sem, evacuated.count(L, m0 + 2 + 2 * i))
                        nc.scalar.activation(g_hi[:, i, :], tmp[:, 2, :], ACT.Copy).then_inc(g_hi_done.sem, 1)
                    n0, m0, done = n0 + 2 * nb, m0 + 2 * nb, done + nb
                    if g < len(GROUPS) - 1:
                        with act.Fori(0, KB // 2) as i:
                            split(L, n0 + 2, i)
                            split(L, n0 + 3, i)
                    else:
                        closing(L, n0, m0, (1, 3)[f])
                    n0, m0 = n0 + KB, m0 + KB

            def relu(L, u):
                n = IDX_COLS[IDX_UNITS[u][0]]
                act.wait_ge(idx_products.sem, idx_products.count(L, u + 1))
                if u >= 2:
                    act.wait_ge(idx_added.sem, idx_added.count(L, u - 1))
                nc.scalar.activation(prob[:, u % 2, 0:n], bank[:, u % 4, 0:n], ACT.Relu).then_inc(relu_done.sem, 1)

            def place_qi(L, h):
                if h >= 2:
                    act.wait_ge(idx_products.sem, idx_products.count(L, 12 + h - 1))
                src = qiT[64 * (h % 2):64 * (h % 2) + 64, h // 2, SEQ:T].rearrange(
                    "p (pair par t) -> p pair par t", pair=4, par=2)
                for par in range(2):
                    dst = qi_diag[64 * par:64 * par + 64, h % 2, :, :].rearrange(
                        "p pair n -> p (pair n)")
                    dst = diagonal(dst, 16 * par, P + 2 * NEW, 4)
                    ins = nc.scalar.activation(dst, src[:, :, par, :], ACT.Copy)
                ins.then_inc(qi_placed.sem, 1)

            def load_cache(L, b):
                act.dma_start(caches[:, b % 2, 0, :], kcache_in[L, b]).then_inc(cache_in[b % 2].sem, 16)
                act.dma_start(caches[:, b % 2, 1, :], vcache_in[L, b]).then_inc(cache_in[b % 2].sem, 16)

            def place_q(L, b):
                if b >= 2:
                    act.wait_ge(logits_done.sem, logits_done.count(L, 5 * (b - 2) + 1))
                for par in range(2):
                    dst = q_diag[64 * par:64 * par + 64, b % 2, :, :].rearrange("p c n -> p (c n)")
                    dst = diagonal(dst, 16 * par, P + 2 * NEW, AB)
                    src = qT[64 * par:64 * par + 64, :, SEQ + NEW * b:SEQ + NEW * (b + 1)]
                    nc.scalar.activation(dst, src, ACT.Copy)
                nc.scalar.activation(spread[:, b % 2, :, :],
                                     ident_b[:, NEW * b:NEW * (b + 1)].unsqueeze(1).to_broadcast([P, HEADS, NEW]),
                                     ACT.Copy).then_inc(q_placed.sem, 1)

            def exps(L, u):
                n = unit_columns(u)
                if u >= 3:
                    act.wait_ge(turned.sem, turned.count(L, u - 2))
                act.wait_ge(max_done.sem, max_done.count(L, u + 1))
                nc.scalar.activation(probs[u % 3][:, 0:n], logit_banks[u % 3][:, 0:n], ACT.Exp,
                                     bias=neg_max[:, u % 3:u % 3 + 1],
                                     accum_out=total[:, u % 3:u % 3 + 1]).then_inc(exp_done.sem, 1)

            def take_turned(L, u):
                n = unit_columns(u)
                if u >= 2:
                    act.wait_ge(pv_done.sem, pv_done.count(L, u - 1))
                act.wait_ge(turned.sem, turned.count(L, u + 1))
                nc.scalar.activation(pT[:, u % 2, 0:n], turn_banks[u % 2][:, 0:n], ACT.Copy).then_inc(pT_done.sem, 1)

            act.dma_start(x[:, :, :], x_in).then_inc(x_landed, 16)
            for dst, src in ((gains[:, :], gains_in), (ident[:, :], ident_in), (cos_t[:, :], cos_in),
                             (sin_t[:, :], sin_in), (tmp[:, 0, 0:P], bmask_in)):
                act.dma_start(dst, src).then_inc(consts_in, 16)
            for s in range(2):
                act.wait_ge(raw_in[s], 16)
                nc.scalar.activation(w_hi[:, s, :], w_raw[:, s, :], ACT.Copy).then_inc(hi_ready.sem, 1)
            act.wait_ge(x_landed, 16)
            act.wait_ge(armed.sem, armed.count(0, 0))
            for j in range(KB):
                def arrived(j=j):
                    if j:
                        act.wait_ge(acc_done.sem, acc_done.count(0, -KB + j))
                norm_block(j, arrived)
            root(0, 0)
            with act.Fori(0, DEPTH) as L:
                ffn(L, 0, FFN1_AT, 0)
                act.dma_start(convw[:, :, :], convw_in[L]).then_inc(layer_in.sem, 16)
                act.dma_start(state[:, :, :, :], state_in[L]).then_inc(layer_in.sem, 16)
                act.dma_start(ki_cache[:, :, :], kidx_in[L]).then_inc(layer_in.sem, 16)
                n = MIX_AT
                m = MIX_RES
                turns = 0

                def swap_halves():
                    nonlocal turns
                    act.wait_ge(evacuated.sem, evacuated.count(L, m + 1))
                    for quarter in range(4):
                        to = 32 * (quarter ^ 1)
                        ins = nc.scalar.activation(tmp[to:to + 32, 1, :], tmp[32 * quarter:32 * quarter + 32, 0, :],
                                                   ACT.Copy)
                    ins.then_inc(swapped.sem, 1)
                    turns += 1
                for what in ["rope"] * 3 + ["wi"] + ["rope"] * (2 * AB) + ["v"] * AB + ["cx", "cc", "cb"] * CB:
                    split(L, n + 2)
                    if what == "rope":
                        swap_halves()
                    if n == MIX_AT + 4:
                        for u in range(8):
                            relu(L, u)
                    if n == MIX_AT + 5:
                        act.wait_ge(diag_cleared.sem, diag_cleared.count(L, 1))
                        for u in range(8, 12):
                            relu(L, u)
                        place_qi(L, 0)
                        place_qi(L, 1)
                        for h in range(IDX_HEADS):
                            relu(L, 12 + h)
                            if h + 2 < IDX_HEADS:
                                place_qi(L, h + 2)
                    ct = (n - MIX_AT - 4 - 3 * AB) // 3
                    if what == "cc":
                        act.wait_ge(evacuated.sem, evacuated.count(L, m + 1))
                        nc.scalar.activation(tails[:, ct, 0:2], tmp[:, 1, SEQ - 2:SEQ], ACT.Copy)
                        nc.scalar.activation(
                            tails[:, ct, 2:].rearrange("p (b t) -> p b t", t=2),
                            tmp[:, 1, SEQ:T].rearrange("p (b t) -> p b t", t=NEW)[:, :, NEW - 2:NEW],
                            ACT.Copy).then_inc(tails_kept.sem, 1)
                    if what == "cb":
                        act.wait_ge(evacuated.sem, evacuated.count(L, m + 1))
                        nc.scalar.activation(g_hi[:, AB + ct, :], tmp[:, 0, :], ACT.Copy).then_inc(o_conv_hi.sem, 1)
                    n, m = n + 1, m + 1
                act.wait_ge(masks_ready.sem, masks_ready.count(L, 1))
                load_cache(L, 0)
                act.wait_ge(q_diag_cleared.sem, q_diag_cleared.count(L, 1))
                load_cache(L, 1)
                act.wait_ge(tails_kept.sem, tails_kept.count(L, CB))
                act.dma_start(ki_out[L], kiT[0:64, :]).then_inc(stored.sem, 16)
                act.dma_start(k_out[L], kT[:, :, :]).then_inc(stored.sem, 16)
                act.dma_start(v_out[L], v_sb[:, :, :]).then_inc(stored.sem, 16)
                act.dma_start(conv_out[L], tails[:, :, :]).then_inc(stored.sem, 16)
                place_q(L, 0)
                for step in range(NU + 2):
                    if step < NU:
                        kind, b, _ = ATT_UNITS[step]
                        exps(L, step)
                        if kind == "stream" and b + 1 < STREAMS:
                            place_q(L, b + 1)
                    if 0 <= step - 2 < NU:
                        take_turned(L, step - 2)
                    if step % 5 == 4 and 1 <= step // 5 < STREAMS - 1:
                        act.wait_ge(pv_done.sem, pv_done.count(L, 5 * (step // 5 - 1) + 1))
                        load_cache(L, step // 5 + 1)
                act.wait_ge(o_kept.sem, o_kept.count(L, NG))
                for c in range(AB):
                    nc.scalar.activation(g_hi[:, c, :], qT[:, c, :], ACT.Copy).then_inc(o_att_hi.sem, 1)
                act.wait_ge(stored.sem, stored.count(L, 64))
                with act.Fori(0, KB // 2) as jj:
                    for j2 in range(2):
                        for s in range(2):
                            split(L, GATE_AT + 3 * j2 + s + 2, jj, 6)
                            act.wait_ge(evacuated.sem, evacuated.count(L, GATE_RES + 1 + 2 * j2 + s + 4 * jj))
                            nc.scalar.activation(tmp[:, s, :], tmp[:, s, :], ACT.Sigmoid).then_inc(gate_done.sem, 1)
                        split(L, GATE_AT + 3 * j2 + 4, jj, 6)
                        act.wait_ge(mixed.sem, mixed.count(L, 3 * j2 + 3 + 6 * jj))
                        nc.scalar.activation(m_hi[:, 2 * jj + j2, :], tmp[:, 2, :], ACT.Copy).then_inc(m_hi_done.sem, 1)
                closing(L, OUT_AT, OUT_RES, 2)
                ffn(L, 1, FFN2_AT, FFN2_RES)
            for j in range(KB):
                act.wait_ge(y_scaled, j + 1)
                act.dma_start(y_out[:, j * T:(j + 1) * T], x[:, j, :]).then_inc(y_stored, 16)
            act.wait_ge(y_stored, 16 * KB)

        @block.vector
        def _(dve):
            def leave(L, n, m, s, out, scaled_by, factor=None):
                dve.wait_ge(tile_done.sem, tile_done.count(L, n + 1))
                if factor is None:
                    ins = nc.vector.tensor_tensor(halves(out), res(s), halves(scaled_by), ALU.mult)
                else:
                    ins = nc.vector.scalar_tensor_tensor(out=halves(out), in0=res(s), scalar=factor,
                                                         in1=halves(scaled_by), op0=ALU.mult, op1=ALU.mult)
                ins.then_inc(evacuated.sem, 1)

            def arm(norm):
                nc.vector.memset(acc[:, :], 0.0)
                nc.vector.tensor_copy(gain[:, :], gains[:, bass.ds(norm * KB, KB)]).then_inc(armed.sem, 1)

            def norm_block(L, p, j):
                dve.wait_ge(sq_done.sem, sq_done.count(L, (p - 1) * KB + j + 1))
                nc.vector.tensor_tensor(acc[:, :], acc[:, :], sq[:, :], ALU.add).then_inc(acc_done.sem, 1)
                dve.wait_ge(h_hi_done.sem, h_hi_done.count(L, (p - 1) * KB + j + 1))
                nc.vector.scalar_tensor_tensor(out=h_lo[:, j, :], in0=x[:, j, :], scalar=gain[:, j:j + 1],
                                               in1=h_hi[:, j, :].bitcast(F), op0=ALU.mult,
                                               op1=ALU.subtract).then_inc(h_ready.sem, 1)

            def reciprocal_root(L, p):
                k = 5 * (p - 1)
                dve.wait_ge(sum_done.sem, sum_done.count(L, p))
                nc.vector.tensor_scalar(halves(tmp[:, 0, :]), bank[:, 2:4, 0:HALF], 1.0 / D_MODEL, EPS,
                                        ALU.mult, ALU.add).then_inc(mean_done.sem, 1)
                dve.wait_ge(root_done.sem, root_done.count(L, p))
                nc.vector.reciprocal(r[:, :], tmp[:, 1, :]).then_inc(newton.sem, 1)
                dve.wait_ge(newton.sem, newton.count(L, k + 1))
                nc.vector.tensor_tensor(tmp[:, 2, :], r[:, :], r[:, :], ALU.mult).then_inc(newton.sem, 1)
                dve.wait_ge(newton.sem, newton.count(L, k + 2))
                nc.vector.tensor_tensor(tmp[:, 2, :], tmp[:, 2, :], tmp[:, 0, :], ALU.mult).then_inc(newton.sem, 1)
                dve.wait_ge(newton.sem, newton.count(L, k + 3))
                nc.vector.tensor_scalar(tmp[:, 2, :], tmp[:, 2, :], -0.5, 1.5, ALU.mult, ALU.add).then_inc(newton.sem, 1)
                dve.wait_ge(newton.sem, newton.count(L, k + 4))
                nc.vector.tensor_tensor(r[:, :], r[:, :], tmp[:, 2, :], ALU.mult).then_inc(newton.sem, 1)

            def closing(L, n0, m0, p, factor):
                arm(3 * L + p)
                dve.wait_ge(armed.sem, armed.count(L, p))
                for j in range(KB):
                    dve.wait_ge(tile_done.sem, tile_done.count(L, n0 + j + 1))
                    nc.vector.scalar_tensor_tensor(out=halves(x[:, j, :]), in0=res((m0 + j) % 2), scalar=factor,
                                                   in1=halves(x[:, j, :]), op0=ALU.mult,
                                                   op1=ALU.add).then_inc(evacuated.sem, 1)
                    norm_block(L, p, j)
                reciprocal_root(L, p)

            def ffn(L, f, n0, m0):
                done = 0
                for g, nb in enumerate(GROUPS):
                    k = f * FB + done
                    with dve.Fori(0, nb) as i:
                        if done == 0:
                            dve.wait_ge(newton.sem, newton.count(L, (0, 10)[f]))
                        leave(L, n0 + 2 * i, m0, 0, tmp[:, 0, :], r[:, :])
                        dve.wait_ge(silu_done.sem, silu_done.count(L, k + 1 + i))
                        nc.vector.tensor_tensor(tmp[:, 1, :], tmp[:, 1, :], r[:, :], ALU.mult).then_inc(silu_scaled.sem, 1)
                        dve.wait_ge(silu_scaled.sem, silu_scaled.count(L, k + 1 + i))
                        leave(L, n0 + 1 + 2 * i, m0, 1, tmp[:, 2, :], tmp[:, 1, :])
                        dve.wait_ge(g_hi_done.sem, g_hi_done.count(L, k + 1 + i))
                        nc.vector.tensor_tensor(g_lo[:, i, :], tmp[:, 2, :], g_hi[:, i, :].bitcast(F),
                                                ALU.subtract).then_inc(g_ready.sem, 1)
                    n0, m0, done = n0 + 2 * nb, m0 + 2 * nb, done + nb
                    if g < len(GROUPS) - 1:
                        with dve.Fori(0, KB // 2) as i:
                            for s in range(2):
                                dve.wait_ge(tile_done.sem, tile_done.count(L, n0 + s + 1 + 2 * i))
                                xb = x[:, 2 * i + s, :]
                                nc.vector.scalar_tensor_tensor(out=halves(xb), in0=res(s), scalar=0.5,
                                                               in1=halves(xb), op0=ALU.mult,
                                                               op1=ALU.add).then_inc(evacuated.sem, 1)
                    else:
                        closing(L, n0, m0, (1, 3)[f], 0.5)
                    n0, m0 = n0 + KB, m0 + KB

            def scores_of(t):
                if t == 4:
                    return s_scores[:, 0:PAST + P]
                start = {1: 0, 2: 2 * P, 3: 5 * P}[t]
                return scores[:, start:start + IDX_COLS[t]]

            def add_head(L, u):
                t, h = IDX_UNITS[u]
                dve.wait_ge(relu_done.sem, relu_done.count(L, u + 1))
                part_ = prob[:, u % 2, 0:IDX_COLS[t]]
                weight = wi[:, t, h:h + 1]
                if h == 0:
                    ins = nc.vector.tensor_scalar(scores_of(t), part_, weight, 0.0, ALU.mult, ALU.add)
                else:
                    dve.wait_ge(idx_added.sem, idx_added.count(L, u))
                    ins = nc.vector.scalar_tensor_tensor(out=scores_of(t), in0=part_, scalar=weight,
                                                         in1=scores_of(t), op0=ALU.mult, op1=ALU.add)
                ins.then_inc(idx_added.sem, 1)

            def choose_round(L, k):
                tiles = [t for t in (3, 2, 1, 4) if k < ROUNDS[t]]
                whole = {t: s_scores[:, :] if t == 4 else scores_of(t) for t in tiles}
                if k:
                    dve.wait_ge(top_taken.sem, top_taken.count(L, k))
                else:
                    dve.wait_ge(scores_ready.sem, scores_ready.count(L, 1))
                nc.vector.memset(waited[:, :], 0.0)
                for t in tiles:
                    ins = nc.vector.max(top8[:, t - 1, :], whole[t])
                ins.then_inc(top_found.sem, 1)
                dve.wait_ge(top_found.sem, top_found.count(L, k + 1))
                nc.vector.memset(waited[:, :], 0.0)
                for t in tiles:
                    ins = nc.vector.match_replace(whole[t], top8[:, t - 1, :], whole[t], TAKEN)
                ins.then_inc(top_taken.sem, 1)

            def rope_result(L, n, m, s, out, turns, factor=None):
                leave(L, n, m, s, tmp[:, 0, :], r[:, :], factor)
                dve.wait_ge(evacuated.sem, evacuated.count(L, m + 1))
                nc.vector.tensor_tensor(out, tmp[:, 0, :], cos_t[:, :], ALU.mult)
                dve.wait_ge(swapped.sem, swapped.count(L, turns + 1))
                nc.vector.tensor_tensor(tmp[:, 1, :], tmp[:, 1, :], sin_t[:, :], ALU.mult).then_inc(sin_done.sem, 1)
                dve.wait_ge(sin_done.sem, sin_done.count(L, turns + 1))
                nc.vector.tensor_tensor(out, out, tmp[:, 1, :], ALU.add).then_inc(roped.sem, 1)

            def convolve(L, ct):
                u, y = tmp[:, 1, :], tmp[:, 2, :]
                us = u[:, SEQ:T].rearrange("p (b t) -> p b t", t=NEW)
                ys = y[:, SEQ:T].rearrange("p (b t) -> p b t", t=NEW)
                w = [convw[:, ct, i:i + 1] for i in range(3)]
                st = state[:, ct, :, :]
                nc.vector.tensor_scalar(y, u, w[2], None, ALU.mult).then_inc(conv_step.sem, 1)
                steps = [(y[:, 1:SEQ], u[:, 0:SEQ - 1], w[1]), (ys[:, :, 1:NEW], us[:, :, 0:NEW - 1], w[1]),
                         (y[:, 2:SEQ], u[:, 0:SEQ - 2], w[0]), (ys[:, :, 2:NEW], us[:, :, 0:NEW - 2], w[0]),
                         (ys[:, :, 0:1], st[:, :, 1:2], w[1]), (ys[:, :, 0:2], st[:, :, 0:2], w[0])]
                for i, (out, src, weight) in enumerate(steps):
                    dve.wait_ge(conv_step.sem, conv_step.count(L, 8 * ct + 1 + i))
                    nc.vector.scalar_tensor_tensor(out=out, in0=src, scalar=weight, in1=out, op0=ALU.mult,
                                                   op1=ALU.add).then_inc(conv_step.sem, 1)
                dve.wait_ge(conv_step.sem, conv_step.count(L, 8 * ct + 7))
                nc.vector.tensor_tensor(y, y, r[:, :], ALU.mult).then_inc(conv_step.sem, 1)
                dve.wait_ge(conv_step.sem, conv_step.count(L, 8 * ct + 8))

            def row_max(L, u):
                dve.wait_ge(logits_done.sem, logits_done.count(L, u + 1))
                nc.vector.tensor_reduce(out=neg_max[:, u % 3:u % 3 + 1], in_=logit_banks[u % 3][:, 0:unit_columns(u)],
                                        axis=AX, op=ALU.max, negate=True).then_inc(max_done.sem, 1)

            def normalise(L, u):
                dve.wait_ge(exp_done.sem, exp_done.count(L, u + 1))
                nc.vector.reciprocal(inv[:, u % 3:u % 3 + 1], total[:, u % 3:u % 3 + 1]).then_inc(inv_done.sem, 1)
                dve.wait_ge(inv_done.sem, inv_done.count(L, u + 1))
                p_ = probs[u % 3][:, 0:unit_columns(u)]
                nc.vector.tensor_scalar(p_, p_, inv[:, u % 3:u % 3 + 1], None, ALU.mult).then_inc(prob_done.sem, 1)

            def keep_out(L, u):
                kind, a, h = ATT_UNITS[u]
                g = GROUP_OF[u]
                dve.wait_ge(pv_done.sem, pv_done.count(L, u + 1))
                if kind == "stream":
                    o = out_banks[g % 2][:, 0:P].rearrange("p (c n) -> p c n", c=AB)
                    for par in range(2):
                        lane = slice(64 * par, 64 * par + 64)
                        ins = nc.vector.tensor_copy(qT[lane, :, SEQ + NEW * a:SEQ + NEW * (a + 1)],
                                                    o[lane, :, NEW * par:NEW * (par + 1)])
                else:
                    ins = nc.vector.tensor_copy(qT[:, h // 2, a * P:(a + 1) * P], out_banks[g % 2][:, 0:P])
                ins.then_inc(o_kept.sem, 1)

            nc.vector.memset(ones[:, :], 1.0).then_inc(evacuated.sem, 1)
            nc.vector.memset(inv[:, :], 1.0).then_inc(evacuated.sem, 1)
            nc.vector.memset(neg_max[:, :], 0.0).then_inc(mixed.sem, 1)
            dve.wait_ge(evacuated.sem, 2)
            nc.vector.memset(masks[:, 0:P], 0.0).then_inc(ones_set, 1)
            dve.wait_ge(ones_set, 1)
            dve.wait_ge(consts_in, 16 * NCONST)
            nc.vector.tensor_copy(bmask[:, :], tmp[:, 0, 0:P])
            nc.vector.tensor_copy(ident_b[:, :], ident[:, :]).then_inc(ones_set, 1)
            dve.wait_ge(ones_set, 2)
            arm(0)
            dve.wait_ge(armed.sem, armed.count(0, 0))
            for j in range(KB):
                norm_block(0, 0, j)
            reciprocal_root(0, 0)
            with dve.Fori(0, DEPTH) as L:
                ffn(L, 0, FFN1_AT, 0)
                nc.vector.memset(qi_diag[:, :, :, :], 0.0)
                nc.vector.memset(masks[:, 0:P], 0.0)
                nc.vector.memset(s_scores[:, PAST + P:SLOTS], -TAKEN).then_inc(diag_cleared.sem, 1)
                dve.wait_ge(diag_cleared.sem, diag_cleared.count(L, 1))
                nc.vector.memset(masks[0:64, 64:P], MASK)
                n, m = MIX_AT, MIX_RES
                turns = 0

                def rope_next(out, factor=None):
                    nonlocal n, m, turns
                    rope_result(L, n, m, n % 2, out, turns, factor)
                    n, m, turns = n + 1, m + 1, turns + 1
                dve.wait_ge(newton.sem, newton.count(L, 5))
                rope_next(qiT[:, 0, :])
                rope_next(qiT[:, 1, :])
                rope_next(kiT[:, :])
                dve.wait_ge(turned_r.sem, turned_r.count(L, 1))
                nc.vector.tensor_copy(r_tok[:, :], bank[:, 1, 0:TT]).then_inc(r_tok_done.sem, 1)
                dve.wait_ge(r_tok_done.sem, r_tok_done.count(L, 1))
                dve.wait_ge(tile_done.sem, tile_done.count(L, n + 1))
                nc.vector.scalar_tensor_tensor(
                    out=wi[:, :, :], in0=flat(1)[:, 0:TT * IDX_HEADS].rearrange("p (t h) -> p t h", t=TT),
                    scalar=(64 ** -0.5) * (IDX_HEADS ** -0.5),
                    in1=r_tok[:, :].unsqueeze(2).to_broadcast([P, TT, IDX_HEADS]),
                    op0=ALU.mult, op1=ALU.mult).then_inc(evacuated.sem, 1)
                n, m = n + 1, m + 1
                rope_next(qT[:, 0, :], HD ** -0.5)
                for u in range(8):
                    add_head(L, u)
                rope_next(qT[:, 1, :], HD ** -0.5)
                for u in range(8, 16):
                    add_head(L, u)
                dve.wait_ge(idx_added.sem, idx_added.count(L, 16))
                for t in (1, 2, 3):
                    nc.vector.memset(scores_of(t)[0:64, IDX_COLS[t] - 64:IDX_COLS[t]], NEG)
                own = s_scores[:, PAST:PAST + P]
                nc.vector.tensor_tensor(own, own, bmask[:, :], ALU.add).then_inc(scores_ready.sem, 1)
                k = 0
                for c in range(2, AB):
                    rope_next(qT[:, c, :], HD ** -0.5)
                for c in range(AB):
                    rope_next(kT[:, c, :])
                    choose_round(L, k)
                    k += 1
                for c in range(AB):
                    dve.wait_ge(tile_done.sem, tile_done.count(L, n + 1))
                    nc.vector.tensor_tensor(v_sb[:, :, c * P:(c + 1) * P],
                                            flat(n % 2)[:, 0:TT * P].rearrange("p (t f) -> p t f", t=TT),
                                            r_tok[:, :].unsqueeze(2).to_broadcast([P, TT, P]),
                                            ALU.mult).then_inc(evacuated.sem, 1)
                    n, m = n + 1, m + 1
                    choose_round(L, k)
                    k += 1
                for ct in range(CB):
                    if ct:
                        dve.wait_ge(o_conv_lo.sem, o_conv_lo.count(L, ct))
                    leave(L, n, m, n % 2, tmp[:, 0, :], r[:, :])
                    dve.wait_ge(evacuated.sem, evacuated.count(L, m + 1))
                    nc.vector.tensor_tensor(tmp[:, 0, :], tmp[:, 0, :], r[:, :], ALU.mult).then_inc(cx_scaled.sem, 1)
                    choose_round(L, k)
                    k += 1
                    if ct:
                        dve.wait_ge(tails_kept.sem, tails_kept.count(L, ct))
                    dve.wait_ge(tile_done.sem, tile_done.count(L, n + 2))
                    dve.wait_ge(cx_scaled.sem, cx_scaled.count(L, ct + 1))
                    nc.vector.tensor_tensor(halves(tmp[:, 1, :]), res((n + 1) % 2), halves(tmp[:, 0, :]),
                                            ALU.mult).then_inc(evacuated.sem, 1)
                    dve.wait_ge(evacuated.sem, evacuated.count(L, m + 2))
                    convolve(L, ct)
                    if ct % 2:
                        choose_round(L, k)
                        k += 1
                    leave(L, n + 2, m + 2, (n + 2) % 2, tmp[:, 0, :], tmp[:, 2, :])
                    dve.wait_ge(o_conv_hi.sem, o_conv_hi.count(L, ct + 1))
                    nc.vector.tensor_tensor(g_lo[:, AB + ct, :], tmp[:, 0, :], g_hi[:, AB + ct, :].bitcast(F),
                                            ALU.subtract).then_inc(o_conv_lo.sem, 1)
                    n, m = n + 3, m + 3
                while k < NROUNDS:
                    choose_round(L, k)
                    k += 1
                dve.wait_ge(top_taken.sem, top_taken.count(L, NROUNDS))
                for t in (1, 2, 3):
                    at_ = t * (t + 1) * P // 2
                    nc.vector.tensor_scalar(masks[:, at_:at_ + IDX_COLS[t]], scores_of(t), -2e38, MASK,
                                            ALU.is_gt, ALU.mult)
                nc.vector.tensor_scalar(s_mask[:, :], scores_of(4), -2e38, MASK, ALU.is_gt,
                                        ALU.mult).then_inc(masks_ready.sem, 1)
                nc.vector.memset(q_diag[:, :, :, :], 0.0).then_inc(q_diag_cleared.sem, 1)
                for step in range(NU + 4):
                    if step < NU:
                        row_max(L, step)
                    if 0 <= step - 1 < NU:
                        normalise(L, step - 1)
                    if step - 4 in LAST_OF:
                        keep_out(L, step - 4)
                for c in range(AB):
                    dve.wait_ge(o_att_hi.sem, o_att_hi.count(L, c + 1))
                    nc.vector.tensor_tensor(g_lo[:, c, :], qT[:, c, :], g_hi[:, c, :].bitcast(F),
                                            ALU.subtract).then_inc(o_att_lo.sem, 1)
                with dve.Fori(0, KB // 2) as jj:
                    for j2 in range(2):
                        for s in range(2):
                            leave(L, GATE_AT + 3 * j2 + s + 6 * jj, 0, s, tmp[:, s, :], r[:, :])
                        dve.wait_ge(gate_done.sem, gate_done.count(L, 2 * j2 + 2 + 4 * jj))
                        dve.wait_ge(tile_done.sem, tile_done.count(L, GATE_AT + 3 * j2 + 3 + 6 * jj))
                        nc.vector.tensor_tensor(halves(tmp[:, 0, :]), bank[:, 0:2, 0:HALF], halves(tmp[:, 0, :]),
                                                ALU.mult).then_inc(mixed.sem, 1)
                        nc.vector.tensor_tensor(halves(tmp[:, 1, :]), bank[:, 2:4, 0:HALF], halves(tmp[:, 1, :]),
                                                ALU.mult).then_inc(mixed.sem, 1)
                        dve.wait_ge(mixed.sem, mixed.count(L, 3 * j2 + 2 + 6 * jj))
                        nc.vector.tensor_tensor(tmp[:, 2, :], tmp[:, 0, :], tmp[:, 1, :], ALU.add).then_inc(mixed.sem, 1)
                        dve.wait_ge(m_hi_done.sem, m_hi_done.count(L, j2 + 1 + 2 * jj))
                        nc.vector.tensor_tensor(m_lo[:, 2 * jj + j2, :], tmp[:, 2, :],
                                                m_hi[:, 2 * jj + j2, :].bitcast(F), ALU.subtract).then_inc(m_ready.sem, 1)
                closing(L, OUT_AT, OUT_RES, 2, 1.0)
                ffn(L, 1, FFN2_AT, FFN2_RES)
            dve.wait_ge(newton.sem, 5 * (3 * DEPTH + 1))
            for j in range(KB):
                nc.vector.scalar_tensor_tensor(out=x[:, j, :], in0=x[:, j, :], scalar=gain[:, j:j + 1], in1=r[:, :],
                                               op0=ALU.mult, op1=ALU.mult).then_inc(y_scaled, 1)


def unit_columns(u):
    kind, a, _ = ATT_UNITS[u]
    return PAST + P if kind == "stream" else (a + 1) * P


def diagonal(ap, start, step, count):
    return bass.AP(ap.tensor, ap.offset + start, [ap.ap[0], (step, count), (1, NEW)])


def kernel(x_prompt, x_sample, cache_k, cache_v, cache_kidx, state_conv, ffn1_norm, ffn1_up, ffn1_down,
           mix_norm, w_in, conv_w, w_branch, w_out, ffn2_norm, ffn2_up, ffn2_down, final_norm):
    import concourse.bacc as bacc
    from concourse.bass_utils import run_bass_kernel_spmd

    f32 = np.float32
    a = {k: np.asarray(v) for k, v in dict(
        x_prompt=x_prompt, x_sample=x_sample, cache_k=cache_k, cache_v=cache_v, cache_kidx=cache_kidx,
        state_conv=state_conv, ffn1_norm=ffn1_norm, ffn1_up=ffn1_up, ffn1_down=ffn1_down, mix_norm=mix_norm,
        w_in=w_in, conv_w=conv_w, w_branch=w_branch, w_out=w_out, ffn2_norm=ffn2_norm, ffn2_up=ffn2_up,
        ffn2_down=ffn2_down, final_norm=final_norm).items()}

    def blocks(w):
        return w.reshape(-1, P, w.shape[1]).transpose(1, 0, 2).reshape(P, -1)

    wts = np.zeros((ALL_TILES + 2, P, KB * P), f32)
    n = 0

    def put(w):
        nonlocal n
        b = blocks(w)
        wts[n, :, :b.shape[1]] = b
        n += 1

    def put_ffn(up, down):
        f0 = 0
        for nb in GROUPS:
            for f in range(f0, f0 + nb):
                put(up[:, f * P:(f + 1) * P])
                put(up[:, D_FF + f * P:D_FF + (f + 1) * P])
            for j in range(KB):
                put(down[f0 * P:(f0 + nb) * P, j * P:(j + 1) * P])
            f0 += nb

    for L in range(DEPTH):
        put_ffn(a["ffn1_up"][L], a["ffn1_down"][L])
        sizes = (ATT_W, ATT_W, ATT_W, 256, 64, IDX_HEADS, CONV_W, CONV_W, CONV_W, D_MODEL, D_MODEL)
        q, k, v, qi, ki, w_idx, cb, cc, cx, ga, gb = np.split(a["w_in"][L], np.cumsum(sizes)[:-1], axis=1)
        cols = lambda w, j: w[:, j * P:(j + 1) * P]
        put(cols(qi, 0))
        put(cols(qi, 1))
        put(np.concatenate([ki, ki], axis=1))
        put(w_idx)
        for w in (q, k, v):
            for j in range(AB):
                put(cols(w, j))
        for j in range(CB):
            put(cols(cx, j))
            put(cols(cc, j))
            put(cols(cb, j))
        for j in range(KB):
            put(cols(ga, j))
            put(cols(gb, j))
            put(cols(a["w_branch"][L], j))
        for j in range(KB):
            put(cols(a["w_out"][L], j))
        put_ffn(a["ffn2_up"][L], a["ffn2_down"][L])
    assert n == ALL_TILES

    x = np.concatenate([a["x_prompt"][0], a["x_sample"].reshape(-1, D_MODEL)]).T
    norms = []
    for L in range(DEPTH):
        norms += [a["ffn1_norm"][L], a["mix_norm"][L], a["ffn2_norm"][L]]
    norms.append(a["final_norm"])
    half = HD // 2
    freqs = (10000.0 ** (-np.arange(half, dtype=np.float64) / half)).astype(f32)
    pos = np.concatenate([np.arange(SEQ), np.tile(PAST + np.arange(NEW), STREAMS)]).astype(f32)
    angle = (pos[None, :] * freqs[:, None]).astype(f32).astype(np.float64)
    cos = np.tile(np.cos(angle), (4, 1)).astype(f32)
    sin = np.tile(np.concatenate([-np.sin(angle), np.sin(angle)]), (2, 1)).astype(f32)
    stream = np.arange(P) // NEW
    kc = a["cache_k"].reshape(DEPTH, STREAMS, PAST, AB, P).transpose(0, 1, 4, 3, 2)
    vc = a["cache_v"].reshape(DEPTH, STREAMS, 2, P, ATT_W).transpose(0, 1, 3, 2, 4)
    kidx = a["cache_kidx"].reshape(DEPTH, 4, 2, PAST, HD).transpose(0, 2, 4, 1, 3)
    arrays = {
        "wts": wts,
        "x_in": x.reshape(KB, P, T).transpose(1, 0, 2),
        "gains_in": np.concatenate([g.reshape(KB, P).T for g in norms], axis=1),
        "cos_in": cos,
        "sin_in": sin,
        "ident_in": np.eye(P, dtype=f32),
        "bmask_in": np.where(stream[:, None] == stream[None, :], 0.0, NEG).astype(f32),
        "convw_in": a["conv_w"].reshape(DEPTH, 3, CB, P).transpose(0, 3, 2, 1),
        "state_in": a["state_conv"].reshape(DEPTH, STREAMS, 2, CB, P).transpose(0, 4, 3, 1, 2),
        "kcache_in": kc.reshape(DEPTH, STREAMS, P, AB * PAST),
        "vcache_in": vc.reshape(DEPTH, STREAMS, P, 2 * ATT_W),
        "kidx_in": kidx.reshape(DEPTH, P, 4, PAST),
    }
    outs = {"y_out": (P, KB * T), "k_out": (DEPTH, P, AB, T), "v_out": (DEPTH, P, TT, ATT_W),
            "ki_out": (DEPTH, HD, T), "conv_out": (DEPTH, P, CB, 2 + 2 * STREAMS)}
    nc = bacc.Bacc("TRN2", target_bir_lowering=False, num_devices=1)
    args, maps = [], {}
    for name, v_ in arrays.items():
        maps[name] = np.ascontiguousarray(v_)
        args.append(nc.dram_tensor(name, v_.shape, F, kind="ExternalInput").ap())
    for name, shape in outs.items():
        args.append(nc.dram_tensor(name, shape, F, kind="ExternalOutput").ap())
    build(nc, *args)
    got = run_bass_kernel_spmd(nc, [maps], core_ids=[0]).results[0]

    y = got["y_out"].reshape(P, KB, T).transpose(2, 1, 0).reshape(T, D_MODEL)
    k_new = got["k_out"].transpose(0, 3, 2, 1).reshape(DEPTH, T, HEADS, HD)
    v_new = got["v_out"].transpose(0, 2, 1, 3).reshape(DEPTH, T, HEADS, HD)
    ki_new = got["ki_out"].transpose(0, 2, 1)
    tails = got["conv_out"].transpose(0, 3, 2, 1).reshape(DEPTH, 2 + 2 * STREAMS, CONV_W)
    prompt = lambda z: np.ascontiguousarray(z[:, None, :SEQ])
    streams = lambda z: np.ascontiguousarray(z[:, SEQ:].reshape((DEPTH, STREAMS, NEW) + z.shape[2:]))
    return (np.ascontiguousarray(y[None, :SEQ]), np.ascontiguousarray(y[SEQ:].reshape(STREAMS, NEW, D_MODEL)),
            prompt(k_new), prompt(v_new), prompt(ki_new), np.ascontiguousarray(tails[:, None, :2]),
            streams(k_new), streams(v_new), streams(ki_new),
            np.ascontiguousarray(tails[:, 2:].reshape(DEPTH, STREAMS, 2, CONV_W)))
```

```python
from contextlib import ExitStack

import numpy as np

import concourse.bass as bass
from concourse import mybir

D_MODEL, SEQ, DEPTH, STREAMS, NEW, PAST = 1024, 512, 2, 8, 16, 256
HEADS, HD, ATT_W = 8, 64, 512
IDX_HEADS, CONV_W, D_FF = 4, 512, 2816
EPS = 1e-6
TOP_PROMPT = min(256, SEQ // 4)
TOP_STREAM = min(256, (PAST + NEW) // 4)

P = 128
T = SEQ + STREAMS * NEW
HALF = T // 2
KB = D_MODEL // P
TT = T // P
FB = D_FF // P
GROUPS = [8, 7, 7]
AB = ATT_W // P
CB = CONV_W // P

FFN_TILES = 2 * FB + KB * len(GROUPS)
Q_AT, K_AT, V_AT = 3, 3 + AB + 1, 3 + 2 * AB + 1
PROJ = V_AT + KB // 2 + 3 * CB
PROJ_RES = 3 + 2 * AB + 3 + 3 * CB
MIX_TILES = PROJ + 3 * KB + KB
FFN1_AT, MIX_AT, FFN2_AT = 0, FFN_TILES, FFN_TILES + MIX_TILES
GATE_AT = MIX_AT + PROJ
OUT_AT = GATE_AT + 3 * KB
TILES = 2 * FFN_TILES + MIX_TILES
MIX_RES, GATE_RES = FFN_TILES, FFN_TILES + PROJ_RES
OUT_RES, FFN2_RES = GATE_RES + 2 * KB, GATE_RES + 3 * KB
RESULTS = FFN2_RES + FFN_TILES
ALL_TILES = DEPTH * TILES

NEG = -1e30
TAKEN = -3.0e38
MASK = -float(2 ** 100)

IDX_UNITS = [(t, h) for t in (3, 2, 1) for h in range(IDX_HEADS)] + [(4, h) for h in range(IDX_HEADS)]
IDX_COLS = {1: 2 * P, 2: 3 * P, 3: 4 * P, 4: PAST + P}
SLOTS = IDX_COLS[4] + (-TOP_STREAM) % 8
ROUNDS = {1: TOP_PROMPT // 8, 2: TOP_PROMPT // 8, 3: TOP_PROMPT // 8, 4: (TOP_STREAM + 7) // 8}
NROUNDS = max(ROUNDS.values())

ATT_UNITS = []
for _b in range(STREAMS):
    ATT_UNITS.append(("stream", _b, 0))
    ATT_UNITS += [("prompt", (4 * _b + i) // HEADS, (4 * _b + i) % HEADS) for i in range(4)]
NU = len(ATT_UNITS)
GROUP_OF, _g = [], -1
for _kind, _, _h in ATT_UNITS:
    _g += 1 if _kind == "stream" or _h % 2 == 0 else 0
    GROUP_OF.append(_g)
LAST_OF = [u for u in range(NU) if u == NU - 1 or GROUP_OF[u + 1] != GROUP_OF[u]]
NG = len(LAST_OF)

CONV_AT, CONV_RES = GATE_AT - 3 * CB, GATE_RES - 3 * CB
assert TILES % 2 == RESULTS % 2 == MIX_AT % 2 == MIX_RES % 2 == CONV_AT % 2 == CONV_RES % 2 == 0
EARLY_CONV = 6
BEFORE_V = 6
LATE_CONV = 3 * CB - EARLY_CONV
PIECES = [[] for _ in range(NU + 3)]
for _i in range(LATE_CONV * KB):
    PIECES[_i * (NU + 1) // (LATE_CONV * KB)].append(divmod(_i, KB))

F = mybir.dt.float32
R = mybir.dt.float32r
B16 = mybir.dt.bfloat16
ALU = mybir.AluOpType
ACT = mybir.ActivationFunctionType
AX = mybir.AxisListType.X


def build(nc, wts, x_in, gains_in, cos_in, sin_in, ident_in, bmask_in, convw_in, state_in,
          kcache_in, vcache_in, kidx_in, y_out, k_out, v_out, ki_out, conv_out):
    ctx = ExitStack()
    with ctx:
        spot = [(nc.sbuf_base + 31) // 32 * 32]

        def at(name, shape, dt, offset):
            return nc.alloc_sbuf_tensor_at(name, shape, dt, offset=offset)

        def new(name, shape, dt=F):
            offset = spot[0]
            spot[0] += (int(np.prod(shape[1:])) * (2 if dt == B16 else 4) + 31) // 32 * 32
            assert spot[0] <= nc.sbuf_usable_end, (name, spot[0] - nc.sbuf_usable_end)
            return at(name, shape, dt, offset), offset

        x, _ = new("x", [P, KB, T])
        h_hi, _ = new("h_hi", [P, KB, T], R)
        h_lo, _ = new("h_lo", [P, KB, T], R)
        g_hi, _ = new("g_hi", [P, KB, T], R)
        g_lo, _ = new("g_lo", [P, KB, T], R)
        w_raw, _ = new("w_raw", [P, 2, KB * P])
        w_hi, _ = new("w_hi", [P, 2, KB * P], R)
        w_lo, _ = new("w_lo", [P, 2, KB * P], R)
        m_hi, mix_at = new("m_hi", [P, KB, T], R)
        m_lo, _ = new("m_lo", [P, KB, T], R)
        part = 4 * T
        qT = at("qT", [P, AB, T], F, mix_at)
        kT = at("kT", [P, AB, T], F, mix_at + 4 * part)
        qiT = at("qiT", [P, 2, T], F, mix_at + 8 * part)
        kiT = at("kiT", [P, T], F, mix_at + 10 * part)
        v_sb = at("v_sb", [P, TT, ATT_W], F, mix_at + 11 * part)
        masks = at("masks", [P, 10 * P], B16, mix_at + 15 * part)
        cos_t, _ = new("cos_t", [P, T])
        sin_t, _ = new("sin_t", [P, T])
        r, _ = new("r", [P, T])
        sq, sq_at = new("sq", [P, T])
        acc, _ = new("acc", [P, T])
        q_diag = at("q_diag", [P, 2, AB, P], F, sq_at)
        caches, cache_at = new("caches", [P, 2, 2, KB * P])
        wiT = at("wiT", [P, T], F, cache_at)
        scores = at("scores", [P, 9 * P], F, cache_at)
        s_scores = at("s_scores", [P, SLOTS], F, cache_at + 4 * 9 * P)
        ki_cache = at("ki_cache", [P, 4, PAST], F, cache_at + 8 * KB * P)
        qi_diag = at("qi_diag", [P, 2, 4, P], F, cache_at + 12 * KB * P)
        assert 4 * 9 * P + 4 * SLOTS <= 8 * KB * P
        tmp, _ = new("tmp", [P, 3, T])
        prob, prob_at = new("prob", [P, 2, 4 * P])
        bmask_f = at("bmask_f", [P, P], F, prob_at)
        prob3 = at("prob3", [P, 4 * P], F, mix_at + 10 * part)
        pT = at("pT", [P, 2, 4 * P], F, mix_at + 8 * part)
        probs = [prob[:, 0, :], prob[:, 1, :], prob3[:, :]]
        s_mask, _ = new("s_mask", [P, IDX_COLS[4]], B16)
        bmask, _ = new("bmask", [P, P], B16)
        ident, _ = new("ident", [P, P])
        ident_b, _ = new("ident_b", [P, P], B16)
        spread, _ = new("spread", [P, 2, HEADS, NEW], B16)
        ones, _ = new("ones", [P, 1])
        gains, _ = new("gains", [P, (3 * DEPTH + 1) * KB])
        gain, _ = new("gain", [P, KB])
        convw, _ = new("convw", [P, CB, 3])
        state, _ = new("state", [P, CB, STREAMS, 2])
        tails, _ = new("tails", [P, CB, 2 + 2 * STREAMS])
        top8, _ = new("top8", [P, 4, 8])
        wi, _ = new("wi", [P, TT, IDX_HEADS])
        r_tok, _ = new("r_tok", [P, TT])
        neg_max, _ = new("neg_max", [P, 4])
        total, _ = new("total", [P, 4])
        inv, _ = new("inv", [P, 4])
        waited, _ = new("waited", [P, 1])

        lin = [ctx.enter_context(nc.psum_tensor(f"lin{i}", [P, 2, 512], F)) for i in range(2)]
        bank = ctx.enter_context(nc.psum_tensor("bank", [P, 4, 512], F))
        logit_banks = [bank[:, 0, :], bank[:, 1, :], lin[1][:, 1, :]]
        turn_bank = bank[:, 2, :]
        value_banks = [lin[1][:, 0, :]] + [bank[:, i, :] for i in range(4)]
        out_banks = [bank[:, 3, :], lin[1][:, 0, :]]

        def halves(ap):
            return ap.rearrange("p (a n) -> p a n", a=2)

        def res(slot):
            return lin[slot][:, :, 0:HALF]

        def flat(slot):
            return lin[slot][:, :, :].rearrange("p a n -> p (a n)")

        class Signal:
            def __init__(self, name, per_layer, ahead=0):
                self.sem = ctx.enter_context(nc.semaphore(name))
                self.per_layer, self.ahead = per_layer, ahead

            def count(self, L, k):
                return L * self.per_layer + (k + self.ahead)

        raw_in = [ctx.enter_context(nc.semaphore(f"raw_in{i}")) for i in range(2)]
        consts_in = ctx.enter_context(nc.semaphore("consts_in"))
        gains_landed = ctx.enter_context(nc.semaphore("gains_landed"))
        x_landed = [ctx.enter_context(nc.semaphore(f"x_landed{j}")) for j in range(KB)]
        hi_ready = Signal("hi_ready", TILES)
        lo_ready = Signal("lo_ready", TILES)
        tile_done = Signal("tile_done", TILES)
        evacuated = Signal("evacuated", RESULTS, 2)
        silu_done = Signal("silu_done", 2 * FB)
        silu_scaled = Signal("silu_scaled", 2 * FB)
        g_hi_done = Signal("g_hi_done", 2 * FB)
        g_ready = Signal("g_ready", 2 * FB)
        armed = Signal("armed", 3, 1)
        sq_done = Signal("sq_done", 3 * KB, KB)
        acc_done = Signal("acc_done", 3 * KB, KB)
        h_hi_done = Signal("h_hi_done", 3 * KB, KB)
        h_ready = Signal("h_ready", 3 * KB, KB)
        sum_done = Signal("sum_done", 3, 1)
        mean_done = Signal("mean_done", 3, 1)
        root_done = Signal("root_done", 3, 1)
        newton = Signal("newton", 15, 5)
        turned_r = Signal("turned_r", 1)
        r_tok_done = Signal("r_tok_done", 2)
        wi_copied = Signal("wi_copied", 1)
        swapped = Signal("swapped", 11)
        sin_done = Signal("sin_done", 11)
        roped = Signal("roped", 11)
        layer_in = Signal("layer_in", 48)
        diag_cleared = Signal("diag_cleared", 1)
        qi_placed = Signal("qi_placed", IDX_HEADS)
        idx_products = Signal("idx_products", 16)
        relu_done = Signal("relu_done", 16)
        idx_added = Signal("idx_added", 16)
        scores_ready = Signal("scores_ready", 1)
        top_found = Signal("top_found", NROUNDS)
        top_taken = Signal("top_taken", NROUNDS)
        masks_ready = Signal("masks_ready", 1)
        cx_scaled = Signal("cx_scaled", CB)
        conv_step = Signal("conv_step", 8 * CB)
        tails_kept = Signal("tails_kept", CB)
        o_conv_hi = Signal("o_conv_hi", CB)
        o_conv_lo = Signal("o_conv_lo", CB)
        q_diag_cleared = Signal("q_diag_cleared", 1)
        q_placed = Signal("q_placed", STREAMS)
        cache_in = [Signal(f"cache_in{i}", 16 * STREAMS) for i in range(2)]
        logits_done = Signal("logits_done", NU)
        max_done = Signal("max_done", NU)
        exp_done = Signal("exp_done", NU)
        inv_done = Signal("inv_done", NU)
        prob_done = Signal("prob_done", NU)
        turned = Signal("turned", NU)
        pT_done = Signal("pT_done", NU)
        pv_done = Signal("pv_done", NU)
        o_kept = Signal("o_kept", NG)
        o_att_hi = Signal("o_att_hi", AB)
        o_att_lo = Signal("o_att_lo", AB)
        gate_done = Signal("gate_done", 2 * KB)
        mixed = Signal("mixed", 3 * KB, 1)
        m_hi_done = Signal("m_hi_done", KB)
        m_ready = Signal("m_ready", KB)
        stored = Signal("stored", 16 * 3)
        tails_stored = Signal("tails_stored", 16)
        y_scaled = ctx.enter_context(nc.semaphore("y_scaled"))
        y_stored = ctx.enter_context(nc.semaphore("y_stored"))
        ident_in_place = ctx.enter_context(nc.semaphore("ident_in_place"))
        ones_set = ctx.enter_context(nc.semaphore("ones_set"))

        block = ctx.enter_context(nc.Block())
        NCONST = 4

        @block.sync
        def _(sp):
            for s in range(2):
                sp.dma_start(w_raw[:, s, :], wts[s]).then_inc(raw_in[s], 16)
            with sp.Fori(0, ALL_TILES // 2) as i:
                for s in range(2):
                    sp.wait_ge(lo_ready.sem, 2 * i + (s + 1))
                    sp.dma_start(w_raw[:, s, :], wts[2 * i + (s + 2)]).then_inc(raw_in[s], 16)

        @block.gpsimd
        def _(pool):
            with pool.Fori(0, ALL_TILES // 2 + 1) as i:
                for s in range(2):
                    pool.wait_ge(hi_ready.sem, 2 * i + (s + 1))
                    nc.gpsimd.tensor_tensor(w_lo[:, s, :], w_raw[:, s, :], w_hi[:, s, :].bitcast(F),
                                            ALU.subtract).then_inc(lo_ready.sem, 1)

        @block.tensor
        def _(pe):
            def passes(out, s, c, rhs_hi, rhs_lo, first, last):
                whi, wlo = w_hi[:, s, c * P:(c + 1) * P], w_lo[:, s, c * P:(c + 1) * P]
                for n, (w, a) in enumerate(((whi, rhs_hi), (whi, rhs_lo), (wlo, rhs_hi))):
                    for half in range(2):
                        ins = nc.tensor.matmul(out[:, half, :], w, a[:, half * HALF:(half + 1) * HALF],
                                               start=first and n == 0, stop=last and n == 2)
                return ins

            def linear(L, n, m, s, hi, lo, blocks=KB, before_last=None, out=None, after_block=None):
                out = res(s) if out is None else out
                pe.wait_ge(evacuated.sem, evacuated.count(L, m - 1))
                pe.wait_ge(lo_ready.sem, lo_ready.count(L, n + 1))
                for c in range(blocks):
                    if before_last and c == blocks - 1:
                        before_last()
                    ins = passes(out, s, c, hi[:, c, :], lo[:, c, :], c == 0, c == blocks - 1)
                    if after_block:
                        after_block()
                ins.then_inc(tile_done.sem, 1)

            def first_linear(L, n, m, p):
                s = n % 2
                pe.wait_ge(evacuated.sem, evacuated.count(L, m - 1))
                pe.wait_ge(lo_ready.sem, lo_ready.count(L, n + 1))
                for c in range(KB):
                    if c == KB - 1:
                        sum_squares(L, p)
                    pe.wait_ge(h_ready.sem, h_ready.count(L, (p - 1) * KB + c + 1))
                    ins = passes(res(m % 2), s, c, h_hi[:, c, :], h_lo[:, c, :], c == 0, c == KB - 1)
                ins.then_inc(tile_done.sem, 1)

            def value_tile(L, j):
                n = MIX_AT + V_AT + j
                pe.wait_ge(lo_ready.sem, lo_ready.count(L, n + 1))
                for c in range(2):
                    w = [z[:, n % 2, c * ATT_W:(c + 1) * ATT_W] for z in (w_hi, w_lo)]
                    for t in range(TT):
                        tok = [z[:, 2 * j + c, t * P:(t + 1) * P] for z in (h_hi, h_lo)]
                        for i, (a, b) in enumerate(((0, 0), (0, 1), (1, 0))):
                            ins = nc.tensor.matmul(value_banks[t], tok[a], w[b], start=j == c == i == 0,
                                                   stop=2 * j + c == KB - 1 and i == 2)
                ins.then_inc(tile_done.sem, 1)

            def sum_squares(L, p):
                pe.wait_ge(acc_done.sem, acc_done.count(L, p * KB))
                for half in range(2):
                    ins = nc.tensor.matmul(bank[:, 2 + half, 0:HALF], ones[:, 0:1].to_broadcast([P, P]),
                                           acc[:, half * HALF:(half + 1) * HALF], start=True, stop=True)
                ins.then_inc(sum_done.sem, 1)

            def ffn(L, f, n0, m0):
                done = 0
                for nb in GROUPS:
                    peeled = 0
                    if done == 0:
                        first_linear(L, n0, m0, (0, 2)[f])
                        linear(L, n0 + 1, m0 + 1, 1, h_hi, h_lo)
                        peeled = 1
                    with pe.Fori(peeled, nb) as i:
                        for s in range(2):
                            linear(L, n0 + s + 2 * i, m0 + s + 2 * i, s, h_hi, h_lo)
                    n0, m0, done = n0 + 2 * nb, m0 + 2 * nb, done + nb

                    def last_hidden():
                        pe.wait_ge(g_ready.sem, g_ready.count(L, f * FB + done))
                    with pe.Fori(0, KB // 2) as i:
                        pe.wait_ge(g_ready.sem, g_ready.count(L, f * FB + done - 1))
                        for s in range(2):
                            linear(L, n0 + s + 2 * i, m0 + s + 2 * i, s, g_hi, g_lo, nb,
                                   last_hidden if s == 0 else None)
                    n0, m0 = n0 + KB, m0 + KB

            def idx_unit(L, u):
                t, h = IDX_UNITS[u]
                out = bank[:, u % 4, :]
                lane = slice(64 * (h % 2), 64 * (h % 2) + 64)
                if u >= 4:
                    pe.wait_ge(relu_done.sem, relu_done.count(L, u - 3))
                if t < 4:
                    ins = nc.tensor.matmul(out[:, 0:IDX_COLS[t]], qiT[lane, h // 2, t * P:(t + 1) * P],
                                           kiT[lane, 0:IDX_COLS[t]], start=True, stop=True)
                else:
                    pe.wait_ge(qi_placed.sem, qi_placed.count(L, h + 1))
                    for pair in range(4):
                        nc.tensor.matmul(out[:, 0:PAST], qi_diag[:, h % 2, pair, :], ki_cache[:, pair, :],
                                         start=pair == 0, stop=pair == 3)
                    ins = nc.tensor.matmul(out[:, PAST:PAST + P], qiT[lane, h // 2, SEQ:T], kiT[lane, SEQ:T],
                                           start=True, stop=True)
                ins.then_inc(idx_products.sem, 1)

            def logits(L, u):
                kind, a, h = ATT_UNITS[u]
                out = logit_banks[u % 3]
                if u >= 3:
                    pe.wait_ge(exp_done.sem, exp_done.count(L, u - 2))
                if kind == "stream":
                    pe.wait_ge(q_placed.sem, q_placed.count(L, a + 1))
                    pe.wait_ge(cache_in[a % 2].sem, cache_in[a % 2].count(L, 32 * (a // 2 + 1)))
                    nc.tensor.matmul(out[:, 0:PAST + P], spread[:, a % 2, :, :].rearrange("p h t -> p (h t)"),
                                     s_mask[:, :], start=True, stop=False)
                    for c in range(AB):
                        w = q_diag[:, a % 2, c, :]
                        nc.tensor.matmul(out[:, 0:PAST], w, caches[:, a % 2, 0, c * PAST:(c + 1) * PAST],
                                         start=False, stop=False)
                        ins = nc.tensor.matmul(out[:, PAST:PAST + P], w, kT[:, c, SEQ:T],
                                               start=False, stop=c == AB - 1)
                else:
                    n = (a + 1) * P
                    lane = slice(64 * (h % 2), 64 * (h % 2) + 64)
                    nc.tensor.matmul(out[:, 0:n], ident_b[:, :], masks[:, a * n // 2:a * n // 2 + n],
                                     start=True, stop=False)
                    ins = nc.tensor.matmul(out[:, 0:n], qT[lane, h // 2, a * P:(a + 1) * P],
                                           kT[lane, h // 2, 0:n], start=False, stop=True)
                ins.then_inc(logits_done.sem, 1)

            def blocks_of(u):
                kind, a, _ = ATT_UNITS[u]
                return 3 if kind == "stream" else a + 1

            def turn(L, u):
                if u >= 1:
                    pe.wait_ge(pT_done.sem, pT_done.count(L, u))
                pe.wait_ge(prob_done.sem, prob_done.count(L, u + 1))
                for c in range(blocks_of(u)):
                    ins = nc.tensor.transpose(turn_bank[:, c * P:(c + 1) * P],
                                              probs[u % 3][:, c * P:(c + 1) * P], ident[:, :])
                ins.then_inc(turned.sem, 1)

            def weigh(L, u):
                kind, a, h = ATT_UNITS[u]
                g, nb = GROUP_OF[u], blocks_of(u)
                out = out_banks[g % 2]
                if g >= 2:
                    pe.wait_ge(o_kept.sem, o_kept.count(L, g - 1))
                pe.wait_ge(pT_done.sem, pT_done.count(L, u + 1))
                if kind == "stream":
                    for c in range(AB):
                        for b in range(nb):
                            v = (caches[:, a % 2, 1, b * ATT_W + c * P:b * ATT_W + (c + 1) * P] if b < 2
                                 else v_sb[:, TT - 1, c * P:(c + 1) * P])
                            ins = nc.tensor.matmul(out[:, c * 32:(c + 1) * 32], v,
                                                   pT[:, u % 2, b * P + c * 32:b * P + (c + 1) * 32],
                                                   start=b == 0, stop=b == nb - 1)
                else:
                    lane = slice(64 * (h % 2), 64 * (h % 2) + 64)
                    for b in range(nb):
                        ins = nc.tensor.matmul(out[lane, 0:P], v_sb[:, b, h * HD:(h + 1) * HD],
                                               pT[:, u % 2, b * P:(b + 1) * P], start=b == 0, stop=b == nb - 1)
                ins.then_inc(pv_done.sem, 1)

            pe.wait_ge(ones_set, 1)
            with pe.Fori(0, DEPTH) as L:
                ffn(L, 0, FFN1_AT, 0)
                first_linear(L, MIX_AT, MIX_RES, 1)
                n, m = MIX_AT + 1, MIX_RES + 1

                units = iter(range(len(IDX_UNITS)))

                def proj(after_block=None):
                    nonlocal n, m
                    linear(L, n, m, n % 2, h_hi, h_lo, out=res(m % 2), after_block=after_block)
                    n, m = n + 1, m + 1

                def next_unit():
                    idx_unit(L, next(units))
                proj()
                proj()
                pe.wait_ge(evacuated.sem, evacuated.count(L, m - 1))
                for part_ in range(2):
                    pe.wait_ge(lo_ready.sem, lo_ready.count(L, n + 1))
                    for c in range(KB // 2):
                        b = KB // 2 * part_ + c
                        ins = passes(res(m % 2), n % 2, c, h_hi[:, b, :], h_lo[:, b, :], b == 0, b == KB - 1)
                    ins.then_inc(tile_done.sem, 1)
                    n += 1
                m += 1
                pe.wait_ge(wi_copied.sem, wi_copied.count(L, 1))
                pe.wait_ge(newton.sem, newton.count(L, 5))
                for t in range(TT):
                    nc.tensor.matmul(bank[:, 1, t:t + 1], r[0:1, t * P:(t + 1) * P], ones[0:1, 0:1],
                                     start=True, stop=True)
                for t in range(TT):
                    ins = nc.tensor.transpose(bank[:, 2, 8 + IDX_HEADS * t:8 + IDX_HEADS * (t + 1)],
                                              wiT[64:64 + IDX_HEADS, t * P:(t + 1) * P],
                                              ident[64:64 + IDX_HEADS, 64:64 + IDX_HEADS])
                ins.then_inc(turned_r.sem, 1)
                pe.wait_ge(roped.sem, roped.count(L, 3))
                pe.wait_ge(r_tok_done.sem, r_tok_done.count(L, 2))
                proj(next_unit)
                pe.wait_ge(layer_in.sem, layer_in.count(L, 48))
                proj(next_unit)
                for _ in range(1 + AB):
                    proj()
                pe.wait_ge(relu_done.sem, relu_done.count(L, len(IDX_UNITS)))
                pe.wait_ge(evacuated.sem, evacuated.count(L, m - 1))
                for j in range(KB // 2):
                    value_tile(L, j)
                n, m = n + KB // 2, m + 3
                for _ in range(EARLY_CONV):
                    proj()
                pe.wait_ge(ident_in_place, 1)
                pe.wait_ge(masks_ready.sem, masks_ready.count(L, 1))
                pe.wait_ge(evacuated.sem, evacuated.count(L, m))
                for step in range(NU + 3):
                    if step < NU:
                        logits(L, step)
                    for tile, c in PIECES[step]:
                        n, m = CONV_AT + EARLY_CONV + tile, CONV_RES + EARLY_CONV + tile
                        if c == 0:
                            pe.wait_ge(evacuated.sem, evacuated.count(L, m))
                            pe.wait_ge(lo_ready.sem, lo_ready.count(L, n + 1))
                        ins = passes(res(0), n % 2, c, h_hi[:, c, :], h_lo[:, c, :], c == 0, c == KB - 1)
                        if c == KB - 1:
                            ins.then_inc(tile_done.sem, 1)
                    if 0 <= step - 2 < NU:
                        turn(L, step - 2)
                    if 0 <= step - 3 < NU:
                        weigh(L, step - 3)
                with pe.Fori(0, KB // 2) as jj:
                    pe.wait_ge(o_kept.sem, o_kept.count(L, NG))
                    pe.wait_ge(evacuated.sem, evacuated.count(L, GATE_RES))
                    for j2 in range(2):
                        for s in range(2):
                            pe.wait_ge(evacuated.sem, evacuated.count(L, GATE_RES - 1 + 2 * j2 + s + 4 * jj))
                            ring = (3 * j2 + s) % 2
                            pe.wait_ge(lo_ready.sem, lo_ready.count(L, GATE_AT + 1 + 3 * j2 + s + 6 * jj))
                            for c in range(KB):
                                ins = passes(res(s), ring, c, h_hi[:, c, :], h_lo[:, c, :], c == 0, c == KB - 1)
                            ins.then_inc(tile_done.sem, 1)
                        ring = (3 * j2 + 2) % 2
                        pe.wait_ge(o_att_lo.sem, o_att_lo.count(L, AB))
                        pe.wait_ge(lo_ready.sem, lo_ready.count(L, GATE_AT + 3 + 3 * j2 + 6 * jj))
                        pe.wait_ge(mixed.sem, mixed.count(L, 3 * j2 + 6 * jj))
                        for part_ in range(2):
                            for c in range(AB):
                                b = part_ * AB + c
                                ins = passes(bank[:, 2 * part_:2 * part_ + 2, 0:HALF], ring, b,
                                             g_hi[:, b, :], g_lo[:, b, :], c == 0, c == AB - 1)
                        ins.then_inc(tile_done.sem, 1)
                with pe.Fori(0, KB // 2) as i:
                    pe.wait_ge(m_ready.sem, m_ready.count(L, KB - 1))

                    def last_sum():
                        pe.wait_ge(m_ready.sem, m_ready.count(L, KB))
                    for s in range(2):
                        linear(L, OUT_AT + s + 2 * i, OUT_RES + s + 2 * i, s, m_hi, m_lo,
                               before_last=last_sum if s == 0 else None)
                ffn(L, 1, FFN2_AT, FFN2_RES)
            sum_squares(DEPTH, 0)

        @block.scalar
        def _(act):
            def split(L, k, i=0, step=2):
                s = k % 2
                act.wait_ge(tile_done.sem, L * TILES + (k - 1) + (step * i))
                act.wait_ge(raw_in[s], L * (8 * TILES) + 16 * (k // 2 + 1) + (8 * step) * i)
                nc.scalar.activation(w_hi[:, s, :], w_raw[:, s, :], ACT.Copy).then_inc(hi_ready.sem, 1)

            def norm_block(j, arrived):
                arrived()
                nc.scalar.activation(h_hi[:, j, :], x[:, j, :], ACT.Copy,
                                     scale=gain[:, j:j + 1]).then_inc(h_hi_done.sem, 1)
                nc.scalar.activation(sq[:, :], x[:, j, :], ACT.Square).then_inc(sq_done.sem, 1)

            def root(L, p):
                act.wait_ge(mean_done.sem, mean_done.count(L, p))
                nc.scalar.activation(tmp[:, 1, :], tmp[:, 0, :], ACT.Sqrt).then_inc(root_done.sem, 1)

            def closing(L, n0, m0, p):
                for j in range(KB):
                    split(L, n0 + j + 2)

                    def arrived():
                        if j:
                            act.wait_ge(acc_done.sem, acc_done.count(L, (p - 1) * KB + j))
                        act.wait_ge(evacuated.sem, evacuated.count(L, m0 + j + 1))
                    norm_block(j, arrived)
                root(L, p)

            def ffn(L, f, n0, m0):
                done = 0
                for g, nb in enumerate(GROUPS):
                    with act.Fori(0, nb) as i:
                        split(L, n0 + 2, i)
                        act.wait_ge(evacuated.sem, evacuated.count(L, m0 + 1 + 2 * i))
                        nc.scalar.activation(tmp[:, 1, :], tmp[:, 0, :], ACT.Silu).then_inc(silu_done.sem, 1)
                        split(L, n0 + 3, i)
                        act.wait_ge(evacuated.sem, evacuated.count(L, m0 + 2 + 2 * i))
                        nc.scalar.activation(g_hi[:, i, :], tmp[:, 2, :], ACT.Copy).then_inc(g_hi_done.sem, 1)
                    n0, m0, done = n0 + 2 * nb, m0 + 2 * nb, done + nb
                    if g < len(GROUPS) - 1:
                        with act.Fori(0, KB // 2) as i:
                            split(L, n0 + 2, i)
                            split(L, n0 + 3, i)
                    else:
                        closing(L, n0, m0, (1, 3)[f])
                    n0, m0 = n0 + KB, m0 + KB

            def relu(L, u):
                n = IDX_COLS[IDX_UNITS[u][0]]
                act.wait_ge(idx_products.sem, idx_products.count(L, u + 1))
                if u >= 2:
                    act.wait_ge(idx_added.sem, idx_added.count(L, u - 1))
                nc.scalar.activation(prob[:, u % 2, 0:n], bank[:, u % 4, 0:n], ACT.Relu).then_inc(relu_done.sem, 1)

            def place_qi(L, h):
                if h >= 2:
                    act.wait_ge(idx_products.sem, idx_products.count(L, 12 + h - 1))
                src = qiT[64 * (h % 2):64 * (h % 2) + 64, h // 2, SEQ:T].rearrange(
                    "p (pair par t) -> p pair par t", pair=4, par=2)
                for par in range(2):
                    dst = qi_diag[64 * par:64 * par + 64, h % 2, :, :].rearrange(
                        "p pair n -> p (pair n)")
                    dst = diagonal(dst, 16 * par, P + 2 * NEW, 4)
                    ins = nc.scalar.activation(dst, src[:, :, par, :], ACT.Copy)
                ins.then_inc(qi_placed.sem, 1)

            def load_cache(L, b):
                act.dma_start(caches[:, b % 2, 0, :], kcache_in[L, b]).then_inc(cache_in[b % 2].sem, 16)
                act.dma_start(caches[:, b % 2, 1, :], vcache_in[L, b]).then_inc(cache_in[b % 2].sem, 16)

            def place_q(L, b):
                if b >= 2:
                    act.wait_ge(logits_done.sem, logits_done.count(L, 5 * (b - 2) + 1))
                for par in range(2):
                    dst = q_diag[64 * par:64 * par + 64, b % 2, :, :].rearrange("p c n -> p (c n)")
                    dst = diagonal(dst, 16 * par, P + 2 * NEW, AB)
                    src = qT[64 * par:64 * par + 64, :, SEQ + NEW * b:SEQ + NEW * (b + 1)]
                    nc.scalar.activation(dst, src, ACT.Copy)
                nc.scalar.activation(spread[:, b % 2, :, :],
                                     ident_b[:, NEW * b:NEW * (b + 1)].unsqueeze(1).to_broadcast([P, HEADS, NEW]),
                                     ACT.Copy).then_inc(q_placed.sem, 1)

            def exps(L, u):
                n = unit_columns(u)
                if u >= 3:
                    act.wait_ge(turned.sem, turned.count(L, u - 2))
                act.wait_ge(max_done.sem, max_done.count(L, u + 1))
                nc.scalar.activation(probs[u % 3][:, 0:n], logit_banks[u % 3][:, 0:n], ACT.Exp,
                                     bias=neg_max[:, u % 3:u % 3 + 1],
                                     accum_out=total[:, u % 3:u % 3 + 1]).then_inc(exp_done.sem, 1)

            def take_turned(L, u):
                n = unit_columns(u)
                if u >= 2:
                    act.wait_ge(pv_done.sem, pv_done.count(L, u - 1))
                act.wait_ge(turned.sem, turned.count(L, u + 1))
                nc.scalar.activation(pT[:, u % 2, 0:n], turn_bank[:, 0:n], ACT.Copy).then_inc(pT_done.sem, 1)

            act.dma_start(gains[:, :], gains_in).then_inc(gains_landed, 16)
            for j in range(KB):
                act.dma_start(x[:, j, :], x_in[:, j, :]).then_inc(x_landed[j], 16)
            for dst, src in ((ident[:, :], ident_in), (cos_t[:, :], cos_in), (sin_t[:, :], sin_in),
                             (bmask_f[:, :], bmask_in)):
                act.dma_start(dst, src).then_inc(consts_in, 16)
            for s in range(2):
                act.wait_ge(raw_in[s], 16)
                nc.scalar.activation(w_hi[:, s, :], w_raw[:, s, :], ACT.Copy).then_inc(hi_ready.sem, 1)
            act.wait_ge(armed.sem, armed.count(0, 0))
            for j in range(KB):
                def arrived(j=j):
                    act.wait_ge(x_landed[j], 16)
                    if j:
                        act.wait_ge(acc_done.sem, acc_done.count(0, -KB + j))
                norm_block(j, arrived)
            root(0, 0)
            with act.Fori(0, DEPTH) as L:
                ffn(L, 0, FFN1_AT, 0)
                act.dma_start(convw[:, :, :], convw_in[L]).then_inc(layer_in.sem, 16)
                act.dma_start(state[:, :, :, :], state_in[L]).then_inc(layer_in.sem, 16)
                act.dma_start(ki_cache[:, :, :], kidx_in[L]).then_inc(layer_in.sem, 16)
                n = MIX_AT
                m = MIX_RES
                turns = 0

                def swap_halves():
                    nonlocal turns
                    act.wait_ge(evacuated.sem, evacuated.count(L, m + 1))
                    ki = turns == 2
                    for quarter in range(4):
                        to = 32 * (quarter ^ 1)
                        src = tmp[32 * (quarter % 2 if ki else quarter):, 0, :][0:32, :]
                        ins = nc.scalar.activation(tmp[to:to + 32, 1, :], src, ACT.Copy)
                    if ki:
                        nc.scalar.activation(wiT[64:64 + IDX_HEADS, :], tmp[64:64 + IDX_HEADS, 0, :],
                                             ACT.Copy).then_inc(wi_copied.sem, 1)
                        ins = nc.scalar.activation(tmp[64:P, 2, :], tmp[0:64, 0, :], ACT.Copy)
                    ins.then_inc(swapped.sem, 1)
                    turns += 1

                def conv_result(n, m):
                    ct, what = divmod(n - CONV_AT, 3)
                    if what == 1:
                        act.wait_ge(evacuated.sem, evacuated.count(L, m + 1))
                        nc.scalar.activation(tails[:, ct, 0:2], tmp[:, 1, SEQ - 2:SEQ], ACT.Copy)
                        nc.scalar.activation(
                            tails[:, ct, 2:].rearrange("p (b t) -> p b t", t=2),
                            tmp[:, 1, SEQ:T].rearrange("p (b t) -> p b t", t=NEW)[:, :, NEW - 2:NEW],
                            ACT.Copy).then_inc(tails_kept.sem, 1)
                    if what == 2:
                        act.wait_ge(evacuated.sem, evacuated.count(L, m + 1))
                        nc.scalar.activation(g_hi[:, AB + ct, :], tmp[:, 0, :], ACT.Copy).then_inc(o_conv_hi.sem, 1)

                def turn_of(n):
                    if n == MIX_AT + Q_AT + 2:
                        for u in range(8):
                            relu(L, u)
                    if n == MIX_AT + Q_AT + 3:
                        act.wait_ge(diag_cleared.sem, diag_cleared.count(L, 1))
                        place_qi(L, 0)
                        place_qi(L, 1)
                        for u in range(8, 12):
                            relu(L, u)
                        for h in range(IDX_HEADS):
                            relu(L, 12 + h)
                            if h + 2 < IDX_HEADS:
                                place_qi(L, h + 2)
                        act.dma_start(ki_out[L], kiT[0:64, :]).then_inc(stored.sem, 16)
                for what in (["rope"] * 3 + ["half", "rope"] + ["rope"] * (2 * AB - 1) + ["v"] * (KB // 2)
                             + ["conv"] * EARLY_CONV):
                    turn_of(n)
                    split(L, n + 2)
                    if what == "rope":
                        swap_halves()
                    if what == "conv":
                        conv_result(n, m)
                    n += 1
                    m += {"rope": 1, "conv": 1, "half": 0, "v": 0}[what]
                    if n == MIX_AT + V_AT + KB // 2:
                        m += 3
                act.wait_ge(masks_ready.sem, masks_ready.count(L, 1))
                load_cache(L, 0)
                act.wait_ge(q_diag_cleared.sem, q_diag_cleared.count(L, 1))
                load_cache(L, 1)
                act.wait_ge(stored.sem, stored.count(L, 16))
                act.dma_start(k_out[L], kT[:, :, :]).then_inc(stored.sem, 16)
                act.dma_start(v_out[L], v_sb[:, :, :]).then_inc(stored.sem, 16)
                place_q(L, 0)
                for step in range(NU + 3):
                    if step < NU:
                        kind, b, _ = ATT_UNITS[step]
                        exps(L, step)
                        if kind == "stream" and b + 1 < STREAMS:
                            place_q(L, b + 1)
                    if 0 <= step - 2 < NU:
                        take_turned(L, step - 2)
                    if step % 5 == 4 and step // 5 + 2 < STREAMS:
                        act.wait_ge(pv_done.sem, pv_done.count(L, 5 * (step // 5) + 1))
                        load_cache(L, step // 5 + 2)
                    for tile, c in PIECES[step]:
                        if c == KB - 1:
                            split(L, CONV_AT + EARLY_CONV + tile + 2)
                            conv_result(CONV_AT + EARLY_CONV + tile, CONV_RES + EARLY_CONV + tile)
                act.wait_ge(tails_kept.sem, tails_kept.count(L, CB))
                act.dma_start(conv_out[L], tails[:, :, :]).then_inc(tails_stored.sem, 16)
                act.wait_ge(o_kept.sem, o_kept.count(L, NG))
                for c in range(AB):
                    nc.scalar.activation(g_hi[:, c, :], qT[:, c, :], ACT.Copy).then_inc(o_att_hi.sem, 1)
                act.wait_ge(stored.sem, stored.count(L, 48))
                with act.Fori(0, KB // 2) as jj:
                    for j2 in range(2):
                        for s in range(2):
                            split(L, GATE_AT + 3 * j2 + s + 2, jj, 6)
                            act.wait_ge(evacuated.sem, evacuated.count(L, GATE_RES + 1 + 2 * j2 + s + 4 * jj))
                            nc.scalar.activation(tmp[:, s, :], tmp[:, s, :], ACT.Sigmoid).then_inc(gate_done.sem, 1)
                        split(L, GATE_AT + 3 * j2 + 4, jj, 6)
                        act.wait_ge(mixed.sem, mixed.count(L, 3 * j2 + 3 + 6 * jj))
                        nc.scalar.activation(m_hi[:, 2 * jj + j2, :], tmp[:, 2, :], ACT.Copy).then_inc(m_hi_done.sem, 1)
                closing(L, OUT_AT, OUT_RES, 2)
                act.wait_ge(tails_stored.sem, tails_stored.count(L, 16))
                ffn(L, 1, FFN2_AT, FFN2_RES)
            for j in range(KB):
                act.wait_ge(y_scaled, j + 1)
                act.dma_start(y_out[:, j * T:(j + 1) * T], x[:, j, :]).then_inc(y_stored, 16)
            act.wait_ge(y_stored, 16 * KB)

        @block.vector
        def _(dve):
            def leave(L, n, m, s, out, scaled_by, factor=None):
                dve.wait_ge(tile_done.sem, tile_done.count(L, n + 1))
                if factor is None:
                    ins = nc.vector.tensor_tensor(halves(out), res(s), halves(scaled_by), ALU.mult)
                else:
                    ins = nc.vector.scalar_tensor_tensor(out=halves(out), in0=res(s), scalar=factor,
                                                         in1=halves(scaled_by), op0=ALU.mult, op1=ALU.mult)
                ins.then_inc(evacuated.sem, 1)

            def arm(norm):
                nc.vector.memset(acc[:, :], 0.0)
                nc.vector.tensor_copy(gain[:, :], gains[:, bass.ds(norm * KB, KB)]).then_inc(armed.sem, 1)

            def norm_block(L, p, j):
                dve.wait_ge(h_hi_done.sem, h_hi_done.count(L, (p - 1) * KB + j + 1))
                nc.vector.scalar_tensor_tensor(out=h_lo[:, j, :], in0=x[:, j, :], scalar=gain[:, j:j + 1],
                                               in1=h_hi[:, j, :].bitcast(F), op0=ALU.mult,
                                               op1=ALU.subtract).then_inc(h_ready.sem, 1)
                dve.wait_ge(sq_done.sem, sq_done.count(L, (p - 1) * KB + j + 1))
                nc.vector.tensor_tensor(acc[:, :], acc[:, :], sq[:, :], ALU.add).then_inc(acc_done.sem, 1)

            def reciprocal_root(L, p):
                k = 5 * (p - 1)
                dve.wait_ge(sum_done.sem, sum_done.count(L, p))
                nc.vector.tensor_scalar(halves(tmp[:, 0, :]), bank[:, 2:4, 0:HALF], 1.0 / D_MODEL, EPS,
                                        ALU.mult, ALU.add).then_inc(mean_done.sem, 1)
                dve.wait_ge(root_done.sem, root_done.count(L, p))
                nc.vector.reciprocal(r[:, :], tmp[:, 1, :]).then_inc(newton.sem, 1)
                dve.wait_ge(newton.sem, newton.count(L, k + 1))
                nc.vector.tensor_tensor(tmp[:, 2, :], r[:, :], r[:, :], ALU.mult).then_inc(newton.sem, 1)
                dve.wait_ge(newton.sem, newton.count(L, k + 2))
                nc.vector.tensor_tensor(tmp[:, 2, :], tmp[:, 2, :], tmp[:, 0, :], ALU.mult).then_inc(newton.sem, 1)
                dve.wait_ge(newton.sem, newton.count(L, k + 3))
                nc.vector.tensor_scalar(tmp[:, 2, :], tmp[:, 2, :], -0.5, 1.5, ALU.mult, ALU.add).then_inc(newton.sem, 1)
                dve.wait_ge(newton.sem, newton.count(L, k + 4))
                nc.vector.tensor_tensor(r[:, :], r[:, :], tmp[:, 2, :], ALU.mult).then_inc(newton.sem, 1)

            def closing(L, n0, m0, p, factor):
                arm(3 * L + p)
                dve.wait_ge(armed.sem, armed.count(L, p))
                for j in range(KB):
                    dve.wait_ge(tile_done.sem, tile_done.count(L, n0 + j + 1))
                    nc.vector.scalar_tensor_tensor(out=halves(x[:, j, :]), in0=res((m0 + j) % 2), scalar=factor,
                                                   in1=halves(x[:, j, :]), op0=ALU.mult,
                                                   op1=ALU.add).then_inc(evacuated.sem, 1)
                    norm_block(L, p, j)
                reciprocal_root(L, p)

            def ffn(L, f, n0, m0):
                done = 0
                for g, nb in enumerate(GROUPS):
                    k = f * FB + done
                    with dve.Fori(0, nb) as i:
                        if done == 0:
                            dve.wait_ge(newton.sem, newton.count(L, (0, 10)[f]))
                        leave(L, n0 + 2 * i, m0, 0, tmp[:, 0, :], r[:, :])
                        dve.wait_ge(silu_done.sem, silu_done.count(L, k + 1 + i))
                        nc.vector.tensor_tensor(tmp[:, 1, :], tmp[:, 1, :], r[:, :], ALU.mult).then_inc(silu_scaled.sem, 1)
                        dve.wait_ge(silu_scaled.sem, silu_scaled.count(L, k + 1 + i))
                        leave(L, n0 + 1 + 2 * i, m0, 1, tmp[:, 2, :], tmp[:, 1, :])
                        dve.wait_ge(g_hi_done.sem, g_hi_done.count(L, k + 1 + i))
                        nc.vector.tensor_tensor(g_lo[:, i, :], tmp[:, 2, :], g_hi[:, i, :].bitcast(F),
                                                ALU.subtract).then_inc(g_ready.sem, 1)
                    n0, m0, done = n0 + 2 * nb, m0 + 2 * nb, done + nb
                    if g < len(GROUPS) - 1:
                        with dve.Fori(0, KB // 2) as i:
                            for s in range(2):
                                dve.wait_ge(tile_done.sem, tile_done.count(L, n0 + s + 1 + 2 * i))
                                xb = x[:, 2 * i + s, :]
                                nc.vector.scalar_tensor_tensor(out=halves(xb), in0=res(s), scalar=0.5,
                                                               in1=halves(xb), op0=ALU.mult,
                                                               op1=ALU.add).then_inc(evacuated.sem, 1)
                    else:
                        closing(L, n0, m0, (1, 3)[f], 0.5)
                    n0, m0 = n0 + KB, m0 + KB

            def scores_of(t):
                if t == 4:
                    return s_scores[:, 0:PAST + P]
                start = {1: 0, 2: 2 * P, 3: 5 * P}[t]
                return scores[:, start:start + IDX_COLS[t]]

            def add_head(L, u):
                t, h = IDX_UNITS[u]
                dve.wait_ge(relu_done.sem, relu_done.count(L, u + 1))
                part_ = prob[:, u % 2, 0:IDX_COLS[t]]
                weight = wi[:, t, h:h + 1]
                if h == 0:
                    ins = nc.vector.tensor_scalar(scores_of(t), part_, weight, 0.0, ALU.mult, ALU.add)
                else:
                    dve.wait_ge(idx_added.sem, idx_added.count(L, u))
                    ins = nc.vector.scalar_tensor_tensor(out=scores_of(t), in0=part_, scalar=weight,
                                                         in1=scores_of(t), op0=ALU.mult, op1=ALU.add)
                ins.then_inc(idx_added.sem, 1)

            def choose_round(L, k):
                tiles = [t for t in (3, 2, 1, 4) if k < ROUNDS[t]]
                whole = {t: s_scores[:, :] if t == 4 else scores_of(t) for t in tiles}
                if k:
                    dve.wait_ge(top_taken.sem, top_taken.count(L, k))
                else:
                    dve.wait_ge(scores_ready.sem, scores_ready.count(L, 1))
                nc.vector.memset(waited[:, :], 0.0)
                for t in tiles:
                    ins = nc.vector.max(top8[:, t - 1, :], whole[t])
                ins.then_inc(top_found.sem, 1)
                dve.wait_ge(top_found.sem, top_found.count(L, k + 1))
                nc.vector.memset(waited[:, :], 0.0)
                for t in tiles:
                    ins = nc.vector.match_replace(whole[t], top8[:, t - 1, :], whole[t], TAKEN)
                ins.then_inc(top_taken.sem, 1)

            def masks_from_scores(L):
                dve.wait_ge(top_taken.sem, top_taken.count(L, NROUNDS))
                for t in (1, 2, 3):
                    at_ = t * (t + 1) * P // 2
                    nc.vector.tensor_scalar(masks[:, at_:at_ + IDX_COLS[t]], scores_of(t), -2e38, MASK,
                                            ALU.is_gt, ALU.mult)
                nc.vector.tensor_scalar(s_mask[:, :], scores_of(4), -2e38, MASK, ALU.is_gt,
                                        ALU.mult).then_inc(masks_ready.sem, 1)
                nc.vector.memset(q_diag[:, :, :, :], 0.0).then_inc(q_diag_cleared.sem, 1)

            def rope_result(L, n, m, s, out, turns, factor=None):
                leave(L, n, m, s, tmp[:, 0, :], r[:, :], factor)
                dve.wait_ge(evacuated.sem, evacuated.count(L, m + 1))
                ki = turns == 2
                rows = slice(0, 64) if ki else slice(0, P)
                nc.vector.tensor_tensor(out[rows, :], tmp[rows, 0, :], cos_t[rows, :], ALU.mult)
                dve.wait_ge(swapped.sem, swapped.count(L, turns + 1))
                if ki:
                    nc.vector.tensor_tensor(out[64:P, :], tmp[64:P, 2, :], cos_t[64:P, :], ALU.mult)
                nc.vector.tensor_tensor(tmp[:, 1, :], tmp[:, 1, :], sin_t[:, :], ALU.mult).then_inc(sin_done.sem, 1)
                dve.wait_ge(sin_done.sem, sin_done.count(L, turns + 1))
                nc.vector.tensor_tensor(out, out, tmp[:, 1, :], ALU.add).then_inc(roped.sem, 1)

            def convolve(L, ct):
                u, y = tmp[:, 1, :], tmp[:, 2, :]
                us = u[:, SEQ:T].rearrange("p (b t) -> p b t", t=NEW)
                ys = y[:, SEQ:T].rearrange("p (b t) -> p b t", t=NEW)
                w = [convw[:, ct, i:i + 1] for i in range(3)]
                st = state[:, ct, :, :]
                nc.vector.tensor_scalar(y, u, w[2], None, ALU.mult).then_inc(conv_step.sem, 1)
                steps = [(y[:, 1:SEQ], u[:, 0:SEQ - 1], w[1]), (ys[:, :, 1:NEW], us[:, :, 0:NEW - 1], w[1]),
                         (y[:, 2:SEQ], u[:, 0:SEQ - 2], w[0]), (ys[:, :, 2:NEW], us[:, :, 0:NEW - 2], w[0]),
                         (ys[:, :, 0:1], st[:, :, 1:2], w[1]), (ys[:, :, 0:2], st[:, :, 0:2], w[0])]
                for i, (out, src, weight) in enumerate(steps):
                    dve.wait_ge(conv_step.sem, conv_step.count(L, 8 * ct + 1 + i))
                    nc.vector.scalar_tensor_tensor(out=out, in0=src, scalar=weight, in1=out, op0=ALU.mult,
                                                   op1=ALU.add).then_inc(conv_step.sem, 1)
                dve.wait_ge(conv_step.sem, conv_step.count(L, 8 * ct + 7))
                nc.vector.tensor_tensor(y, y, r[:, :], ALU.mult).then_inc(conv_step.sem, 1)
                dve.wait_ge(conv_step.sem, conv_step.count(L, 8 * ct + 8))

            def row_max(L, u):
                dve.wait_ge(logits_done.sem, logits_done.count(L, u + 1))
                nc.vector.tensor_reduce(out=neg_max[:, u % 3:u % 3 + 1], in_=logit_banks[u % 3][:, 0:unit_columns(u)],
                                        axis=AX, op=ALU.max, negate=True).then_inc(max_done.sem, 1)

            def normalise(L, u):
                dve.wait_ge(exp_done.sem, exp_done.count(L, u + 1))
                nc.vector.reciprocal(inv[:, u % 3:u % 3 + 1], total[:, u % 3:u % 3 + 1]).then_inc(inv_done.sem, 1)
                dve.wait_ge(inv_done.sem, inv_done.count(L, u + 1))
                p_ = probs[u % 3][:, 0:unit_columns(u)]
                nc.vector.tensor_scalar(p_, p_, inv[:, u % 3:u % 3 + 1], None, ALU.mult).then_inc(prob_done.sem, 1)

            def keep_out(L, u):
                kind, a, h = ATT_UNITS[u]
                g = GROUP_OF[u]
                dve.wait_ge(pv_done.sem, pv_done.count(L, u + 1))
                if kind == "stream":
                    o = out_banks[g % 2][:, 0:P].rearrange("p (c n) -> p c n", c=AB)
                    for par in range(2):
                        lane = slice(64 * par, 64 * par + 64)
                        ins = nc.vector.tensor_copy(qT[lane, :, SEQ + NEW * a:SEQ + NEW * (a + 1)],
                                                    o[lane, :, NEW * par:NEW * (par + 1)])
                else:
                    ins = nc.vector.tensor_copy(qT[:, h // 2, a * P:(a + 1) * P], out_banks[g % 2][:, 0:P])
                ins.then_inc(o_kept.sem, 1)

            nc.vector.memset(ones[:, :], 1.0).then_inc(evacuated.sem, 1)
            nc.vector.memset(inv[:, :], 1.0).then_inc(evacuated.sem, 1)
            nc.vector.memset(neg_max[:, :], 0.0).then_inc(mixed.sem, 1)
            dve.wait_ge(evacuated.sem, 2)
            nc.vector.memset(waited[:, :], 0.0).then_inc(ones_set, 1)
            dve.wait_ge(ones_set, 1)
            dve.wait_ge(gains_landed, 16)
            arm(0)
            dve.wait_ge(armed.sem, armed.count(0, 0))
            for j in range(KB):
                norm_block(0, 0, j)
            dve.wait_ge(consts_in, 16 * NCONST)
            nc.vector.tensor_copy(bmask[:, :], bmask_f[:, :])
            nc.vector.tensor_copy(ident_b[:, :], ident[:, :]).then_inc(ident_in_place, 1)
            reciprocal_root(0, 0)
            with dve.Fori(0, DEPTH) as L:
                ffn(L, 0, FFN1_AT, 0)
                nc.vector.memset(qi_diag[:, :, :, :], 0.0)
                nc.vector.memset(masks[:, 0:P], 0.0)
                nc.vector.memset(s_scores[:, PAST + P:SLOTS], -TAKEN).then_inc(diag_cleared.sem, 1)
                dve.wait_ge(diag_cleared.sem, diag_cleared.count(L, 1))
                nc.vector.memset(masks[0:64, 64:P], MASK)
                n, m = MIX_AT, MIX_RES
                turns = 0

                def rope_next(out, factor=None):
                    nonlocal n, m, turns
                    rope_result(L, n, m, m % 2, out, turns, factor)
                    n, m, turns = n + 1, m + 1, turns + 1
                dve.wait_ge(newton.sem, newton.count(L, 5))
                rope_next(qiT[:, 0, :])
                rope_next(qiT[:, 1, :])
                rope_next(kiT[:, :])
                n += 1
                rope_next(qT[:, 0, :], HD ** -0.5)
                dve.wait_ge(turned_r.sem, turned_r.count(L, 1))
                nc.vector.tensor_copy(r_tok[:, :], bank[:, 1, 0:TT]).then_inc(r_tok_done.sem, 1)
                nc.vector.tensor_scalar(
                    wi[:, :, :], bank[:, 2, 8:8 + TT * IDX_HEADS].rearrange("p (t h) -> p t h", t=TT),
                    (64 ** -0.5) * (IDX_HEADS ** -0.5), None, ALU.mult).then_inc(r_tok_done.sem, 1)
                dve.wait_ge(r_tok_done.sem, r_tok_done.count(L, 2))
                for u in range(8):
                    add_head(L, u)
                rope_next(qT[:, 1, :], HD ** -0.5)
                for u in range(8, 16):
                    add_head(L, u)
                rope_next(qT[:, 2, :], HD ** -0.5)
                dve.wait_ge(idx_added.sem, idx_added.count(L, 16))
                for t in (1, 2, 3):
                    nc.vector.memset(scores_of(t)[0:64, IDX_COLS[t] - 64:IDX_COLS[t]], NEG)
                own = s_scores[:, PAST:PAST + P]
                nc.vector.tensor_tensor(own, own, bmask[:, :], ALU.add).then_inc(scores_ready.sem, 1)
                k = 0
                rope_next(qT[:, 3, :], HD ** -0.5)
                choose_round(L, k)
                k += 1
                for c in range(AB):
                    rope_next(kT[:, c, :])
                    choose_round(L, k)
                    k += 1
                for _ in range(BEFORE_V):
                    choose_round(L, k)
                    k += 1
                n += KB // 2
                dve.wait_ge(tile_done.sem, tile_done.count(L, n))
                for t in range(TT):
                    ins = nc.vector.tensor_scalar(v_sb[:, t, :], value_banks[t], r_tok[:, t:t + 1], None, ALU.mult)
                    if t in (0, 1, TT - 1):
                        ins.then_inc(evacuated.sem, 1)
                m += 3

                def conv_result(n, m, s):
                    ct, what = divmod(n - CONV_AT, 3)
                    if what == 0:
                        if ct:
                            dve.wait_ge(o_conv_lo.sem, o_conv_lo.count(L, ct))
                        leave(L, n, m, s, tmp[:, 0, :], r[:, :])
                        dve.wait_ge(evacuated.sem, evacuated.count(L, m + 1))
                        nc.vector.tensor_tensor(tmp[:, 0, :], tmp[:, 0, :], r[:, :], ALU.mult).then_inc(cx_scaled.sem, 1)
                    elif what == 1:
                        if ct:
                            dve.wait_ge(tails_kept.sem, tails_kept.count(L, ct))
                        dve.wait_ge(tile_done.sem, tile_done.count(L, n + 1))
                        dve.wait_ge(cx_scaled.sem, cx_scaled.count(L, ct + 1))
                        nc.vector.tensor_tensor(halves(tmp[:, 1, :]), res(s), halves(tmp[:, 0, :]),
                                                ALU.mult).then_inc(evacuated.sem, 1)
                        dve.wait_ge(evacuated.sem, evacuated.count(L, m + 1))
                        convolve(L, ct)
                    else:
                        leave(L, n, m, s, tmp[:, 0, :], tmp[:, 2, :])
                        dve.wait_ge(o_conv_hi.sem, o_conv_hi.count(L, ct + 1))
                        nc.vector.tensor_tensor(g_lo[:, AB + ct, :], tmp[:, 0, :], g_hi[:, AB + ct, :].bitcast(F),
                                                ALU.subtract).then_inc(o_conv_lo.sem, 1)
                for _ in range(EARLY_CONV):
                    conv_result(n, m, m % 2)
                    n, m = n + 1, m + 1
                    if k < NROUNDS:
                        choose_round(L, k)
                        k += 1
                    if k == NROUNDS:
                        k += 1
                        masks_from_scores(L)
                for step in range(NU + 4):
                    if step < NU:
                        row_max(L, step)
                    if 0 <= step - 1 < NU:
                        normalise(L, step - 1)
                    if step - 4 in LAST_OF:
                        keep_out(L, step - 4)
                    for tile, c in PIECES[step] if step < NU + 3 else []:
                        if c == KB - 1:
                            conv_result(CONV_AT + EARLY_CONV + tile, CONV_RES + EARLY_CONV + tile, 0)
                for c in range(AB):
                    dve.wait_ge(o_att_hi.sem, o_att_hi.count(L, c + 1))
                    nc.vector.tensor_tensor(g_lo[:, c, :], qT[:, c, :], g_hi[:, c, :].bitcast(F),
                                            ALU.subtract).then_inc(o_att_lo.sem, 1)
                with dve.Fori(0, KB // 2) as jj:
                    for j2 in range(2):
                        for s in range(2):
                            leave(L, GATE_AT + 3 * j2 + s + 6 * jj, 0, s, tmp[:, s, :], r[:, :])
                        dve.wait_ge(gate_done.sem, gate_done.count(L, 2 * j2 + 2 + 4 * jj))
                        dve.wait_ge(tile_done.sem, tile_done.count(L, GATE_AT + 3 * j2 + 3 + 6 * jj))
                        nc.vector.tensor_tensor(halves(tmp[:, 0, :]), bank[:, 0:2, 0:HALF], halves(tmp[:, 0, :]),
                                                ALU.mult).then_inc(mixed.sem, 1)
                        nc.vector.tensor_tensor(halves(tmp[:, 1, :]), bank[:, 2:4, 0:HALF], halves(tmp[:, 1, :]),
                                                ALU.mult).then_inc(mixed.sem, 1)
                        dve.wait_ge(mixed.sem, mixed.count(L, 3 * j2 + 2 + 6 * jj))
                        nc.vector.tensor_tensor(tmp[:, 2, :], tmp[:, 0, :], tmp[:, 1, :], ALU.add).then_inc(mixed.sem, 1)
                        dve.wait_ge(m_hi_done.sem, m_hi_done.count(L, j2 + 1 + 2 * jj))
                        nc.vector.tensor_tensor(m_lo[:, 2 * jj + j2, :], tmp[:, 2, :],
                                                m_hi[:, 2 * jj + j2, :].bitcast(F), ALU.subtract).then_inc(m_ready.sem, 1)
                closing(L, OUT_AT, OUT_RES, 2, 1.0)
                ffn(L, 1, FFN2_AT, FFN2_RES)
            dve.wait_ge(newton.sem, 5 * (3 * DEPTH + 1))
            for j in range(KB):
                nc.vector.scalar_tensor_tensor(out=x[:, j, :], in0=x[:, j, :], scalar=gain[:, j:j + 1], in1=r[:, :],
                                               op0=ALU.mult, op1=ALU.mult).then_inc(y_scaled, 1)


def unit_columns(u):
    kind, a, _ = ATT_UNITS[u]
    return PAST + P if kind == "stream" else (a + 1) * P


def diagonal(ap, start, step, count):
    return bass.AP(ap.tensor, ap.offset + start, [ap.ap[0], (step, count), (1, NEW)])


def kernel(x_prompt, x_sample, cache_k, cache_v, cache_kidx, state_conv, ffn1_norm, ffn1_up, ffn1_down,
           mix_norm, w_in, conv_w, w_branch, w_out, ffn2_norm, ffn2_up, ffn2_down, final_norm):
    import concourse.bacc as bacc
    from concourse.bass_utils import run_bass_kernel_spmd

    f32 = np.float32
    a = {k: np.asarray(v) for k, v in dict(
        x_prompt=x_prompt, x_sample=x_sample, cache_k=cache_k, cache_v=cache_v, cache_kidx=cache_kidx,
        state_conv=state_conv, ffn1_norm=ffn1_norm, ffn1_up=ffn1_up, ffn1_down=ffn1_down, mix_norm=mix_norm,
        w_in=w_in, conv_w=conv_w, w_branch=w_branch, w_out=w_out, ffn2_norm=ffn2_norm, ffn2_up=ffn2_up,
        ffn2_down=ffn2_down, final_norm=final_norm).items()}

    def blocks(w):
        return w.reshape(-1, P, w.shape[1]).transpose(1, 0, 2).reshape(P, -1)

    wts = np.zeros((ALL_TILES + 2, P, KB * P), f32)
    n = 0

    def put(w):
        nonlocal n
        b = blocks(w)
        wts[n, :, :b.shape[1]] = b
        n += 1

    def put_ffn(up, down):
        f0 = 0
        for nb in GROUPS:
            for f in range(f0, f0 + nb):
                put(up[:, f * P:(f + 1) * P])
                put(up[:, D_FF + f * P:D_FF + (f + 1) * P])
            for j in range(KB):
                put(down[f0 * P:(f0 + nb) * P, j * P:(j + 1) * P])
            f0 += nb

    for L in range(DEPTH):
        put_ffn(a["ffn1_up"][L], a["ffn1_down"][L])
        sizes = (ATT_W, ATT_W, ATT_W, 256, 64, IDX_HEADS, CONV_W, CONV_W, CONV_W, D_MODEL, D_MODEL)
        q, k, v, qi, ki, w_idx, cb, cc, cx, ga, gb = np.split(a["w_in"][L], np.cumsum(sizes)[:-1], axis=1)
        cols = lambda w, j: w[:, j * P:(j + 1) * P]
        put(cols(qi, 0))
        put(cols(qi, 1))
        put(np.concatenate([ki, w_idx, np.zeros((D_MODEL, P - HD - IDX_HEADS), f32)], axis=1))
        put(cols(q, 0)[:D_MODEL // 2])
        put(cols(q, 0)[D_MODEL // 2:])
        for j in range(1, AB):
            put(cols(q, j))
        for j in range(AB):
            put(cols(k, j))
        for j in range(KB // 2):
            put(v[2 * j * P:2 * (j + 1) * P])
        for j in range(CB):
            put(cols(cx, j))
            put(cols(cc, j))
            put(cols(cb, j))
        for j in range(KB):
            put(cols(ga, j))
            put(cols(gb, j))
            put(cols(a["w_branch"][L], j))
        for j in range(KB):
            put(cols(a["w_out"][L], j))
        put_ffn(a["ffn2_up"][L], a["ffn2_down"][L])
    assert n == ALL_TILES

    x = np.concatenate([a["x_prompt"][0], a["x_sample"].reshape(-1, D_MODEL)]).T
    norms = []
    for L in range(DEPTH):
        norms += [a["ffn1_norm"][L], a["mix_norm"][L], a["ffn2_norm"][L]]
    norms.append(a["final_norm"])
    half = HD // 2
    freqs = (10000.0 ** (-np.arange(half, dtype=np.float64) / half)).astype(f32)
    pos = np.concatenate([np.arange(SEQ), np.tile(PAST + np.arange(NEW), STREAMS)]).astype(f32)
    angle = (pos[None, :] * freqs[:, None]).astype(f32).astype(np.float64)
    cos = np.tile(np.cos(angle), (4, 1)).astype(f32)
    sin = np.tile(np.concatenate([-np.sin(angle), np.sin(angle)]), (2, 1)).astype(f32)
    stream = np.arange(P) // NEW
    kc = a["cache_k"].reshape(DEPTH, STREAMS, PAST, AB, P).transpose(0, 1, 4, 3, 2)
    vc = a["cache_v"].reshape(DEPTH, STREAMS, 2, P, ATT_W).transpose(0, 1, 3, 2, 4)
    kidx = a["cache_kidx"].reshape(DEPTH, 4, 2, PAST, HD).transpose(0, 2, 4, 1, 3)
    arrays = {
        "wts": wts,
        "x_in": x.reshape(KB, P, T).transpose(1, 0, 2),
        "gains_in": np.concatenate([g.reshape(KB, P).T for g in norms], axis=1),
        "cos_in": cos,
        "sin_in": sin,
        "ident_in": np.eye(P, dtype=f32),
        "bmask_in": np.where(stream[:, None] == stream[None, :], 0.0, NEG).astype(f32),
        "convw_in": a["conv_w"].reshape(DEPTH, 3, CB, P).transpose(0, 3, 2, 1),
        "state_in": a["state_conv"].reshape(DEPTH, STREAMS, 2, CB, P).transpose(0, 4, 3, 1, 2),
        "kcache_in": kc.reshape(DEPTH, STREAMS, P, AB * PAST),
        "vcache_in": vc.reshape(DEPTH, STREAMS, P, 2 * ATT_W),
        "kidx_in": kidx.reshape(DEPTH, P, 4, PAST),
    }
    outs = {"y_out": (P, KB * T), "k_out": (DEPTH, P, AB, T), "v_out": (DEPTH, P, TT, ATT_W),
            "ki_out": (DEPTH, HD, T), "conv_out": (DEPTH, P, CB, 2 + 2 * STREAMS)}
    nc = bacc.Bacc("TRN2", target_bir_lowering=False, num_devices=1)
    args, maps = [], {}
    for name, v_ in arrays.items():
        maps[name] = np.ascontiguousarray(v_)
        args.append(nc.dram_tensor(name, v_.shape, F, kind="ExternalInput").ap())
    for name, shape in outs.items():
        args.append(nc.dram_tensor(name, shape, F, kind="ExternalOutput").ap())
    build(nc, *args)
    got = run_bass_kernel_spmd(nc, [maps], core_ids=[0]).results[0]

    y = got["y_out"].reshape(P, KB, T).transpose(2, 1, 0).reshape(T, D_MODEL)
    k_new = got["k_out"].transpose(0, 3, 2, 1).reshape(DEPTH, T, HEADS, HD)
    v_new = got["v_out"].transpose(0, 2, 1, 3).reshape(DEPTH, T, HEADS, HD)
    ki_new = got["ki_out"].transpose(0, 2, 1)
    tails = got["conv_out"].transpose(0, 3, 2, 1).reshape(DEPTH, 2 + 2 * STREAMS, CONV_W)
    prompt = lambda z: np.ascontiguousarray(z[:, None, :SEQ])
    streams = lambda z: np.ascontiguousarray(z[:, SEQ:].reshape((DEPTH, STREAMS, NEW) + z.shape[2:]))
    return (np.ascontiguousarray(y[None, :SEQ]), np.ascontiguousarray(y[SEQ:].reshape(STREAMS, NEW, D_MODEL)),
            prompt(k_new), prompt(v_new), prompt(ki_new), np.ascontiguousarray(tails[:, None, :2]),
            streams(k_new), streams(v_new), streams(ki_new),
            np.ascontiguousarray(tails[:, 2:].reshape(DEPTH, STREAMS, 2, CONV_W)))
```

```python
from contextlib import ExitStack

import numpy as np

import concourse.bass as bass
from concourse import mybir

D_MODEL, SEQ, DEPTH, STREAMS, NEW, PAST = 1024, 512, 2, 8, 16, 256
HEADS, HD, ATT_W = 8, 64, 512
IDX_HEADS, CONV_W, D_FF = 4, 512, 2816
EPS = 1e-6
TOP_PROMPT = min(256, SEQ // 4)
TOP_STREAM = min(256, (PAST + NEW) // 4)

P = 128
T = SEQ + STREAMS * NEW
KEYS = PAST + NEW
HALF = T // 2
KB = D_MODEL // P
TT = T // P
FB = D_FF // P
GROUPS = [8, 7, 7]
AB = ATT_W // P
CB = CONV_W // P

FFN_TILES = 2 * FB + KB * len(GROUPS)
Q_AT, V_AT = 3, 3 + 2 * AB + 1
PROJ = V_AT + KB // 2 + 3 * CB
PROJ_RES = 3 + 2 * AB + 1 + 3 * CB
MIX_TILES = PROJ + 3 * KB + KB
FFN1_AT, MIX_AT, FFN2_AT = 0, FFN_TILES, FFN_TILES + MIX_TILES
GATE_AT = MIX_AT + PROJ
OUT_AT = GATE_AT + 3 * KB
TILES = 2 * FFN_TILES + MIX_TILES
MIX_RES, GATE_RES = FFN_TILES, FFN_TILES + PROJ_RES
OUT_RES, FFN2_RES = GATE_RES + 2 * KB, GATE_RES + 3 * KB
RESULTS = FFN2_RES + FFN_TILES
ALL_TILES = DEPTH * TILES

NEG = -1e30
TAKEN = -3.0e38
MASK = -float(2 ** 100)

IDX_UNITS = [(t, h) for t in (3, 2, 1) for h in range(IDX_HEADS)] + [(4, h) for h in range(IDX_HEADS)]
IDX_COLS = {1: 2 * P, 2: 3 * P, 3: 4 * P, 4: PAST + P}
SLOTS = IDX_COLS[4] + (-TOP_STREAM) % 8
ROUNDS = {1: TOP_PROMPT // 8, 2: TOP_PROMPT // 8, 3: TOP_PROMPT // 8, 4: (TOP_STREAM + 7) // 8}
NROUNDS = max(ROUNDS.values())

ATT_UNITS = []
for _b in range(STREAMS):
    ATT_UNITS.append(("stream", _b, 0))
    ATT_UNITS += [("prompt", (4 * _b + i) // HEADS, (4 * _b + i) % HEADS) for i in range(4)]
NU = len(ATT_UNITS)
GROUP_OF, _g = [], -1
for _kind, _, _h in ATT_UNITS:
    _g += 1 if _kind == "stream" or _h % 2 == 0 else 0
    GROUP_OF.append(_g)
LAST_OF = [u for u in range(NU) if u == NU - 1 or GROUP_OF[u + 1] != GROUP_OF[u]]
NG = len(LAST_OF)

CONV_AT, CONV_RES = GATE_AT - 3 * CB, GATE_RES - 3 * CB
assert TILES % 2 == RESULTS % 2 == MIX_AT % 2 == MIX_RES % 2 == CONV_AT % 2 == CONV_RES % 2 == 0
EARLY_CONV = 6
SPREAD_AFTER = 4
BEFORE_V = 5
LATE_CONV = 3 * CB - EARLY_CONV
PIECES = [[] for _ in range(NU + 3)]
for _i in range(LATE_CONV * KB):
    PIECES[_i * (NU + 1) // (LATE_CONV * KB)].append(divmod(_i, KB))

F = mybir.dt.float32
R = mybir.dt.float32r
B16 = mybir.dt.bfloat16
ALU = mybir.AluOpType
ACT = mybir.ActivationFunctionType
AX = mybir.AxisListType.X


def build(nc, wts, x_in, gains_in, cos_in, sin_in, ident_in, bmask_in, convw_in, state_in,
          kcache_in, vcache_in, kidx_in, y_out, k_out, v_out, ki_out, conv_out):
    ctx = ExitStack()
    with ctx:
        spot = [(nc.sbuf_base + 31) // 32 * 32]

        def at(name, shape, dt, offset):
            return nc.alloc_sbuf_tensor_at(name, shape, dt, offset=offset)

        def new(name, shape, dt=F):
            offset = spot[0]
            spot[0] += (int(np.prod(shape[1:])) * (2 if dt == B16 else 4) + 31) // 32 * 32
            assert spot[0] <= nc.sbuf_usable_end, (name, spot[0] - nc.sbuf_usable_end)
            return at(name, shape, dt, offset), offset

        x, _ = new("x", [P, KB, T])
        h_hi, _ = new("h_hi", [P, KB, T], R)
        h_lo, _ = new("h_lo", [P, KB, T], R)
        g_hi, g_hi_at = new("g_hi", [P, KB, T], R)
        g_lo, g_lo_at = new("g_lo", [P, KB, T], R)
        w_raw, _ = new("w_raw", [P, 2, KB * P])
        w_hi, _ = new("w_hi", [P, 2, KB * P], R)
        w_lo, _ = new("w_lo", [P, 2, KB * P], R)
        OWN = 4 * T // ATT_W
        v_own_hi = at("v_own_hi", [NEW, OWN, ATT_W], F, g_hi_at)
        v_own_lo = at("v_own_lo", [NEW, OWN, ATT_W], F, g_lo_at)
        v_own = [(v_own_hi, v_own_lo)[b // OWN][:, b % OWN, :] for b in range(STREAMS)]
        m_hi, mix_at = new("m_hi", [P, KB, T], R)
        m_lo, _ = new("m_lo", [P, KB, T], R)
        part = 4 * T
        qT = at("qT", [P, AB, T], F, mix_at)
        kT = at("kT", [P, AB, T], F, mix_at + 4 * part)
        qiT = at("qiT", [P, 2, T], F, mix_at + 8 * part)
        kiT = at("kiT", [P, T], F, mix_at + 10 * part)
        v_sb = at("v_sb", [P, TT, ATT_W], F, mix_at + 11 * part)
        masks = at("masks", [P, 10 * P], B16, mix_at + 15 * part)
        cos_t, _ = new("cos_t", [P, T])
        sin_t, _ = new("sin_t", [P, T])
        r, _ = new("r", [P, T])
        sq, sq_at = new("sq", [P, T])
        acc, _ = new("acc", [P, T])
        q_diag = at("q_diag", [P, 2, AB, P], F, sq_at)
        cache_words = AB * KEYS + 2 * ATT_W
        caches, cache_at = new("caches", [P, 2, cache_words])
        k_cache = [caches[:, i, 0:AB * KEYS].rearrange("p (c n) -> p c n", c=AB) for i in range(2)]
        v_cache = [caches[:, i, AB * KEYS:] for i in range(2)]
        wiT = at("wiT", [P, T], F, cache_at)
        scores = at("scores", [P, 9 * P], F, cache_at)
        s_scores = at("s_scores", [P, SLOTS], F, cache_at + 4 * 9 * P)
        ki_cache = at("ki_cache", [P, 4, PAST], F, cache_at + 4 * cache_words)
        qi_diag = at("qi_diag", [P, 2, 4, P], F, cache_at + 4 * cache_words + 16 * PAST)
        assert 9 * P + SLOTS <= cache_words and 4 * PAST + 8 * P <= cache_words
        tmp, _ = new("tmp", [P, 3, T])
        prob, prob_at = new("prob", [P, 2, 4 * P])
        bmask_f = at("bmask_f", [P, P], F, prob_at)
        prob3 = at("prob3", [P, 4 * P], F, mix_at + 10 * part)
        pT = at("pT", [P, 2, 4 * P], F, mix_at + 8 * part)
        probs = [prob[:, 0, :], prob[:, 1, :], prob3[:, :]]
        s_mask, _ = new("s_mask", [P, KEYS], B16)
        bmask, _ = new("bmask", [P, P], B16)
        ident, _ = new("ident", [P, P])
        ident_b, _ = new("ident_b", [P, P], B16)
        spread, _ = new("spread", [P, 2, HEADS, NEW], B16)
        ones, _ = new("ones", [P, 1])
        gains, _ = new("gains", [P, (3 * DEPTH + 1) * KB])
        gain, _ = new("gain", [P, KB])
        convw, _ = new("convw", [P, CB, 3])
        state, _ = new("state", [P, CB, STREAMS, 2])
        tails, _ = new("tails", [P, CB, 2 + 2 * STREAMS])
        top8, _ = new("top8", [P, 4, 8])
        wi, _ = new("wi", [P, TT, IDX_HEADS])
        stats, _ = new("stats", [P, 3, TT])
        r_tok, _ = new("r_tok", [P, TT])
        neg_max, _ = new("neg_max", [P, 4])
        total, _ = new("total", [P, 4])
        inv, _ = new("inv", [P, 4])
        waited, _ = new("waited", [P, 1])

        lin = [ctx.enter_context(nc.psum_tensor(f"lin{i}", [P, 2, 512], F)) for i in range(2)]
        bank = ctx.enter_context(nc.psum_tensor("bank", [P, 4, 512], F))
        logit_banks = [bank[:, 0, :], bank[:, 1, :], lin[1][:, 1, :]]
        turn_bank = bank[:, 2, :]
        value_banks = [lin[1][:, 0, :]] + [bank[:, i, :] for i in range(4)]
        out_banks = [bank[:, 3, :], lin[1][:, 0, :]]

        def halves(ap):
            return ap.rearrange("p (a n) -> p a n", a=2)

        def res(slot):
            return lin[slot][:, :, 0:HALF]

        class Signal:
            def __init__(self, name, per_layer, ahead=0):
                self.sem = ctx.enter_context(nc.semaphore(name))
                self.per_layer, self.ahead = per_layer, ahead

            def count(self, L, k):
                return L * self.per_layer + (k + self.ahead)

        raw_in = [ctx.enter_context(nc.semaphore(f"raw_in{i}")) for i in range(2)]
        consts_in = ctx.enter_context(nc.semaphore("consts_in"))
        gains_landed = ctx.enter_context(nc.semaphore("gains_landed"))
        x_landed = [ctx.enter_context(nc.semaphore(f"x_landed{j}")) for j in range(KB)]
        hi_ready = Signal("hi_ready", TILES)
        lo_ready = Signal("lo_ready", TILES)
        tile_done = Signal("tile_done", TILES)
        evacuated = Signal("evacuated", RESULTS, 2)
        silu_done = Signal("silu_done", 2 * FB)
        silu_scaled = Signal("silu_scaled", 2 * FB)
        g_hi_done = Signal("g_hi_done", 2 * FB)
        g_ready = Signal("g_ready", 2 * FB)
        armed = Signal("armed", 3, 1)
        sq_done = Signal("sq_done", 3 * KB, KB)
        acc_done = Signal("acc_done", 3 * KB, KB)
        h_hi_done = Signal("h_hi_done", 3 * KB, KB)
        h_ready = Signal("h_ready", 3 * KB, KB)
        sum_done = Signal("sum_done", 3, 1)
        mean_done = Signal("mean_done", 3, 1)
        diag_done = Signal("diag_done", 3, 1)
        spread_done = Signal("spread_done", 3, 1)
        r_ready = Signal("r_ready", 3, 1)
        tables_in = Signal("tables_in", 32)
        tables_scaled = Signal("tables_scaled", 2)
        r2_done = Signal("r2_done", 1)
        root_done = Signal("root_done", 3, 1)
        newton = Signal("newton", 15, 5)
        turned_wi = Signal("turned_wi", 1)
        wi_ready = Signal("wi_ready", 1)
        swapped = Signal("swapped", 11)
        sin_done = Signal("sin_done", 11)
        roped = Signal("roped", 11)
        layer_in = Signal("layer_in", 48)
        diag_cleared = Signal("diag_cleared", 1)
        qi_placed = Signal("qi_placed", IDX_HEADS)
        idx_products = Signal("idx_products", 16)
        relu_done = Signal("relu_done", 16)
        idx_added = Signal("idx_added", 16)
        scores_ready = Signal("scores_ready", 1)
        top_found = Signal("top_found", NROUNDS)
        top_taken = Signal("top_taken", NROUNDS)
        own_found = Signal("own_found", 1)
        masks_ready = Signal("masks_ready", 1)
        conv_step = Signal("conv_step", 8 * CB)
        tails_kept = Signal("tails_kept", CB)
        o_conv_hi = Signal("o_conv_hi", CB)
        o_conv_lo = Signal("o_conv_lo", CB)
        q_diag_cleared = Signal("q_diag_cleared", 1)
        q_placed = Signal("q_placed", STREAMS)
        cache_in = [Signal(f"cache_in{i}", 16 * STREAMS) for i in range(2)]
        logits_done = Signal("logits_done", NU)
        max_done = Signal("max_done", NU)
        exp_done = Signal("exp_done", NU)
        inv_done = Signal("inv_done", NU)
        prob_done = Signal("prob_done", NU)
        turned = Signal("turned", NU)
        pT_done = Signal("pT_done", NU)
        pv_done = Signal("pv_done", NU)
        o_kept = Signal("o_kept", NG)
        o_att_hi = Signal("o_att_hi", AB)
        o_att_lo = Signal("o_att_lo", AB)
        gate_done = Signal("gate_done", 2 * KB)
        mixed = Signal("mixed", 3 * KB, 1)
        m_hi_done = Signal("m_hi_done", KB)
        m_ready = Signal("m_ready", KB)
        v_scaled = Signal("v_scaled", 1)
        own_in = Signal("own_in", 16 * STREAMS)
        stored = Signal("stored", 16 * 3)
        tails_stored = Signal("tails_stored", 16)
        y_scaled = ctx.enter_context(nc.semaphore("y_scaled"))
        y_stored = ctx.enter_context(nc.semaphore("y_stored"))
        ident_in_place = ctx.enter_context(nc.semaphore("ident_in_place"))
        ones_set = ctx.enter_context(nc.semaphore("ones_set"))

        block = ctx.enter_context(nc.Block())
        NCONST = 2

        @block.sync
        def _(sp):
            for j in range(KB):
                if j in (0, 3):
                    s = j // 3
                    sp.dma_start(w_raw[:, s, :], wts[s]).then_inc(raw_in[s], 16)
                sp.dma_start(x[:, j, :], x_in[:, j, :]).then_inc(x_landed[j], 16)
            for dst, src in ((ident[:, :], ident_in), (bmask_f[:, :], bmask_in)):
                sp.dma_start(dst, src).then_inc(consts_in, 16)
            for dst, src in ((cos_t[:, :], cos_in), (sin_t[:, :], sin_in)):
                sp.dma_start(dst, src).then_inc(tables_in.sem, 16)
            with sp.Fori(0, ALL_TILES // 2) as i:
                for s in range(2):
                    sp.wait_ge(lo_ready.sem, 2 * i + (s + 1))
                    sp.dma_start(w_raw[:, s, :], wts[2 * i + (s + 2)]).then_inc(raw_in[s], 16)

        @block.gpsimd
        def _(pool):
            with pool.Fori(0, ALL_TILES // 2 + 1) as i:
                for s in range(2):
                    pool.wait_ge(hi_ready.sem, 2 * i + (s + 1))
                    nc.gpsimd.tensor_tensor(w_lo[:, s, :], w_raw[:, s, :], w_hi[:, s, :].bitcast(F),
                                            ALU.subtract).then_inc(lo_ready.sem, 1)

        @block.tensor
        def _(pe):
            def passes(out, s, c, rhs_hi, rhs_lo, first, last):
                whi, wlo = w_hi[:, s, c * P:(c + 1) * P], w_lo[:, s, c * P:(c + 1) * P]
                for n, (w, a) in enumerate(((whi, rhs_hi), (whi, rhs_lo), (wlo, rhs_hi))):
                    for half in range(2):
                        ins = nc.tensor.matmul(out[:, half, :], w, a[:, half * HALF:(half + 1) * HALF],
                                               start=first and n == 0, stop=last and n == 2)
                return ins

            def linear(L, n, m, s, hi, lo, blocks=KB, before_last=None, out=None, after_block=None):
                out = res(s) if out is None else out
                pe.wait_ge(evacuated.sem, evacuated.count(L, m - 1))
                pe.wait_ge(lo_ready.sem, lo_ready.count(L, n + 1))
                for c in range(blocks):
                    if before_last and c == blocks - 1:
                        before_last()
                    ins = passes(out, s, c, hi[:, c, :], lo[:, c, :], c == 0, c == blocks - 1)
                    if after_block:
                        after_block()
                ins.then_inc(tile_done.sem, 1)

            def first_linear(L, n, m, p):
                s = n % 2
                pe.wait_ge(evacuated.sem, evacuated.count(L, m - 1))
                pe.wait_ge(lo_ready.sem, lo_ready.count(L, n + 1))
                for c in range(KB):
                    if c == KB - 1:
                        sum_squares(L, p)
                    pe.wait_ge(h_ready.sem, h_ready.count(L, (p - 1) * KB + c + 1))
                    ins = passes(res(m % 2), s, c, h_hi[:, c, :], h_lo[:, c, :], c == 0, c == KB - 1)
                ins.then_inc(tile_done.sem, 1)

            def value_tile(L, j):
                n = MIX_AT + V_AT + j
                pe.wait_ge(lo_ready.sem, lo_ready.count(L, n + 1))
                for c in range(2):
                    w = [z[:, n % 2, c * ATT_W:(c + 1) * ATT_W] for z in (w_hi, w_lo)]
                    for t in range(TT):
                        tok = [z[:, 2 * j + c, t * P:(t + 1) * P] for z in (h_hi, h_lo)]
                        for i, (a, b) in enumerate(((0, 0), (0, 1), (1, 0))):
                            ins = nc.tensor.matmul(value_banks[t], tok[a], w[b], start=j == c == i == 0,
                                                   stop=2 * j + c == KB - 1 and i == 2)
                ins.then_inc(tile_done.sem, 1)

            def sum_squares(L, p):
                pe.wait_ge(acc_done.sem, acc_done.count(L, p * KB))
                for t in range(TT):
                    ins = nc.tensor.matmul(bank[:, 2, t:t + 1], acc[:, t * P:(t + 1) * P], ones[:, 0:1],
                                           start=True, stop=True)
                ins.then_inc(sum_done.sem, 1)

            def spread_r(L, p):
                pe.wait_ge(diag_done.sem, diag_done.count(L, p))
                for half in range(2):
                    ins = nc.tensor.matmul(bank[:, 2 + half, 0:HALF], ones[:, 0:1].to_broadcast([P, P]),
                                           tmp[:, 2, half * HALF:(half + 1) * HALF], start=True, stop=True)
                ins.then_inc(spread_done.sem, 1)

            def second_linear(L, n, m, p):
                blocks = iter(range(KB))

                def after_block():
                    if next(blocks) == SPREAD_AFTER:
                        spread_r(L, p)
                linear(L, n, m, n % 2, h_hi, h_lo, out=res(m % 2), after_block=after_block)

            def ffn(L, f, n0, m0):
                done = 0
                for nb in GROUPS:
                    peeled = 0
                    if done == 0:
                        first_linear(L, n0, m0, (0, 2)[f])
                        second_linear(L, n0 + 1, m0 + 1, (0, 2)[f])
                        peeled = 1
                    with pe.Fori(peeled, nb) as i:
                        for s in range(2):
                            linear(L, n0 + s + 2 * i, m0 + s + 2 * i, s, h_hi, h_lo)
                    n0, m0, done = n0 + 2 * nb, m0 + 2 * nb, done + nb

                    def last_hidden():
                        pe.wait_ge(g_ready.sem, g_ready.count(L, f * FB + done))
                    with pe.Fori(0, KB // 2) as i:
                        pe.wait_ge(g_ready.sem, g_ready.count(L, f * FB + done - 1))
                        for s in range(2):
                            linear(L, n0 + s + 2 * i, m0 + s + 2 * i, s, g_hi, g_lo, nb,
                                   last_hidden if s == 0 else None)
                    n0, m0 = n0 + KB, m0 + KB

            def idx_unit(L, u):
                t, h = IDX_UNITS[u]
                out = bank[:, u % 4, :]
                lane = slice(64 * (h % 2), 64 * (h % 2) + 64)
                if u >= 4:
                    pe.wait_ge(relu_done.sem, relu_done.count(L, u - 3))
                if t < 4:
                    ins = nc.tensor.matmul(out[:, 0:IDX_COLS[t]], qiT[lane, h // 2, t * P:(t + 1) * P],
                                           kiT[lane, 0:IDX_COLS[t]], start=True, stop=True)
                else:
                    pe.wait_ge(qi_placed.sem, qi_placed.count(L, h + 1))
                    for pair in range(4):
                        nc.tensor.matmul(out[:, 0:PAST], qi_diag[:, h % 2, pair, :], ki_cache[:, pair, :],
                                         start=pair == 0, stop=pair == 3)
                    ins = nc.tensor.matmul(out[:, PAST:PAST + P], qiT[lane, h // 2, SEQ:T], kiT[lane, SEQ:T],
                                           start=True, stop=True)
                ins.then_inc(idx_products.sem, 1)

            def logits(L, u):
                kind, a, h = ATT_UNITS[u]
                out = logit_banks[u % 3]
                if u >= 3:
                    pe.wait_ge(exp_done.sem, exp_done.count(L, u - 2))
                if kind == "stream":
                    pe.wait_ge(q_placed.sem, q_placed.count(L, a + 1))
                    pe.wait_ge(cache_in[a % 2].sem, cache_in[a % 2].count(L, 32 * (a // 2 + 1)))
                    rows = spread[:, a % 2, :, :].rearrange("p h t -> p (h t)")
                    nc.tensor.matmul(out[:, 0:KEYS], rows, s_mask[:, :], start=True, stop=False)
                    for c in range(AB):
                        w = q_diag[:, a % 2, c, :]
                        ins = nc.tensor.matmul(out[:, 0:KEYS], w, k_cache[(a + 1) % 2][:, c, :],
                                               start=False, stop=c == AB - 1)
                else:
                    n = unit_columns(u)
                    lane = slice(64 * (h % 2), 64 * (h % 2) + 64)
                    nc.tensor.matmul(out[:, 0:n], ident_b[:, :], masks[:, a * n // 2:a * n // 2 + n],
                                     start=True, stop=False)
                    ins = nc.tensor.matmul(out[:, 0:n], qT[lane, h // 2, a * P:(a + 1) * P],
                                           kT[lane, h // 2, 0:n], start=False, stop=True)
                ins.then_inc(logits_done.sem, 1)

            def turn(L, u):
                if u >= 1:
                    pe.wait_ge(pT_done.sem, pT_done.count(L, u))
                pe.wait_ge(prob_done.sem, prob_done.count(L, u + 1))
                for c in range(blocks_of(u)):
                    keys = min(P, unit_columns(u) - c * P)
                    ins = nc.tensor.transpose(turn_bank[0:keys, c * P:(c + 1) * P],
                                              probs[u % 3][:, c * P:c * P + keys], ident[:, :])
                ins.then_inc(turned.sem, 1)

            def weigh(L, u):
                kind, a, h = ATT_UNITS[u]
                g, nb = GROUP_OF[u], blocks_of(u)
                out = out_banks[g % 2]
                if g >= 2:
                    pe.wait_ge(o_kept.sem, o_kept.count(L, g - 1))
                pe.wait_ge(pT_done.sem, pT_done.count(L, u + 1))
                if kind == "stream":
                    for c in range(AB):
                        for b in range(nb):
                            v = (v_cache[(a + 1) % 2][:, b * ATT_W + c * P:b * ATT_W + (c + 1) * P] if b < 2
                                 else v_own[a][:, c * P:(c + 1) * P])
                            keys = P if b < 2 else NEW
                            ins = nc.tensor.matmul(out[:, c * 32:(c + 1) * 32], v,
                                                   pT[0:keys, u % 2, b * P + c * 32:b * P + (c + 1) * 32],
                                                   start=b == 0, stop=b == nb - 1)
                else:
                    lane = slice(64 * (h % 2), 64 * (h % 2) + 64)
                    for b in range(nb):
                        ins = nc.tensor.matmul(out[lane, 0:P], v_sb[:, b, h * HD:(h + 1) * HD],
                                               pT[:, u % 2, b * P:(b + 1) * P], start=b == 0, stop=b == nb - 1)
                ins.then_inc(pv_done.sem, 1)

            pe.wait_ge(ones_set, 1)
            with pe.Fori(0, DEPTH) as L:
                ffn(L, 0, FFN1_AT, 0)
                first_linear(L, MIX_AT, MIX_RES, 1)
                n, m = MIX_AT + 1, MIX_RES + 1

                units = iter(range(len(IDX_UNITS)))

                def proj(after_block=None):
                    nonlocal n, m
                    linear(L, n, m, n % 2, h_hi, h_lo, out=res(m % 2), after_block=after_block)
                    n, m = n + 1, m + 1

                def next_unit():
                    u = next(units)
                    if u == 0:
                        pe.wait_ge(roped.sem, roped.count(L, 3))
                        pe.wait_ge(wi_ready.sem, wi_ready.count(L, 1))
                    idx_unit(L, u)
                second_linear(L, n, m, 1)
                n, m = n + 1, m + 1
                proj()
                pe.wait_ge(evacuated.sem, evacuated.count(L, m - 1))
                for part_ in range(2):
                    pe.wait_ge(lo_ready.sem, lo_ready.count(L, n + 1))
                    for c in range(KB // 2):
                        b = KB // 2 * part_ + c
                        if b == KB - 1:
                            pe.wait_ge(swapped.sem, swapped.count(L, 3))
                        ins = passes(res(m % 2), n % 2, c, h_hi[:, b, :], h_lo[:, b, :], b == 0, b == KB - 1)
                    ins.then_inc(tile_done.sem, 1)
                    n += 1
                m += 1
                for t in range(TT):
                    ins = nc.tensor.transpose(bank[:, 2, IDX_HEADS * t:IDX_HEADS * (t + 1)],
                                              wiT[64:64 + IDX_HEADS, t * P:(t + 1) * P],
                                              ident[64:64 + IDX_HEADS, 64:64 + IDX_HEADS])
                ins.then_inc(turned_wi.sem, 1)
                proj(next_unit)
                pe.wait_ge(layer_in.sem, layer_in.count(L, 48))
                proj(next_unit)
                for _ in range(1 + AB):
                    proj()
                pe.wait_ge(relu_done.sem, relu_done.count(L, len(IDX_UNITS)))
                pe.wait_ge(evacuated.sem, evacuated.count(L, m - 1))
                for j in range(KB // 2):
                    value_tile(L, j)
                n, m = n + KB // 2, m + 1
                for _ in range(EARLY_CONV):
                    proj()
                pe.wait_ge(ident_in_place, 1)
                pe.wait_ge(masks_ready.sem, masks_ready.count(L, 1))
                pe.wait_ge(evacuated.sem, evacuated.count(L, m))
                pe.wait_ge(own_in.sem, own_in.count(L, 16 * STREAMS))
                for step in range(NU + 3):
                    if step < NU:
                        logits(L, step)
                    for tile, c in PIECES[step]:
                        n, m = CONV_AT + EARLY_CONV + tile, CONV_RES + EARLY_CONV + tile
                        if c == 0:
                            pe.wait_ge(evacuated.sem, evacuated.count(L, m))
                            pe.wait_ge(lo_ready.sem, lo_ready.count(L, n + 1))
                        ins = passes(res(0), n % 2, c, h_hi[:, c, :], h_lo[:, c, :], c == 0, c == KB - 1)
                        if c == KB - 1:
                            ins.then_inc(tile_done.sem, 1)
                    if 0 <= step - 2 < NU:
                        turn(L, step - 2)
                    if 0 <= step - 3 < NU:
                        weigh(L, step - 3)
                with pe.Fori(0, KB // 2) as jj:
                    pe.wait_ge(o_kept.sem, o_kept.count(L, NG))
                    pe.wait_ge(evacuated.sem, evacuated.count(L, GATE_RES))
                    for j2 in range(2):
                        for s in range(2):
                            pe.wait_ge(evacuated.sem, evacuated.count(L, GATE_RES - 1 + 2 * j2 + s + 4 * jj))
                            ring = (3 * j2 + s) % 2
                            pe.wait_ge(lo_ready.sem, lo_ready.count(L, GATE_AT + 1 + 3 * j2 + s + 6 * jj))
                            for c in range(KB):
                                ins = passes(res(s), ring, c, h_hi[:, c, :], h_lo[:, c, :], c == 0, c == KB - 1)
                            ins.then_inc(tile_done.sem, 1)
                        ring = (3 * j2 + 2) % 2
                        pe.wait_ge(o_att_lo.sem, o_att_lo.count(L, AB))
                        pe.wait_ge(lo_ready.sem, lo_ready.count(L, GATE_AT + 3 + 3 * j2 + 6 * jj))
                        pe.wait_ge(mixed.sem, mixed.count(L, 3 * j2 + 6 * jj))
                        for part_ in range(2):
                            for c in range(AB):
                                b = part_ * AB + c
                                ins = passes(bank[:, 2 * part_:2 * part_ + 2, 0:HALF], ring, b,
                                             g_hi[:, b, :], g_lo[:, b, :], c == 0, c == AB - 1)
                        ins.then_inc(tile_done.sem, 1)
                with pe.Fori(0, KB // 2) as i:
                    pe.wait_ge(m_ready.sem, m_ready.count(L, KB - 1))

                    def last_sum():
                        pe.wait_ge(m_ready.sem, m_ready.count(L, KB))
                    for s in range(2):
                        linear(L, OUT_AT + s + 2 * i, OUT_RES + s + 2 * i, s, m_hi, m_lo,
                               before_last=last_sum if s == 0 else None)
                ffn(L, 1, FFN2_AT, FFN2_RES)
            sum_squares(DEPTH, 0)
            spread_r(DEPTH, 0)

        @block.scalar
        def _(act):
            def split(L, k, i=0, step=2):
                s = k % 2
                act.wait_ge(tile_done.sem, L * TILES + (k - 1) + (step * i))
                act.wait_ge(raw_in[s], L * (8 * TILES) + 16 * (k // 2 + 1) + (8 * step) * i)
                nc.scalar.activation(w_hi[:, s, :], w_raw[:, s, :], ACT.Copy).then_inc(hi_ready.sem, 1)

            def norm_block(L, p, j):
                nc.scalar.activation(h_hi[:, j, :], x[:, j, :], ACT.Copy,
                                     scale=gain[:, j:j + 1]).then_inc(h_hi_done.sem, 1)
                if j:
                    act.wait_ge(acc_done.sem, acc_done.count(L, (p - 1) * KB + j))
                nc.scalar.activation(sq[:, :], x[:, j, :], ACT.Square).then_inc(sq_done.sem, 1)

            def root(L, p):
                act.wait_ge(mean_done.sem, mean_done.count(L, p))
                nc.scalar.activation(stats[:, 1, :], stats[:, 0, :], ACT.Sqrt).then_inc(root_done.sem, 1)

            def closing(L, n0, m0, p):
                for j in range(KB):
                    split(L, n0 + j + 2)
                    act.wait_ge(evacuated.sem, evacuated.count(L, m0 + j + 1))
                    norm_block(L, p, j)
                root(L, p)

            def ffn(L, f, n0, m0):
                done = 0
                for g, nb in enumerate(GROUPS):
                    with act.Fori(0, nb) as i:
                        split(L, n0 + 2, i)
                        act.wait_ge(evacuated.sem, evacuated.count(L, m0 + 1 + 2 * i))
                        nc.scalar.activation(tmp[:, 1, :], tmp[:, 0, :], ACT.Silu).then_inc(silu_done.sem, 1)
                        split(L, n0 + 3, i)
                        act.wait_ge(evacuated.sem, evacuated.count(L, m0 + 2 + 2 * i))
                        nc.scalar.activation(g_hi[:, i, :], tmp[:, 2, :], ACT.Copy).then_inc(g_hi_done.sem, 1)
                    n0, m0, done = n0 + 2 * nb, m0 + 2 * nb, done + nb
                    if g < len(GROUPS) - 1:
                        with act.Fori(0, KB // 2) as i:
                            split(L, n0 + 2, i)
                            split(L, n0 + 3, i)
                    else:
                        closing(L, n0, m0, (1, 3)[f])
                    n0, m0 = n0 + KB, m0 + KB

            def relu(L, u):
                n = IDX_COLS[IDX_UNITS[u][0]]
                act.wait_ge(idx_products.sem, idx_products.count(L, u + 1))
                if u >= 2:
                    act.wait_ge(idx_added.sem, idx_added.count(L, u - 1))
                nc.scalar.activation(prob[:, u % 2, 0:n], bank[:, u % 4, 0:n], ACT.Relu).then_inc(relu_done.sem, 1)

            def place_qi(L, h):
                if h >= 2:
                    act.wait_ge(idx_products.sem, idx_products.count(L, 12 + h - 1))
                src = qiT[64 * (h % 2):64 * (h % 2) + 64, h // 2, SEQ:T].rearrange(
                    "p (pair par t) -> p pair par t", pair=4, par=2)
                for par in range(2):
                    dst = qi_diag[64 * par:64 * par + 64, h % 2, :, :].rearrange(
                        "p pair n -> p (pair n)")
                    dst = diagonal(dst, 16 * par, P + 2 * NEW, 4)
                    ins = nc.scalar.activation(dst, src[:, :, par, :], ACT.Copy)
                ins.then_inc(qi_placed.sem, 1)

            def load_cache(L, b):
                act.dma_start(k_cache[(b + 1) % 2][:, :, 0:PAST], kcache_in[L, b]).then_inc(cache_in[b % 2].sem, 16)
                act.dma_start(v_cache[(b + 1) % 2], vcache_in[L, b]).then_inc(cache_in[b % 2].sem, 16)

            def place_q(L, b):
                if b >= 2:
                    act.wait_ge(logits_done.sem, logits_done.count(L, 5 * (b - 2) + 1))
                for par in range(2):
                    dst = q_diag[64 * par:64 * par + 64, b % 2, :, :].rearrange("p c n -> p (c n)")
                    dst = diagonal(dst, 16 * par, P + 2 * NEW, AB)
                    src = qT[64 * par:64 * par + 64, :, SEQ + NEW * b:SEQ + NEW * (b + 1)]
                    nc.scalar.activation(dst, src, ACT.Copy)
                nc.scalar.activation(k_cache[(b + 1) % 2][:, :, PAST:KEYS],
                                     kT[:, :, SEQ + NEW * b:SEQ + NEW * (b + 1)], ACT.Copy)
                nc.scalar.activation(spread[:, b % 2, :, :],
                                     ident_b[:, NEW * b:NEW * (b + 1)].unsqueeze(1).to_broadcast([P, HEADS, NEW]),
                                     ACT.Copy).then_inc(q_placed.sem, 1)

            def exps(L, u):
                n = unit_columns(u)
                if u >= 3:
                    act.wait_ge(turned.sem, turned.count(L, u - 2))
                act.wait_ge(max_done.sem, max_done.count(L, u + 1))
                nc.scalar.activation(probs[u % 3][:, 0:n], logit_banks[u % 3][:, 0:n], ACT.Exp,
                                     bias=neg_max[:, u % 3:u % 3 + 1],
                                     accum_out=total[:, u % 3:u % 3 + 1]).then_inc(exp_done.sem, 1)

            def take_turned(L, u):
                n = blocks_of(u) * P
                if u >= 2:
                    act.wait_ge(pv_done.sem, pv_done.count(L, u - 1))
                act.wait_ge(turned.sem, turned.count(L, u + 1))
                nc.scalar.activation(pT[:, u % 2, 0:n], turn_bank[:, 0:n], ACT.Copy).then_inc(pT_done.sem, 1)

            act.dma_start(gains[:, :], gains_in).then_inc(gains_landed, 16)
            def first_split(s):
                act.wait_ge(raw_in[s], 16)
                nc.scalar.activation(w_hi[:, s, :], w_raw[:, s, :], ACT.Copy).then_inc(hi_ready.sem, 1)
            first_split(0)
            act.wait_ge(armed.sem, armed.count(0, 0))
            for j in range(KB):
                act.wait_ge(x_landed[j], 16)
                norm_block(0, 0, j)
                if j == 3:
                    first_split(1)
            root(0, 0)
            with act.Fori(0, DEPTH) as L:
                ffn(L, 0, FFN1_AT, 0)
                act.dma_start(convw[:, :, :], convw_in[L]).then_inc(layer_in.sem, 16)
                act.dma_start(state[:, :, :, :], state_in[L]).then_inc(layer_in.sem, 16)
                act.dma_start(ki_cache[:, :, :], kidx_in[L]).then_inc(layer_in.sem, 16)
                n = MIX_AT
                m = MIX_RES
                turns = 0

                def swap_halves():
                    nonlocal turns
                    if turns >= 2:
                        act.wait_ge(roped.sem, roped.count(L, turns - 1))
                    act.wait_ge(tile_done.sem, tile_done.count(L, n + 1))
                    ki = turns == 2
                    src = res(m % 2)
                    scale = HD ** -0.5 if 3 <= turns < 3 + AB else 1.0
                    for quarter in range(4):
                        to, from_ = 32 * (quarter ^ 1), 32 * (quarter % 2 if ki else quarter)
                        ins = nc.scalar.activation(halves(tmp[to:to + 32, turns % 2, :]), src[from_:from_ + 32],
                                                   ACT.Copy, scale=scale)
                    if ki:
                        nc.scalar.activation(halves(wiT[64:64 + IDX_HEADS, :]), src[64:64 + IDX_HEADS],
                                             ACT.Copy).then_inc(swapped.sem, 1)
                    else:
                        ins.then_inc(swapped.sem, 1)
                    turns += 1

                def conv_result(n, m):
                    ct, what = divmod(n - CONV_AT, 3)
                    if what == 1:
                        act.wait_ge(evacuated.sem, evacuated.count(L, m + 1))
                        nc.scalar.activation(tails[:, ct, 0:2], tmp[:, 1, SEQ - 2:SEQ], ACT.Copy)
                        nc.scalar.activation(
                            tails[:, ct, 2:].rearrange("p (b t) -> p b t", t=2),
                            tmp[:, 1, SEQ:T].rearrange("p (b t) -> p b t", t=NEW)[:, :, NEW - 2:NEW],
                            ACT.Copy).then_inc(tails_kept.sem, 1)
                    if what == 2:
                        act.wait_ge(evacuated.sem, evacuated.count(L, m + 1))
                        nc.scalar.activation(g_hi[:, AB + ct, :], tmp[:, 0, :], ACT.Copy).then_inc(o_conv_hi.sem, 1)

                def turn_of(n):
                    if n == MIX_AT + Q_AT + 2:
                        for u in range(8):
                            relu(L, u)
                    if n == MIX_AT + Q_AT + 3:
                        act.wait_ge(diag_cleared.sem, diag_cleared.count(L, 1))
                        place_qi(L, 0)
                        place_qi(L, 1)
                        for u in range(8, 12):
                            relu(L, u)
                        for h in range(IDX_HEADS):
                            relu(L, 12 + h)
                            if h + 2 < IDX_HEADS:
                                place_qi(L, h + 2)
                        act.dma_start(ki_out[L], kiT[0:64, :]).then_inc(stored.sem, 16)
                for what in (["rope"] * 3 + ["half", "rope"] + ["rope"] * (2 * AB - 1) + ["v"] * (KB // 2)
                             + ["conv"] * EARLY_CONV):
                    turn_of(n)
                    if n == MIX_AT + V_AT:
                        act.wait_ge(idx_products.sem, idx_products.count(L, len(IDX_UNITS)))
                        load_cache(L, 0)
                    if n == CONV_AT + 2:
                        act.wait_ge(v_scaled.sem, v_scaled.count(L, 1))
                        for b in range(STREAMS):
                            act.dma_start(v_own[b], v_sb[NEW * b:NEW * (b + 1), TT - 1, :]).then_inc(own_in.sem, 16)
                    if n == CONV_AT:
                        act.wait_ge(q_diag_cleared.sem, q_diag_cleared.count(L, 1))
                        place_q(L, 0)
                    split(L, n + 2)
                    if what == "rope":
                        swap_halves()
                    if what == "conv":
                        conv_result(n, m)
                    n += 1
                    m += {"rope": 1, "conv": 1, "half": 0, "v": 0}[what]
                    if n == MIX_AT + V_AT + KB // 2:
                        m += 1
                act.wait_ge(masks_ready.sem, masks_ready.count(L, 1))
                load_cache(L, 1)
                act.wait_ge(stored.sem, stored.count(L, 16))
                act.dma_start(k_out[L], kT[:, :, :]).then_inc(stored.sem, 16)
                act.dma_start(v_out[L], v_sb[:, :, :]).then_inc(stored.sem, 16)
                for step in range(NU + 3):
                    if step < NU:
                        kind, b, _ = ATT_UNITS[step]
                        exps(L, step)
                        if kind == "stream" and b + 1 < STREAMS:
                            place_q(L, b + 1)
                    if 0 <= step - 2 < NU:
                        take_turned(L, step - 2)
                    if step % 5 == 4 and step // 5 + 2 < STREAMS:
                        act.wait_ge(pv_done.sem, pv_done.count(L, 5 * (step // 5) + 1))
                        load_cache(L, step // 5 + 2)
                    for tile, c in PIECES[step]:
                        if c == KB - 1:
                            split(L, CONV_AT + EARLY_CONV + tile + 2)
                            conv_result(CONV_AT + EARLY_CONV + tile, CONV_RES + EARLY_CONV + tile)
                act.wait_ge(tails_kept.sem, tails_kept.count(L, CB))
                act.dma_start(conv_out[L], tails[:, :, :]).then_inc(tails_stored.sem, 16)
                act.wait_ge(o_conv_lo.sem, o_conv_lo.count(L, CB))
                act.dma_start(cos_t[:, :], cos_in).then_inc(tables_in.sem, 16)
                act.dma_start(sin_t[:, :], sin_in).then_inc(tables_in.sem, 16)
                act.wait_ge(o_kept.sem, o_kept.count(L, NG))
                for c in range(AB):
                    nc.scalar.activation(g_hi[:, c, :], qT[:, c, :], ACT.Copy).then_inc(o_att_hi.sem, 1)
                act.wait_ge(stored.sem, stored.count(L, 48))
                with act.Fori(0, KB // 2) as jj:
                    for j2 in range(2):
                        for s in range(2):
                            split(L, GATE_AT + 3 * j2 + s + 2, jj, 6)
                            act.wait_ge(evacuated.sem, evacuated.count(L, GATE_RES + 1 + 2 * j2 + s + 4 * jj))
                            nc.scalar.activation(tmp[:, s, :], tmp[:, s, :], ACT.Sigmoid).then_inc(gate_done.sem, 1)
                        split(L, GATE_AT + 3 * j2 + 4, jj, 6)
                        act.wait_ge(mixed.sem, mixed.count(L, 3 * j2 + 3 + 6 * jj))
                        nc.scalar.activation(m_hi[:, 2 * jj + j2, :], tmp[:, 2, :], ACT.Copy).then_inc(m_hi_done.sem, 1)
                closing(L, OUT_AT, OUT_RES, 2)
                act.wait_ge(tails_stored.sem, tails_stored.count(L, 16))
                ffn(L, 1, FFN2_AT, FFN2_RES)
            for j in range(KB):
                act.wait_ge(y_scaled, j + 1)
                act.dma_start(y_out[:, j * T:(j + 1) * T], x[:, j, :]).then_inc(y_stored, 16)
            act.wait_ge(y_stored, 16 * KB)

        @block.vector
        def _(dve):
            def leave(L, n, m, s, out, scaled_by, factor=None):
                dve.wait_ge(tile_done.sem, tile_done.count(L, n + 1))
                if factor is None:
                    ins = nc.vector.tensor_tensor(halves(out), res(s), halves(scaled_by), ALU.mult)
                else:
                    ins = nc.vector.scalar_tensor_tensor(out=halves(out), in0=res(s), scalar=factor,
                                                         in1=halves(scaled_by), op0=ALU.mult, op1=ALU.mult)
                ins.then_inc(evacuated.sem, 1)

            def arm(norm):
                nc.vector.memset(acc[:, :], 0.0)
                nc.vector.tensor_copy(gain[:, :], gains[:, bass.ds(norm * KB, KB)]).then_inc(armed.sem, 1)

            def norm_block(L, p, j):
                dve.wait_ge(h_hi_done.sem, h_hi_done.count(L, (p - 1) * KB + j + 1))
                nc.vector.scalar_tensor_tensor(out=h_lo[:, j, :], in0=x[:, j, :], scalar=gain[:, j:j + 1],
                                               in1=h_hi[:, j, :].bitcast(F), op0=ALU.mult,
                                               op1=ALU.subtract).then_inc(h_ready.sem, 1)
                dve.wait_ge(sq_done.sem, sq_done.count(L, (p - 1) * KB + j + 1))
                nc.vector.tensor_tensor(acc[:, :], acc[:, :], sq[:, :], ALU.add).then_inc(acc_done.sem, 1)

            def reciprocal_root(L, p):
                k = 5 * (p - 1)
                mean, table_root, step = stats[:, 0, :], stats[:, 1, :], stats[:, 2, :]
                dve.wait_ge(sum_done.sem, sum_done.count(L, p))
                nc.vector.tensor_scalar(mean, bank[:, 2, 0:TT], 1.0 / D_MODEL, EPS,
                                        ALU.mult, ALU.add).then_inc(mean_done.sem, 1)
                dve.wait_ge(root_done.sem, root_done.count(L, p))
                nc.vector.reciprocal(r_tok[:, :], table_root).then_inc(newton.sem, 1)
                dve.wait_ge(newton.sem, newton.count(L, k + 1))
                nc.vector.tensor_tensor(step, r_tok[:, :], r_tok[:, :], ALU.mult).then_inc(newton.sem, 1)
                dve.wait_ge(newton.sem, newton.count(L, k + 2))
                nc.vector.tensor_tensor(step, step, mean, ALU.mult).then_inc(newton.sem, 1)
                dve.wait_ge(newton.sem, newton.count(L, k + 3))
                nc.vector.tensor_scalar(step, step, -0.5, 1.5, ALU.mult, ALU.add).then_inc(newton.sem, 1)
                dve.wait_ge(newton.sem, newton.count(L, k + 4))
                nc.vector.tensor_tensor(r_tok[:, :], r_tok[:, :], step, ALU.mult).then_inc(newton.sem, 1)
                dve.wait_ge(newton.sem, newton.count(L, k + 5))
                nc.vector.tensor_tensor(tmp[:, 2, :].rearrange("p (t q) -> p t q", t=TT),
                                        ident[:, :].unsqueeze(1).to_broadcast([P, TT, P]),
                                        r_tok[:, :].unsqueeze(2).to_broadcast([P, TT, P]),
                                        ALU.mult).then_inc(diag_done.sem, 1)

            def take_r(L, p):
                dve.wait_ge(spread_done.sem, spread_done.count(L, p))
                nc.vector.tensor_copy(halves(r[:, :]), bank[:, 2:4, 0:HALF]).then_inc(r_ready.sem, 1)

            def closing(L, n0, m0, p, factor):
                arm(3 * L + p)
                dve.wait_ge(armed.sem, armed.count(L, p))
                for j in range(KB):
                    dve.wait_ge(tile_done.sem, tile_done.count(L, n0 + j + 1))
                    nc.vector.scalar_tensor_tensor(out=halves(x[:, j, :]), in0=res((m0 + j) % 2), scalar=factor,
                                                   in1=halves(x[:, j, :]), op0=ALU.mult,
                                                   op1=ALU.add).then_inc(evacuated.sem, 1)
                    norm_block(L, p, j)
                reciprocal_root(L, p)

            def ffn(L, f, n0, m0):
                done = 0
                for g, nb in enumerate(GROUPS):
                    k = f * FB + done
                    if done == 0:
                        take_r(L, (0, 2)[f])
                        dve.wait_ge(r_ready.sem, r_ready.count(L, (0, 2)[f]))
                        nc.vector.memset(waited[:, :], 0.0)
                    with dve.Fori(0, nb) as i:
                        leave(L, n0 + 2 * i, m0, 0, tmp[:, 0, :], r[:, :])
                        dve.wait_ge(silu_done.sem, silu_done.count(L, k + 1 + i))
                        nc.vector.tensor_tensor(tmp[:, 1, :], tmp[:, 1, :], r[:, :], ALU.mult).then_inc(silu_scaled.sem, 1)
                        dve.wait_ge(silu_scaled.sem, silu_scaled.count(L, k + 1 + i))
                        leave(L, n0 + 1 + 2 * i, m0, 1, tmp[:, 2, :], tmp[:, 1, :])
                        dve.wait_ge(g_hi_done.sem, g_hi_done.count(L, k + 1 + i))
                        nc.vector.tensor_tensor(g_lo[:, i, :], tmp[:, 2, :], g_hi[:, i, :].bitcast(F),
                                                ALU.subtract).then_inc(g_ready.sem, 1)
                    n0, m0, done = n0 + 2 * nb, m0 + 2 * nb, done + nb
                    if g < len(GROUPS) - 1:
                        with dve.Fori(0, KB // 2) as i:
                            for s in range(2):
                                dve.wait_ge(tile_done.sem, tile_done.count(L, n0 + s + 1 + 2 * i))
                                xb = x[:, 2 * i + s, :]
                                nc.vector.scalar_tensor_tensor(out=halves(xb), in0=res(s), scalar=0.5,
                                                               in1=halves(xb), op0=ALU.mult,
                                                               op1=ALU.add).then_inc(evacuated.sem, 1)
                    else:
                        closing(L, n0, m0, (1, 3)[f], 0.5)
                    n0, m0 = n0 + KB, m0 + KB

            def scores_of(t):
                if t == 4:
                    return s_scores[:, 0:PAST + P]
                start = {1: 0, 2: 2 * P, 3: 5 * P}[t]
                return scores[:, start:start + IDX_COLS[t]]

            def add_head(L, u):
                t, h = IDX_UNITS[u]
                dve.wait_ge(relu_done.sem, relu_done.count(L, u + 1))
                part_ = prob[:, u % 2, 0:IDX_COLS[t]]
                weight = wi[:, t, h:h + 1]
                if h == 0:
                    ins = nc.vector.tensor_scalar(scores_of(t), part_, weight, 0.0, ALU.mult, ALU.add)
                else:
                    dve.wait_ge(idx_added.sem, idx_added.count(L, u))
                    ins = nc.vector.scalar_tensor_tensor(out=scores_of(t), in0=part_, scalar=weight,
                                                         in1=scores_of(t), op0=ALU.mult, op1=ALU.add)
                ins.then_inc(idx_added.sem, 1)

            def in_round(k):
                return [(t, s_scores[:, :] if t == 4 else scores_of(t)) for t in (3, 2, 1, 4) if k < ROUNDS[t]]

            def find_top(L, k):
                if k:
                    dve.wait_ge(top_taken.sem, top_taken.count(L, k))
                else:
                    dve.wait_ge(scores_ready.sem, scores_ready.count(L, 1))
                nc.vector.memset(waited[:, :], 0.0)
                for t, left in in_round(k):
                    ins = nc.vector.max(top8[:, t - 1, :], left)
                ins.then_inc(top_found.sem, 1)

            def take_top(L, k):
                dve.wait_ge(top_found.sem, top_found.count(L, k + 1))
                nc.vector.memset(waited[:, :], 0.0)
                for t, left in in_round(k):
                    ins = nc.vector.match_replace(left, top8[:, t - 1, :], left, TAKEN)
                ins.then_inc(top_taken.sem, 1)

            def choose_round(L, k):
                find_top(L, k)
                take_top(L, k)

            def masks_from_scores(L):
                dve.wait_ge(top_taken.sem, top_taken.count(L, NROUNDS))
                for t in (1, 2, 3):
                    at_ = t * (t + 1) * P // 2
                    nc.vector.tensor_scalar(masks[:, at_:at_ + IDX_COLS[t]], scores_of(t), -2e38, MASK,
                                            ALU.is_gt, ALU.mult)
                lowest = top8[:, 0:2, :].rearrange("p a k -> p (a k)")
                nc.vector.tensor_reduce(out=lowest, in_=s_scores[:, PAST:PAST + P].rearrange("p (b t) -> p t b", t=NEW),
                                        axis=AX, op=ALU.min).then_inc(own_found.sem, 1)
                nc.vector.tensor_scalar(s_mask[:, 0:PAST], s_scores[:, 0:PAST], -2e38, MASK, ALU.is_gt, ALU.mult)
                dve.wait_ge(own_found.sem, own_found.count(L, 1))
                nc.vector.tensor_scalar(s_mask[:, PAST:KEYS], lowest, -2e38, MASK, ALU.is_gt,
                                        ALU.mult).then_inc(masks_ready.sem, 1)

            def rope_result(L, m, out, turns, factor, between):
                rows = slice(0, 64) if turns == 2 else slice(0, P)
                other = tmp[:, turns % 2, :]
                dve.wait_ge(swapped.sem, swapped.count(L, turns + 1))
                x_, o_, c_ = res(m % 2)[rows], halves(out[rows, :]), halves(cos_t[rows, :])
                if factor is None:
                    ins = nc.vector.tensor_tensor(o_, x_, c_, ALU.mult)
                else:
                    ins = nc.vector.scalar_tensor_tensor(out=o_, in0=x_, scalar=factor, in1=c_,
                                                         op0=ALU.mult, op1=ALU.mult)
                if turns == 2:
                    ins = nc.vector.tensor_tensor(halves(out[64:P, :]), x_, c_, ALU.mult)
                ins.then_inc(evacuated.sem, 1)
                if between:
                    between()
                nc.vector.tensor_tensor(other, other, sin_t[:, :], ALU.mult).then_inc(sin_done.sem, 1)
                dve.wait_ge(sin_done.sem, sin_done.count(L, turns + 1))
                nc.vector.tensor_tensor(out, out, other, ALU.add).then_inc(roped.sem, 1)

            def convolve(L, ct):
                u, y = tmp[:, 1, :], tmp[:, 2, :]
                us = u[:, SEQ:T].rearrange("p (b t) -> p b t", t=NEW)
                ys = y[:, SEQ:T].rearrange("p (b t) -> p b t", t=NEW)
                w = [convw[:, ct, i:i + 1] for i in range(3)]
                st = state[:, ct, :, :]
                nc.vector.tensor_scalar(y, u, w[2], None, ALU.mult).then_inc(conv_step.sem, 1)
                steps = [(y[:, 1:SEQ], u[:, 0:SEQ - 1], w[1], 1), (ys[:, :, 1:NEW], us[:, :, 0:NEW - 1], w[1], 1),
                         (y[:, 2:SEQ], u[:, 0:SEQ - 2], w[0], 2), (ys[:, :, 0:1], st[:, :, 1:2], w[1], 1),
                         (ys[:, :, 2:NEW], us[:, :, 0:NEW - 2], w[0], 3), (ys[:, :, 0:2], st[:, :, 0:2], w[0], 5)]
                for out, src, weight, after in steps:
                    dve.wait_ge(conv_step.sem, conv_step.count(L, 8 * ct + after))
                    nc.vector.scalar_tensor_tensor(out=out, in0=src, scalar=weight, in1=out, op0=ALU.mult,
                                                   op1=ALU.add).then_inc(conv_step.sem, 1)
                dve.wait_ge(conv_step.sem, conv_step.count(L, 8 * ct + 7))
                nc.vector.tensor_tensor(y, y, r[:, :], ALU.mult).then_inc(conv_step.sem, 1)
                dve.wait_ge(conv_step.sem, conv_step.count(L, 8 * ct + 8))

            def row_max(L, u):
                dve.wait_ge(logits_done.sem, logits_done.count(L, u + 1))
                nc.vector.tensor_reduce(out=neg_max[:, u % 3:u % 3 + 1], in_=logit_banks[u % 3][:, 0:unit_columns(u)],
                                        axis=AX, op=ALU.max, negate=True).then_inc(max_done.sem, 1)

            def normalise(L, u):
                dve.wait_ge(exp_done.sem, exp_done.count(L, u + 1))
                nc.vector.reciprocal(inv[:, u % 3:u % 3 + 1], total[:, u % 3:u % 3 + 1]).then_inc(inv_done.sem, 1)
                dve.wait_ge(inv_done.sem, inv_done.count(L, u + 1))
                p_ = probs[u % 3][:, 0:unit_columns(u)]
                nc.vector.tensor_scalar(p_, p_, inv[:, u % 3:u % 3 + 1], None, ALU.mult).then_inc(prob_done.sem, 1)

            def keep_out(L, u):
                kind, a, h = ATT_UNITS[u]
                g = GROUP_OF[u]
                dve.wait_ge(pv_done.sem, pv_done.count(L, u + 1))
                if kind == "stream":
                    o = out_banks[g % 2][:, 0:P].rearrange("p (c n) -> p c n", c=AB)
                    for par in range(2):
                        lane = slice(64 * par, 64 * par + 64)
                        ins = nc.vector.tensor_copy(qT[lane, :, SEQ + NEW * a:SEQ + NEW * (a + 1)],
                                                    o[lane, :, NEW * par:NEW * (par + 1)])
                else:
                    ins = nc.vector.tensor_copy(qT[:, h // 2, a * P:(a + 1) * P], out_banks[g % 2][:, 0:P])
                ins.then_inc(o_kept.sem, 1)

            nc.vector.memset(ones[:, :], 1.0).then_inc(evacuated.sem, 1)
            nc.vector.memset(inv[:, :], 1.0).then_inc(evacuated.sem, 1)
            nc.vector.memset(neg_max[:, :], 0.0).then_inc(mixed.sem, 1)
            dve.wait_ge(evacuated.sem, 2)
            nc.vector.memset(waited[:, :], 0.0).then_inc(ones_set, 1)
            dve.wait_ge(ones_set, 1)
            dve.wait_ge(gains_landed, 16)
            arm(0)
            dve.wait_ge(armed.sem, armed.count(0, 0))
            for j in range(KB):
                norm_block(0, 0, j)
            dve.wait_ge(consts_in, 16 * NCONST)
            nc.vector.tensor_copy(bmask[:, :], bmask_f[:, :])
            nc.vector.tensor_copy(ident_b[:, :], ident[:, :]).then_inc(ident_in_place, 1)
            reciprocal_root(0, 0)
            with dve.Fori(0, DEPTH) as L:
                ffn(L, 0, FFN1_AT, 0)
                nc.vector.memset(qi_diag[:, :, :, :], 0.0)
                nc.vector.memset(masks[:, 0:P], 0.0)
                nc.vector.memset(s_scores[:, PAST + P:SLOTS], -TAKEN).then_inc(diag_cleared.sem, 1)
                dve.wait_ge(diag_cleared.sem, diag_cleared.count(L, 1))
                nc.vector.memset(masks[0:64, 64:P], MASK)
                n, m = MIX_AT, MIX_RES
                turns = 0

                def rope_next(out, factor=None, between=None):
                    nonlocal m, turns
                    rope_result(L, m, out, turns, factor, between)
                    m, turns = m + 1, turns + 1

                dve.wait_ge(tables_in.sem, tables_in.count(L, 32))
                dve.wait_ge(spread_done.sem, spread_done.count(L, 1))
                nc.vector.tensor_tensor(halves(cos_t[:, :]), halves(cos_t[:, :]), bank[:, 2:4, 0:HALF],
                                        ALU.mult).then_inc(tables_scaled.sem, 1)
                dve.wait_ge(tables_scaled.sem, tables_scaled.count(L, 1))

                def scale_sin():
                    nc.vector.tensor_tensor(halves(sin_t[:, :]), halves(sin_t[:, :]), bank[:, 2:4, 0:HALF],
                                            ALU.mult).then_inc(tables_scaled.sem, 1)
                    take_r(L, 1)
                    dve.wait_ge(tables_scaled.sem, tables_scaled.count(L, 2))
                rope_next(qiT[:, 0, :], between=scale_sin)
                rope_next(qiT[:, 1, :])
                rope_next(kiT[:, :])

                def take_wi():
                    dve.wait_ge(turned_wi.sem, turned_wi.count(L, 1))
                    nc.vector.scalar_tensor_tensor(
                        out=wi[:, :, :], in0=bank[:, 2, 0:TT * IDX_HEADS].rearrange("p (t h) -> p t h", t=TT),
                        scalar=(64 ** -0.5) * (IDX_HEADS ** -0.5),
                        in1=r_tok[:, :].unsqueeze(2).to_broadcast([P, TT, IDX_HEADS]),
                        op0=ALU.mult, op1=ALU.mult).then_inc(wi_ready.sem, 1)
                take_wi()
                rope_next(qT[:, 0, :], HD ** -0.5)
                dve.wait_ge(wi_ready.sem, wi_ready.count(L, 1))
                for u in range(8):
                    add_head(L, u)
                rope_next(qT[:, 1, :], HD ** -0.5)
                for u in range(8, 16):
                    add_head(L, u)
                rope_next(qT[:, 2, :], HD ** -0.5)
                dve.wait_ge(idx_added.sem, idx_added.count(L, 16))
                for t in (1, 2, 3):
                    nc.vector.memset(scores_of(t)[0:64, IDX_COLS[t] - 64:IDX_COLS[t]], NEG)
                own = s_scores[:, PAST:PAST + P]
                nc.vector.tensor_tensor(own, own, bmask[:, :], ALU.add).then_inc(scores_ready.sem, 1)
                k = 0
                find_top(L, k)
                for out, factor in [(qT[:, 3, :], HD ** -0.5)] + [(kT[:, c, :], None) for c in range(AB)]:
                    rope_next(out, factor, between=lambda: take_top(L, k))
                    k += 1
                    find_top(L, k)
                nc.vector.memset(q_diag[:, :, :, :], 0.0).then_inc(q_diag_cleared.sem, 1)
                take_top(L, k)
                k += 1
                for _ in range(BEFORE_V - 1):
                    choose_round(L, k)
                    k += 1
                dve.wait_ge(roped.sem, roped.count(L, 3 + 2 * AB))
                r2 = cos_t
                nc.vector.tensor_tensor(r2[:, :], r[:, :], r[:, :], ALU.mult).then_inc(r2_done.sem, 1)
                n = MIX_AT + V_AT
                n += KB // 2
                dve.wait_ge(tile_done.sem, tile_done.count(L, n))
                for t in range(TT):
                    ins = nc.vector.tensor_scalar(v_sb[:, t, :], value_banks[t], r_tok[:, t:t + 1], None, ALU.mult)
                    if t == 0:
                        ins.then_inc(evacuated.sem, 1)
                ins.then_inc(v_scaled.sem, 1)
                m += 1

                def conv_result(n, m, s):
                    ct, what = divmod(n - CONV_AT, 3)
                    if what == 0:
                        if ct:
                            dve.wait_ge(o_conv_lo.sem, o_conv_lo.count(L, ct))
                        else:
                            dve.wait_ge(r2_done.sem, r2_done.count(L, 1))
                        leave(L, n, m, s, tmp[:, 0, :], r2[:, :])
                    elif what == 1:
                        if ct:
                            dve.wait_ge(tails_kept.sem, tails_kept.count(L, ct))
                        dve.wait_ge(tile_done.sem, tile_done.count(L, n + 1))
                        dve.wait_ge(evacuated.sem, evacuated.count(L, m))
                        nc.vector.tensor_tensor(halves(tmp[:, 1, :]), res(s), halves(tmp[:, 0, :]),
                                                ALU.mult).then_inc(evacuated.sem, 1)
                        dve.wait_ge(evacuated.sem, evacuated.count(L, m + 1))
                        convolve(L, ct)
                    else:
                        leave(L, n, m, s, tmp[:, 0, :], tmp[:, 2, :])
                        dve.wait_ge(o_conv_hi.sem, o_conv_hi.count(L, ct + 1))
                        nc.vector.tensor_tensor(g_lo[:, AB + ct, :], tmp[:, 0, :], g_hi[:, AB + ct, :].bitcast(F),
                                                ALU.subtract).then_inc(o_conv_lo.sem, 1)
                for _ in range(EARLY_CONV):
                    conv_result(n, m, m % 2)
                    n, m = n + 1, m + 1
                    for _ in range(2 if (n - 1 - CONV_AT) % 3 == 0 else 1):
                        if k < NROUNDS:
                            choose_round(L, k)
                            k += 1
                    if k == NROUNDS:
                        k += 1
                        masks_from_scores(L)
                for step in range(NU + 4):
                    if step < NU:
                        row_max(L, step)
                    if 0 <= step - 1 < NU:
                        normalise(L, step - 1)
                    if step - 4 in LAST_OF:
                        keep_out(L, step - 4)
                    for tile, c in PIECES[step] if step < NU + 3 else []:
                        if c == KB - 1:
                            conv_result(CONV_AT + EARLY_CONV + tile, CONV_RES + EARLY_CONV + tile, 0)
                for c in range(AB):
                    dve.wait_ge(o_att_hi.sem, o_att_hi.count(L, c + 1))
                    nc.vector.tensor_tensor(g_lo[:, c, :], qT[:, c, :], g_hi[:, c, :].bitcast(F),
                                            ALU.subtract).then_inc(o_att_lo.sem, 1)
                with dve.Fori(0, KB // 2) as jj:
                    for j2 in range(2):
                        for s in range(2):
                            leave(L, GATE_AT + 3 * j2 + s + 6 * jj, 0, s, tmp[:, s, :], r[:, :])
                        dve.wait_ge(gate_done.sem, gate_done.count(L, 2 * j2 + 2 + 4 * jj))
                        dve.wait_ge(tile_done.sem, tile_done.count(L, GATE_AT + 3 * j2 + 3 + 6 * jj))
                        nc.vector.tensor_tensor(halves(tmp[:, 0, :]), bank[:, 0:2, 0:HALF], halves(tmp[:, 0, :]),
                                                ALU.mult).then_inc(mixed.sem, 1)
                        nc.vector.tensor_tensor(halves(tmp[:, 1, :]), bank[:, 2:4, 0:HALF], halves(tmp[:, 1, :]),
                                                ALU.mult).then_inc(mixed.sem, 1)
                        dve.wait_ge(mixed.sem, mixed.count(L, 3 * j2 + 2 + 6 * jj))
                        nc.vector.tensor_tensor(tmp[:, 2, :], tmp[:, 0, :], tmp[:, 1, :], ALU.add).then_inc(mixed.sem, 1)
                        dve.wait_ge(m_hi_done.sem, m_hi_done.count(L, j2 + 1 + 2 * jj))
                        nc.vector.tensor_tensor(m_lo[:, 2 * jj + j2, :], tmp[:, 2, :],
                                                m_hi[:, 2 * jj + j2, :].bitcast(F), ALU.subtract).then_inc(m_ready.sem, 1)
                closing(L, OUT_AT, OUT_RES, 2, 1.0)
                ffn(L, 1, FFN2_AT, FFN2_RES)
            dve.wait_ge(spread_done.sem, spread_done.count(DEPTH, 0))
            for j in range(KB):
                nc.vector.scalar_tensor_tensor(out=halves(x[:, j, :]), in0=halves(x[:, j, :]),
                                               scalar=gain[:, j:j + 1], in1=bank[:, 2:4, 0:HALF],
                                               op0=ALU.mult, op1=ALU.mult).then_inc(y_scaled, 1)


def unit_columns(u):
    kind, a, _ = ATT_UNITS[u]
    return KEYS if kind == "stream" else (a + 1) * P


def blocks_of(u):
    return (unit_columns(u) + P - 1) // P


def diagonal(ap, start, step, count):
    return bass.AP(ap.tensor, ap.offset + start, [ap.ap[0], (step, count), (1, NEW)])


def kernel(x_prompt, x_sample, cache_k, cache_v, cache_kidx, state_conv, ffn1_norm, ffn1_up, ffn1_down,
           mix_norm, w_in, conv_w, w_branch, w_out, ffn2_norm, ffn2_up, ffn2_down, final_norm):
    import concourse.bacc as bacc
    from concourse.bass_utils import run_bass_kernel_spmd

    f32 = np.float32
    a = {k: np.asarray(v) for k, v in dict(
        x_prompt=x_prompt, x_sample=x_sample, cache_k=cache_k, cache_v=cache_v, cache_kidx=cache_kidx,
        state_conv=state_conv, ffn1_norm=ffn1_norm, ffn1_up=ffn1_up, ffn1_down=ffn1_down, mix_norm=mix_norm,
        w_in=w_in, conv_w=conv_w, w_branch=w_branch, w_out=w_out, ffn2_norm=ffn2_norm, ffn2_up=ffn2_up,
        ffn2_down=ffn2_down, final_norm=final_norm).items()}

    def blocks(w):
        return w.reshape(-1, P, w.shape[1]).transpose(1, 0, 2).reshape(P, -1)

    wts = np.zeros((ALL_TILES + 2, P, KB * P), f32)
    n = 0

    def put(w):
        nonlocal n
        b = blocks(w)
        wts[n, :, :b.shape[1]] = b
        n += 1

    def put_ffn(up, down):
        f0 = 0
        for nb in GROUPS:
            for f in range(f0, f0 + nb):
                put(up[:, f * P:(f + 1) * P])
                put(up[:, D_FF + f * P:D_FF + (f + 1) * P])
            for j in range(KB):
                put(down[f0 * P:(f0 + nb) * P, j * P:(j + 1) * P])
            f0 += nb

    for L in range(DEPTH):
        put_ffn(a["ffn1_up"][L], a["ffn1_down"][L])
        sizes = (ATT_W, ATT_W, ATT_W, 256, 64, IDX_HEADS, CONV_W, CONV_W, CONV_W, D_MODEL, D_MODEL)
        q, k, v, qi, ki, w_idx, cb, cc, cx, ga, gb = np.split(a["w_in"][L], np.cumsum(sizes)[:-1], axis=1)
        cols = lambda w, j: w[:, j * P:(j + 1) * P]
        put(cols(qi, 0))
        put(cols(qi, 1))
        put(np.concatenate([ki, w_idx, np.zeros((D_MODEL, P - HD - IDX_HEADS), f32)], axis=1))
        put(cols(q, 0)[:D_MODEL // 2])
        put(cols(q, 0)[D_MODEL // 2:])
        for j in range(1, AB):
            put(cols(q, j))
        for j in range(AB):
            put(cols(k, j))
        for j in range(KB // 2):
            put(v[2 * j * P:2 * (j + 1) * P])
        for j in range(CB):
            put(cols(cx, j))
            put(cols(cc, j))
            put(cols(cb, j))
        for j in range(KB):
            put(cols(ga, j))
            put(cols(gb, j))
            put(cols(a["w_branch"][L], j))
        for j in range(KB):
            put(cols(a["w_out"][L], j))
        put_ffn(a["ffn2_up"][L], a["ffn2_down"][L])
    assert n == ALL_TILES

    x = np.concatenate([a["x_prompt"][0], a["x_sample"].reshape(-1, D_MODEL)]).T
    norms = []
    for L in range(DEPTH):
        norms += [a["ffn1_norm"][L], a["mix_norm"][L], a["ffn2_norm"][L]]
    norms.append(a["final_norm"])
    half = HD // 2
    freqs = (10000.0 ** (-np.arange(half, dtype=np.float64) / half)).astype(f32)
    pos = np.concatenate([np.arange(SEQ), np.tile(PAST + np.arange(NEW), STREAMS)]).astype(f32)
    angle = (pos[None, :] * freqs[:, None]).astype(f32).astype(np.float64)
    cos = np.tile(np.cos(angle), (4, 1)).astype(f32)
    sin = np.tile(np.concatenate([-np.sin(angle), np.sin(angle)]), (2, 1)).astype(f32)
    stream = np.arange(P) // NEW
    kc = a["cache_k"].reshape(DEPTH, STREAMS, PAST, AB, P).transpose(0, 1, 4, 3, 2)
    vc = a["cache_v"].reshape(DEPTH, STREAMS, 2, P, ATT_W).transpose(0, 1, 3, 2, 4)
    kidx = a["cache_kidx"].reshape(DEPTH, 4, 2, PAST, HD).transpose(0, 2, 4, 1, 3)
    arrays = {
        "wts": wts,
        "x_in": x.reshape(KB, P, T).transpose(1, 0, 2),
        "gains_in": np.concatenate([g.reshape(KB, P).T for g in norms], axis=1),
        "cos_in": cos,
        "sin_in": sin,
        "ident_in": np.eye(P, dtype=f32),
        "bmask_in": np.where(stream[:, None] == stream[None, :], 0.0, NEG).astype(f32),
        "convw_in": a["conv_w"].reshape(DEPTH, 3, CB, P).transpose(0, 3, 2, 1),
        "state_in": a["state_conv"].reshape(DEPTH, STREAMS, 2, CB, P).transpose(0, 4, 3, 1, 2),
        "kcache_in": kc.reshape(DEPTH, STREAMS, P, AB, PAST),
        "vcache_in": vc.reshape(DEPTH, STREAMS, P, 2 * ATT_W),
        "kidx_in": kidx.reshape(DEPTH, P, 4, PAST),
    }
    outs = {"y_out": (P, KB * T), "k_out": (DEPTH, P, AB, T), "v_out": (DEPTH, P, TT, ATT_W),
            "ki_out": (DEPTH, HD, T), "conv_out": (DEPTH, P, CB, 2 + 2 * STREAMS)}
    nc = bacc.Bacc("TRN2", target_bir_lowering=False, num_devices=1)
    args, maps = [], {}
    for name, v_ in arrays.items():
        maps[name] = np.ascontiguousarray(v_)
        args.append(nc.dram_tensor(name, v_.shape, F, kind="ExternalInput").ap())
    for name, shape in outs.items():
        args.append(nc.dram_tensor(name, shape, F, kind="ExternalOutput").ap())
    build(nc, *args)
    got = run_bass_kernel_spmd(nc, [maps], core_ids=[0]).results[0]

    y = got["y_out"].reshape(P, KB, T).transpose(2, 1, 0).reshape(T, D_MODEL)
    k_new = got["k_out"].transpose(0, 3, 2, 1).reshape(DEPTH, T, HEADS, HD)
    v_new = got["v_out"].transpose(0, 2, 1, 3).reshape(DEPTH, T, HEADS, HD)
    ki_new = got["ki_out"].transpose(0, 2, 1)
    tails = got["conv_out"].transpose(0, 3, 2, 1).reshape(DEPTH, 2 + 2 * STREAMS, CONV_W)
    prompt = lambda z: np.ascontiguousarray(z[:, None, :SEQ])
    streams = lambda z: np.ascontiguousarray(z[:, SEQ:].reshape((DEPTH, STREAMS, NEW) + z.shape[2:]))
    return (np.ascontiguousarray(y[None, :SEQ]), np.ascontiguousarray(y[SEQ:].reshape(STREAMS, NEW, D_MODEL)),
            prompt(k_new), prompt(v_new), prompt(ki_new), np.ascontiguousarray(tails[:, None, :2]),
            streams(k_new), streams(v_new), streams(ki_new),
            np.ascontiguousarray(tails[:, 2:].reshape(DEPTH, STREAMS, 2, CONV_W)))
```
